# Optimizing a Trainium2 kernel written in Bass

```python
import math
import jax, jax.numpy as jnp
from jax import lax
import numpy as np

D_MODEL = 1024
BATCH = 1
SEQ = 1024
DEPTH = 2
DEC_BATCH = 1
DEC_SEQ = 32
PAST_LEN = 512

CHUNK = 64
QBLOCK = 128
N_A = DEPTH // 2
N_B = DEPTH - N_A
H_A = 8
DK_A = D_MODEL // (2 * H_A)
DV_A = D_MODEL // H_A
QK_A = H_A * DK_A
V_A = H_A * DV_A
IN_A = 2 * QK_A + 2 * V_A + 2 * H_A
H_B = 8
HD_B = D_MODEL // (2 * H_B)
K_B = H_B * 2 * HD_B
V_B = H_B * 2 * HD_B
Q_B = H_B * 2 * HD_B
D_FF = 4 * D_MODEL
EPS = 1e-6
NEG_INF = -1e30

kernel_name = 'yoco_mlstm_diffattn_stream_step'

def rmsnorm(x, g):
    xf = x.astype(jnp.float32)
    y = xf * lax.rsqrt(jnp.mean(xf * xf, axis=-1, keepdims=True) + EPS)
    return (y * g.astype(jnp.float32)).astype(x.dtype)

def sqrelu_mlp(x, w_up, w_down):
    return jnp.square(jax.nn.relu(x @ w_up)) @ w_down

def lambda_init(layer_idx):
    return 0.8 - 0.6 * math.exp(-0.3 * layer_idx)

def mlstm_chunk(carry, inp):
    c0, n0, m0 = carry
    q, k, v, li, lf = inp
    seg = q.shape[1]
    fcum = jnp.cumsum(lf, axis=1).transpose(0, 2, 1)
    li_t = li.transpose(0, 2, 1)
    causal = jnp.tril(jnp.ones((seg, seg), dtype=bool))
    dmat = jnp.where(causal, fcum[..., :, None] - fcum[..., None, :] + li_t[..., None, :], NEG_INF)
    a = fcum + m0[..., None]
    m = jnp.maximum(a, jnp.max(dmat, axis=-1))
    s = jnp.einsum('blhd,bshd->bhls', q, k) * jnp.exp(dmat - m[..., None])
    inter = jnp.exp(a - m)
    num = jnp.einsum('bhls,bshe->bhle', s, v) + inter[..., None] * jnp.einsum('blhd,bhde->bhle', q, c0)
    qn = jnp.sum(s, axis=-1) + inter * jnp.einsum('blhd,bhd->bhl', q, n0)
    h = num / jnp.maximum(jnp.abs(qn), jnp.exp(-m))[..., None]
    m_last = m[..., -1]
    w_last = jnp.exp(dmat[..., -1, :] - m_last[..., None])
    decay = jnp.exp(a[..., -1] - m_last)
    c1 = decay[..., None, None] * c0 + jnp.einsum('bhs,bshd,bshe->bhde', w_last, k, v)
    n1 = decay[..., None] * n0 + jnp.einsum('bhs,bshd->bhd', w_last, k)
    return (c1, n1, m_last), h.transpose(0, 2, 1, 3)

def mlstm_mixer(xn, w_in, b_i, b_f, g_h, w_out, state0, seg):
    bsz, seqlen, _ = xn.shape
    proj = xn @ w_in
    q, k, v, o, ig, fg = jnp.split(proj, [QK_A, 2 * QK_A, 2 * QK_A + V_A, 2 * QK_A + 2 * V_A,
                                          2 * QK_A + 2 * V_A + H_A], axis=-1)
    f32 = jnp.float32
    q = q.astype(f32).reshape(bsz, seqlen, H_A, DK_A)
    k = k.astype(f32).reshape(bsz, seqlen, H_A, DK_A) * (DK_A ** -0.5)
    v = v.astype(f32).reshape(bsz, seqlen, H_A, DV_A)
    li = ig.astype(f32) + b_i.astype(f32)
    lf = jax.nn.log_sigmoid(fg.astype(f32) + b_f.astype(f32))
    nc = seqlen // seg

    def to_chunks(t):
        return jnp.moveaxis(t.reshape((bsz, nc, seg) + t.shape[2:]), 1, 0)

    carry0 = (state0[0].astype(f32), state0[1].astype(f32), state0[2].astype(f32))
    state, h = lax.scan(mlstm_chunk, carry0, (to_chunks(q), to_chunks(k), to_chunks(v), to_chunks(li), to_chunks(lf)))
    h = jnp.moveaxis(h, 0, 1).reshape(bsz, seqlen, H_A, DV_A)
    h = rmsnorm(h, g_h.reshape(H_A, DV_A)).reshape(bsz, seqlen, V_A) * jax.nn.sigmoid(o.astype(f32))
    return h.astype(xn.dtype) @ w_out, state

def diff_attn_core(q, k, v, qpos, kpos, lam):
    s = jnp.einsum('bqhcd,bkhcd->bchqk', q.astype(jnp.float32), k.astype(jnp.float32)) * (HD_B ** -0.5)
    allowed = (kpos[None, :] // CHUNK) <= (qpos[:, None] // CHUNK)
    p = jax.nn.softmax(jnp.where(allowed, s, NEG_INF), axis=-1)
    w = p[:, 0] - lam * p[:, 1]
    return jnp.einsum('bhqk,bkhe->bqhe', w, v.astype(jnp.float32))

def diff_attn_mixer(xn, k, v, w_q, lq1, lk1, lq2, lk2, g_sub, w_o, lam_init, qpos, kpos, blocked):
    bsz, seqlen, _ = xn.shape
    f32 = jnp.float32
    q = (xn @ w_q).reshape(bsz, seqlen, H_B, 2, HD_B)
    lam = (jnp.exp(jnp.sum(lq1.astype(f32) * lk1.astype(f32)))
           - jnp.exp(jnp.sum(lq2.astype(f32) * lk2.astype(f32))) + lam_init)
    if blocked:
        nb = seqlen // QBLOCK
        qb = jnp.moveaxis(q.reshape(bsz, nb, QBLOCK, H_B, 2, HD_B), 1, 0)
        pb = qpos.reshape(nb, QBLOCK)
        o = lax.map(lambda blk: diff_attn_core(blk[0], k, v, blk[1], kpos, lam), (qb, pb))
        o = jnp.moveaxis(o, 0, 1).reshape(bsz, seqlen, H_B, 2 * HD_B)
    else:
        o = diff_attn_core(q, k, v, qpos, kpos, lam)
    o = rmsnorm(o, g_sub.reshape(H_B, 2 * HD_B)) * (1.0 - lam_init)
    return o.reshape(bsz, seqlen, V_B).astype(xn.dtype) @ w_o

def run_trunk(x, states0, past_k, past_v, seg, blocked, p):
    bsz, seqlen, _ = x.shape
    past = 0 if past_k is None else past_k.shape[1]
    qpos = past + jnp.arange(seqlen)
    kpos = jnp.arange(past + seqlen)
    c_list, n_list, m_list = [], [], []
    k_new = v_new = k_all = v_all = None
    for l in range(DEPTH):
        h = rmsnorm(x, p['g_mix_pre'][l])
        if l < N_A:
            h, (c1, n1, m1) = mlstm_mixer(h, p['w_in_a'][l], p['b_i_a'][l], p['b_f_a'][l], p['g_h_a'][l],
                                          p['w_out_a'][l], (states0[0][l], states0[1][l], states0[2][l]), seg)
            c_list.append(c1)
            n_list.append(n1)
            m_list.append(m1)
        else:
            if l == N_A:
                kv = rmsnorm(x, p['g_kv']) @ p['w_kv']
                k_new = kv[..., :K_B].reshape(bsz, seqlen, H_B, 2, HD_B)
                v_new = kv[..., K_B:].reshape(bsz, seqlen, H_B, 2 * HD_B)
                if past_k is None:
                    k_all, v_all = k_new, v_new
                else:
                    k_all = jnp.concatenate([past_k.astype(k_new.dtype), k_new], axis=1)
                    v_all = jnp.concatenate([past_v.astype(v_new.dtype), v_new], axis=1)
            j = l - N_A
            h = diff_attn_mixer(h, k_all, v_all, p['w_q_b'][j], p['lambda_q1'][j], p['lambda_k1'][j],
                                p['lambda_q2'][j], p['lambda_k2'][j], p['g_sub_b'][j], p['w_o_b'][j],
                                lambda_init(l), qpos, kpos, blocked)
        x = x + rmsnorm(h, p['g_mix_post'][l])
        f = sqrelu_mlp(rmsnorm(x, p['g_ffn_pre'][l]), p['w_up'][l], p['w_down'][l])
        x = x + rmsnorm(f, p['g_ffn_post'][l])
    return x, (jnp.stack(c_list), jnp.stack(n_list), jnp.stack(m_list)), k_new, v_new

def setup_inputs(seed: int = 0) -> dict:
    key = jax.random.key(seed)
    ks = jax.random.split(key, 32)

    def nrm(k, shape, scale):
        return jax.random.normal(k, shape, jnp.float32) * scale

    return {
        'x_prompt': nrm(ks[0], (BATCH, SEQ, D_MODEL), 1.0),
        'x_sample': nrm(ks[1], (DEC_BATCH, DEC_SEQ, D_MODEL), 1.0),
        'cache_k': nrm(ks[2], (DEC_BATCH, PAST_LEN, H_B, 2, HD_B), 1.0),
        'cache_v': nrm(ks[3], (DEC_BATCH, PAST_LEN, H_B, 2 * HD_B), 1.0),
        'state_c': nrm(ks[4], (N_A, DEC_BATCH, H_A, DK_A, DV_A), 0.5),
        'state_n': nrm(ks[5], (N_A, DEC_BATCH, H_A, DK_A), 0.5),
        'state_m': nrm(ks[6], (N_A, DEC_BATCH, H_A), 1.0),
        'w_in_a': nrm(ks[7], (N_A, D_MODEL, IN_A), D_MODEL ** -0.5),
        'b_i_a': nrm(ks[8], (N_A, H_A), 0.1),
        'b_f_a': 3.0 + nrm(ks[9], (N_A, H_A), 0.5),
        'g_h_a': 1.0 + nrm(ks[10], (N_A, V_A), 0.02),
        'w_out_a': nrm(ks[11], (N_A, V_A, D_MODEL), V_A ** -0.5),
        'g_kv': 1.0 + nrm(ks[12], (D_MODEL,), 0.02),
        'w_kv': nrm(ks[13], (D_MODEL, K_B + V_B), D_MODEL ** -0.5),
        'w_q_b': nrm(ks[14], (N_B, D_MODEL, Q_B), D_MODEL ** -0.5),
        'lambda_q1': nrm(ks[15], (N_B, HD_B), 0.1),
        'lambda_k1': nrm(ks[16], (N_B, HD_B), 0.1),
        'lambda_q2': nrm(ks[17], (N_B, HD_B), 0.1),
        'lambda_k2': nrm(ks[18], (N_B, HD_B), 0.1),
        'g_sub_b': 1.0 + nrm(ks[19], (N_B, V_B), 0.02),
        'w_o_b': nrm(ks[20], (N_B, V_B, D_MODEL), V_B ** -0.5),
        'g_mix_pre': 1.0 + nrm(ks[21], (DEPTH, D_MODEL), 0.02),
        'g_mix_post': 1.0 + nrm(ks[22], (DEPTH, D_MODEL), 0.02),
        'g_ffn_pre': 1.0 + nrm(ks[23], (DEPTH, D_MODEL), 0.02),
        'g_ffn_post': 1.0 + nrm(ks[24], (DEPTH, D_MODEL), 0.02),
        'w_up': nrm(ks[25], (DEPTH, D_MODEL, D_FF), D_MODEL ** -0.5),
        'w_down': nrm(ks[26], (DEPTH, D_FF, D_MODEL), D_FF ** -0.5),
    }

def reference(x_prompt, x_sample, cache_k, cache_v, state_c, state_n, state_m,
              w_in_a, b_i_a, b_f_a, g_h_a, w_out_a, g_kv, w_kv, w_q_b,
              lambda_q1, lambda_k1, lambda_q2, lambda_k2, g_sub_b, w_o_b,
              g_mix_pre, g_mix_post, g_ffn_pre, g_ffn_post, w_up, w_down):
    p = {'w_in_a': w_in_a, 'b_i_a': b_i_a, 'b_f_a': b_f_a, 'g_h_a': g_h_a, 'w_out_a': w_out_a,
         'g_kv': g_kv, 'w_kv': w_kv, 'w_q_b': w_q_b, 'lambda_q1': lambda_q1, 'lambda_k1': lambda_k1,
         'lambda_q2': lambda_q2, 'lambda_k2': lambda_k2, 'g_sub_b': g_sub_b, 'w_o_b': w_o_b,
         'g_mix_pre': g_mix_pre, 'g_mix_post': g_mix_post, 'g_ffn_pre': g_ffn_pre,
         'g_ffn_post': g_ffn_post, 'w_up': w_up, 'w_down': w_down}
    bsz = x_prompt.shape[0]
    zero_state = (jnp.zeros((N_A, bsz, H_A, DK_A, DV_A), jnp.float32),
                  jnp.zeros((N_A, bsz, H_A, DK_A), jnp.float32),
                  jnp.zeros((N_A, bsz, H_A), jnp.float32))
    y_prompt, (c_p, n_p, m_p), k_p, v_p = run_trunk(x_prompt, zero_state, None, None, CHUNK, True, p)
    y_sample, (c_s, n_s, m_s), k_s, v_s = run_trunk(x_sample, (state_c, state_n, state_m), cache_k, cache_v,
                                                    x_sample.shape[1], False, p)
    return (y_prompt, y_sample, c_p, n_p, m_p, k_p, v_p, c_s, n_s, m_s, k_s, v_s)


_drawn_inputs = setup_inputs


def setup_inputs(seed=0):
    import zlib

    import numpy as np

    out = dict(_drawn_inputs(seed))
    spreads = {}
    factors = {'g_h_a': 3.607,
     'g_kv': 2.857,
     'lambda_k2': 3.9,
     'g_sub_b': 5.544,
     'g_mix_post': 2.903,
     'g_ffn_pre': 3.21,
     'g_ffn_post': 3.373}
    for name, (base, spread) in spreads.items():
        noise = np.random.default_rng([zlib.crc32(name.encode()), seed]).standard_normal(out[name].shape)
        drawn = base * np.exp(spread * noise) if base else spread * noise
        out[name] = __import__('jax').numpy.asarray(drawn.astype(out[name].dtype))
    for name, factor in factors.items():
        out[name] = (out[name] * factor).astype(out[name].dtype)
    return out
```

```python
from contextlib import ExitStack
import math

import concourse.bass as bass
from concourse import mybir

F32 = mybir.dt.float32
F32R = mybir.dt.float32r
ALU = mybir.AluOpType
ACT = mybir.ActivationFunctionType
AX = mybir.AxisListType.X

P = 128
D = 1024
KB = D // P
SEQ, DEC = 1024, 32
T = SEQ + DEC
NG = 3
G = T // NG
PAST = 512
H = 8
DK, DV = 64, 128
LC = 128
NT = SEQ // P
NCH = NT + 1
NPAIR = H // 2
DFF = 4 * D
FFG = DFF // 512
EPS = 1e-6
NEG = -1e30
LAM_INIT = 0.8 - 0.6 * math.exp(-0.3)
ATT_SCALE = 64 ** -0.5
K_SCALE = DK ** -0.5
SCOL = SEQ + PAST
NKEY = SCOL + DEC

U_PROJ, N_PROJ = 0, 24
U_OUT = U_PROJ + N_PROJ
U_MLP0 = U_OUT + KB
U_KV, N_KV = U_MLP0 + 8 * FFG, 16
U_Q = U_KV + N_KV
U_WO = U_Q + KB
U_MLP1 = U_WO + KB
G_PROJ = 0
G_OUT = G_PROJ + NG * N_PROJ
G_MLP0 = G_OUT + NG * KB
G_KV = G_MLP0 + 36 * FFG
G_Q = G_KV + NG * N_KV
G_WO = G_Q + NG * KB
G_MLP1 = G_WO + NG * KB
RING = 6

GAINS = ["mix_pre0", "mix_pre1", "mix_post0", "mix_post1", "ffn_pre0", "ffn_pre1", "ffn_post0", "ffn_post1",
         "kv", "h", "sub"]
R_U, R_INTER, R_G, R_EM, R_LI, R_LF, R_M, R_FC = range(8)


def stream_step(nc, x_prompt, x_sample, cache_k, cache_v, state_c, state_n, state_m, w_in, b_i, b_f, g_h, w_out,
                g_kv, w_kv, w_q, lq1, lk1, lq2, lk2, g_sub, w_o, g_mix_pre, g_mix_post, g_ffn_pre, g_ffn_post,
                w_up, w_down, y_prompt, y_sample, c_prompt, n_prompt, m_prompt, k_prompt, v_prompt,
                c_sample, n_sample, m_sample, k_sample, v_sample, proj_s, kT_s, qT_s):
    with ExitStack() as ctx:
        def sb(name, shape, dt=F32, scope=ctx):
            return scope.enter_context(nc.sbuf_tensor(name, shape, dt))

        sems = {}

        def sem(name):
            if name not in sems:
                sems[name] = ctx.enter_context(nc.semaphore(name))
            return sems[name]

        X = sb("X", [P, KB, T])
        XH = sb("XH", [P, KB, T], F32R)
        XL = sb("XL", [P, KB, T], F32R)
        WR = sb("WR", [P, 2, D])
        WH = sb("WH", [P, 2, D], F32R)
        WL = sb("WL", [P, 2, D], F32R)
        RB = sb("RB", [P, T])
        STG = sb("STG", [P, 2, T])
        SQ = sb("SQ", [P, T])
        ident = sb("ident", [P, P])
        ones = sb("ones", [P, P])
        gain_rows = sb("gain_rows", [len(GAINS) * KB, P])
        GN = sb("GN", [P, len(GAINS) * KB])
        eps = sb("eps", [P, 1])
        lam_in = sb("lam_in", [P, 4, DK])
        lam = sb("lam", [P, 8])
        half = sb("half", [P, H])
        mask = sb("mask", [P, LC])
        bg = sb("bg", [H, 4])
        MP = sb("MP", [H, NCH])
        with ExitStack() as sc:
            KR = sb("KR", [P, T], F32, sc)
            QR = sb("QR", [P, T], F32, sc)
            VR = sb("VR", [P, 13, P], F32, sc)
            CK = sb("CK", [P, 4, P], F32, sc)
            KH = sb("KH", [P, NKEY], F32R, sc)
            KL = sb("KL", [P, NKEY], F32R, sc)
            QH = sb("QH", [P, T], F32R, sc)
            QL = sb("QL", [P, T], F32R, sc)
            VH = sb("VH", [P, 13, P], F32R, sc)
            VL = sb("VL", [P, 13, P], F32R, sc)
            PR = sb("PR", [P, 2, D], F32, sc)
            TH = sb("TH", [P, KB, P], F32R, sc)
            TL = sb("TL", [P, KB, P], F32R, sc)
            ON = sb("ON", [P, P], F32, sc)
            OS = sb("OS", [P, P], F32, sc)
            AS = sb("AS", [P, 16], F32, sc)
            MA = sb("MA", [P, P], F32R, sc)
            MB = sb("MB", [P, P], F32R, sc)
            MF = sb("MF", [P, 2, P], F32, sc)
        with ExitStack() as sc:
            OT = sb("OT", [P, 2, NCH, P], F32, sc)
        Y = sb("Y", [P, KB, T])
        rows = Y
        with ExitStack() as sc:
            HH = sb("HH", [P, 4, T], F32R, sc)
            HL = sb("HL", [P, 4, T], F32R, sc)
            MT = sb("MT", [P, 2, G], F32, sc)
            M2 = sb("M2", [P, 2, G], F32, sc)
        with ExitStack() as sc:
            WG = sb("WG", [P, KB, 16], F32, sc)
            WGH = sb("WGH", [P, KB, 40], F32R, sc)
            WGL = sb("WGL", [P, KB, 40], F32R, sc)
            RST = sb("RST", [H, T], F32, sc)
        with ExitStack() as sc:
            CH = sb("CH", [P, 24, LC], F32, sc)
            RC = sb("RC", [H, 4, LC], F32, sc)
            KN = sb("KN", [P, 4 * P], F32, sc)
            VC = sb("VC", [P, H, DV + 1], F32, sc)
            DT = sb("DT", [P, H, LC], F32, sc)
            SD = sb("SD", [P, H, LC], F32, sc)
            QI = sb("QI", [P, NPAIR, LC], F32, sc)
            CB = sb("CB", [P, NPAIR, 2, DV + 1], F32, sc)
            HN = sb("HN", [P, H, DV + 1], F32, sc)
            MS = sb("MS", [P, 8, H], F32, sc)
            DEC4 = sb("DEC4", [P, NPAIR], F32, sc)
            SEL = sb("SEL", [H, H, P], F32, sc)
            SELP = sb("SELP", [H, NPAIR, P], F32, sc)
        PS = ctx.enter_context(nc.psum_tensor("PS", [P, 8, 512], F32))
        KN3 = KN[:, :].rearrange("p (a b) -> p a b", b=P)

        def gcol(name, k):
            j = GAINS.index(name) * KB
            return GN[:, j + k:j + k + 1] if isinstance(k, int) else GN[:, bass.ds(k + j, 1)]

        def grp(g):
            return slice(g * G, (g + 1) * G)

        def tok(t, L=P):
            return bass.ds(t * P, L)

        block = ctx.enter_context(nc.Block())
        w_in2, w_out2 = w_in[0], w_out[0]

        def weight_cols(w, c):
            return w[:, bass.ds(c * P, P)].rearrange("(k p) n -> p k n", p=P)

        def barrier(e, n):
            e.drain().then_inc(sem("phase"), 1)
            e.wait_ge(sem("phase"), 4 * n)

        PHASES = ["load", "norm0", "proj", "gates", "mlstm", "out", "bound0", "mlp0", "bound1", "kv", "norm2", "q",
                  "attn", "wo", "bound2", "mlp1", "bound3", "final"]
        PH = {n: i + 1 for i, n in enumerate(PHASES)}

        NORMS = {n: i for i, n in enumerate(["n0", "b0y", "b0x", "b1y", "b1x", "b2y", "b2x", "b3y"])}
        SPLITS = {n: i for i, n in enumerate(["n0", "b0", "b1", "n2", "b2"])}
        BOUNDS = {n: i for i, n in enumerate(["b0", "b1", "b2", "b3"])}

        @block.sync
        def _(sp):
            consts = sem("consts")
            for j, (w, r) in enumerate([(g_mix_pre, 0), (g_mix_post, 16), (g_ffn_pre, 32), (g_ffn_post, 48)]):
                sp.dma_start(gain_rows[r:r + 16, :], w.rearrange("l (k p) -> (l k) p", p=P)).then_inc(consts, 16)
            sp.dma_start(gain_rows[64:72, :], g_kv.rearrange("(k p) -> k p", p=P)).then_inc(consts, 16)
            sp.dma_start(gain_rows[72:80, :], g_h.rearrange("l (k p) -> (l k) p", p=P)).then_inc(consts, 16)
            sp.dma_start(gain_rows[80:88, :], g_sub.rearrange("l (k p) -> (l k) p", p=P)).then_inc(consts, 16)
            x_t = x_prompt[0].rearrange("(t p) n -> t p n", p=P)
            for j in range(2):
                sp.dma_start(STG[:, j, 0:D], x_t[j]).then_inc(sem(f"x_in{j}"), 16)
            for s in range(2):
                sp.dma_start(WR[:, s, :].rearrange("p (k n) -> p k n", k=KB),
                             weight_cols(w_in2, s)).then_inc(sem(f"w_in{s}"), 16)
            for j, v in enumerate([b_i, b_f, state_m[0]]):
                sp.dma_start(bg[:, j:j + 1], v.rearrange("l h -> h l")).then_inc(consts, 16)
            for j, v in enumerate([lq1, lk1, lq2, lk2]):
                sp.dma_start(lam_in[:, j, :], v.to_broadcast([P, DK])).then_inc(consts, 16)
            sp.dma_start(WG[:, :, :], w_in2[:, 3072:3088].rearrange("(k p) n -> p k n", p=P)).then_inc(sem("wg_in"), 16)
            with sp.Fori(0, 3) as i:
                for j in range(2):
                    sp.wait_ge(sem("x_turned"), 2 * i + j + 1)
                    sp.dma_start(STG[:, j, 0:D], x_t[2 * i + j + 2]).then_inc(sem(f"x_in{j}"), 16)
            sp.wait_ge(sem("x_turned"), 7)
            sp.dma_start(STG[0:DEC, 0, 0:D], x_sample[0]).then_inc(sem("x_in0"), 16)

            def load(w, s, src, k=KB):
                sp.wait_ge(sem("w_lo"), w - 1)
                sp.dma_start(WR[:, s, :].rearrange("p (k n) -> p k n", k=k), src).then_inc(sem(f"w_in{s}"), 16)

            def load_cols(w, u0, n, i0=0):
                with sp.Fori(i0, n // 2) as i:
                    for s in range(2):
                        load(2 * i + (u0 + s), s, weight_cols(w, 2 * i + s))

            def load_mlp(l, u0):
                up = w_up[l]
                down = w_down[l]
                with sp.Fori(0, FFG) as j:
                    for m in range(4):
                        load(8 * j + (u0 + m), m % 2, weight_cols(up, 4 * j + m))
                    for d in range(4):
                        src = down[bass.ds(j * 512, 512), 256 * d:256 * d + 256].rearrange("(k p) n -> p k n", p=P)
                        load(8 * j + (u0 + 4 + d), d % 2, src, 4)

            load_cols(w_in2, U_PROJ, N_PROJ, 1)
            load_cols(w_out2, U_OUT, KB)
            load_mlp(0, U_MLP0)
            load_cols(w_kv, U_KV, N_KV)
            load_cols(w_q[0], U_Q, KB)
            load_cols(w_o[0], U_WO, KB)
            load_mlp(1, U_MLP1)

            y_t = y_prompt[0].rearrange("(t p) n -> t p n", p=P)
            for i in range(NT):
                j = i % 2
                sp.wait_ge(sem("y_out_a"), i + 1)
                sp.wait_ge(sem("y_out_d"), i + 1)
                sp.dma_start(y_t[i], STG[:, j, 0:D]).then_inc(sem(f"y_st{j}"), 16)
            sp.wait_ge(sem("y_out_a"), NT + 1)
            sp.wait_ge(sem("y_out_d"), NT + 1)
            sp.dma_start(y_sample[0], STG[0:DEC, 0, 0:D]).then_inc(sem("y_st0"), 16)
            sp.wait_ge(sem("y_st0"), 16 * (NT // 2 + 1))
            sp.wait_ge(sem("y_st1"), 16 * (NT // 2))

        @block.tensor
        def _(pe):
            mm_done, bank_free, w_lo = sem("mm_done"), sem("bank_free"), sem("w_lo")

            def three(out, lh, ll, rh, rl, start, stop):
                pe.matmul(out, lh, rh, start=start, stop=False)
                pe.matmul(out, lh, rl, start=False, stop=False)
                return pe.matmul(out, ll, rh, start=False, stop=stop)

            def unit(s, w_count, g0):
                pe.wait_ge(w_lo, w_count)
                for g in range(NG):
                    bank = PS[:, 3 * s + g, 0:G]
                    pe.wait_ge(bank_free, g0 + (g + 1))
                    for k in range(KB):
                        ws = slice(k * P, k * P + P)
                        mm = three(bank, WH[:, s, ws], WL[:, s, ws], XH[:, k, grp(g)], XL[:, k, grp(g)],
                                   k == 0, k == KB - 1)
                    mm.then_inc(mm_done, 1)

            def dense(n, u0, g0):
                with pe.Fori(0, n // 2) as i:
                    for s in range(2):
                        unit(s, 2 * i + (u0 + s + 1), 6 * i + (g0 + 3 * s))

            def token_sums(name):
                n = NORMS[name]
                pe.wait_ge(sem("sq_sum"), KB * (n + 1))
                for g in range(NG):
                    if g == 2:
                        pe.wait_ge(sem("root"), NG * n + 1)
                    pe.matmul(PS[:, 6 + g % 2, 0:G], ones[:, :], SQ[:, grp(g)], start=True, stop=True)\
                        .then_inc(sem("tok_sum"), 1)

            barrier(pe, PH["load"])
            pe.wait_ge(sem("consts"), 16 * 14)
            pe.wait_ge(sem("ident"), 2)
            pe.transpose(PS[:, 7, 0:88], gain_rows[:, :], ident[0:88, 0:88]).then_inc(sem("gains_turned"), 1)
            with pe.Fori(0, NT // 2) as i:
                for j in range(2):
                    pe.wait_ge(sem(f"x_in{j}"), 16 * i + 16)
                    pe.wait_ge(sem("x_cp_a"), 2 * i + (j + 1))
                    pe.wait_ge(sem("x_cp_d"), 2 * i + (j + 1))
                    for b in range(KB):
                        mm = pe.transpose(PS[:, 2 * j + b // 4, (b % 4) * P:(b % 4) * P + P],
                                          STG[:, j, b * P:b * P + P], ident[:, :])
                    mm.then_inc(sem("x_turned"), 1)
            pe.wait_ge(sem("x_in0"), 16 * 5)
            pe.wait_ge(sem("x_cp_a"), NT + 1)
            for b in range(KB):
                mm = pe.transpose(PS[:, 0, b * DEC:(b + 1) * DEC], STG[0:DEC, 0, b * P:b * P + P], ident[0:DEC, 0:DEC])
            mm.then_inc(sem("x_turned"), 1)

            barrier(pe, PH["norm0"])
            token_sums("n0")

            barrier(pe, PH["proj"])
            pe.wait_ge(sem("wg_lo"), 1)
            for g in range(NG):
                pe.wait_ge(bank_free, 1)
                for k in range(KB):
                    mm = three(PS[0:40, 5 + g, 0:G], WGH[:, k, :], WGL[:, k, :], XH[:, k, grp(g)], XL[:, k, grp(g)],
                               k == 0, k == KB - 1)
                mm.then_inc(sem("gates_mm"), 1)
            pe.wait_ge(sem("gates_read"), 6)
            dense(N_PROJ, U_PROJ, G_PROJ)

            barrier(pe, PH["gates"])
            barrier(pe, PH["mlstm"])
            pe.wait_ge(sem("sel"), 4)

            def chunk(L, c1):
                f = slice(0, L)
                c9 = lambda name: pe.wait_ge(sem(name), c1)
                pe.wait_ge(sem("ch_in"), c1 * 32)
                for b in range(4):
                    pe.transpose(PS[f, 0, b * P:b * P + P], CH[:, 4 + b, f], ident[:, :])
                for b in range(H):
                    mm = pe.transpose(PS[f, 1 + b // 4, (b % 4) * P:(b % 4) * P + P], CH[:, 8 + b, f], ident[:, :])
                pe.transpose(PS[f, 7, 0:H], RC[:, 2, f], ident[0:H, 0:H])
                pe.transpose(PS[f, 7, H:2 * H], RC[:, 3, f], ident[0:H, 0:H])\
                    .then_inc(sem("c_turned"), 1)
                for h in range(H):
                    pe.matmul(PS[f, 3 + h // 4, (h % 4) * L:(h % 4 + 1) * L], SEL[:, h, f], RC[:, 0, f],
                              start=True, stop=True)
                for p in range(NPAIR):
                    mm = pe.matmul(PS[:, 5, p * L:(p + 1) * L], SELP[:, p, :], RC[:, 1, f], start=True, stop=True)
                mm.then_inc(sem("c_spread"), 1)
                c9("c_cols")
                for h in range(H):
                    r = slice(64 * (h % 2), 64 * (h % 2) + 64)
                    mm = pe.matmul(PS[f, 6 + h % 2, (h // 2) * L:(h // 2 + 1) * L], CH[r, 4 + h // 2, f],
                                   CH[r, h // 2, f], start=True, stop=True)
                mm.then_inc(sem("c_scores"), 1)
                c9("c_kn")
                c9("c_vc")
                c9("c_vc2")
                pe.wait_ge(sem("c_sd"), 2 * c1)
                c9("c_qi")
                for p in range(NPAIR):
                    pe.matmul(PS[f, p, 0:2 * (DV + 1)], QI[:, p, f], CB[:, p, :, :].rearrange("p a b -> p (a b)"),
                              start=True, stop=False, skip_group_check=True)
                    for a in range(2):
                        h = 2 * p + a
                        mm = pe.matmul(PS[f, p, a * (DV + 1):(a + 1) * (DV + 1)], SD[f, h, f], VC[f, h, :],
                                       start=False, stop=True, skip_group_check=True)
                mm.then_inc(sem("c_num"), 1)
                c9("c_kw")
                for p in range(NPAIR):
                    mm = pe.matmul(PS[:, 4 + p, 0:2 * (DV + 1)], KN[f, p * P:p * P + P],
                                   VC[f, 2 * p:2 * p + 2, :].rearrange("p a b -> p (a b)"), start=True, stop=True)
                mm.then_inc(sem("c_kv"), 1)
                c9("c_hs")
                for h in range(H):
                    mm = pe.transpose(PS[:, h // 4, (h % 4) * L:(h % 4 + 1) * L], HN[f, h, 0:DV], ident[f, f])
                mm.then_inc(sem("c_hT"), 1)

            with pe.Fori(0, NT) as c:
                pe.wait_ge(sem("c_prev"), c + 1)
                chunk(LC, c + 1)
            pe.wait_ge(sem("c_prev"), NT + 1)
            pe.wait_ge(sem("c_state"), 1)
            chunk(DEC, NCH)

            barrier(pe, PH["out"])
            dense(KB, U_OUT, G_OUT)

            def boundary(n, name, pre=True):
                barrier(pe, PH[n])
                token_sums(name + "y")
                if pre:
                    token_sums(name + "x")

            def mlp(l, u0, g0):
                barrier(pe, PH[f"mlp{l}"])

                def group(j):
                    for m in range(4):
                        unit(m % 2, 8 * j + (u0 + m + 1), 36 * j + (g0 + 3 * m))
                    for d in range(4):
                        s = d % 2
                        pe.wait_ge(w_lo, 8 * j + (u0 + 5 + d))
                        for b in range(2):
                            for g in range(NG):
                                pe.wait_ge(bank_free, 36 * j + (g0 + 12 + 6 * d + 3 * b + g + 1))
                                for k in range(4):
                                    if d == 0 and b == 0:
                                        pe.wait_ge(sem("h_lo"), 12 * j + (96 * l + 3 * k + g + 1))
                                    ws = slice(k * 256 + b * P, k * 256 + b * P + P)
                                    mm = three(PS[:, 3 * b + g, 0:G], WH[:, s, ws], WL[:, s, ws],
                                               HH[:, k, grp(g)], HL[:, k, grp(g)], k == 0, k == 3)
                                mm.then_inc(mm_done, 1)

                with pe.Fori(0, FFG) as j:
                    group(j)

            boundary("bound0", "b0")
            mlp(0, U_MLP0, G_MLP0)
            boundary("bound1", "b1")

            barrier(pe, PH["kv"])
            with pe.Fori(0, N_KV // 2) as i:
                for s in range(2):
                    unit(s, 2 * i + (U_KV + s + 1), 6 * i + (G_KV + 3 * s))
                    pe.wait_ge(bank_free, RING + 6 * i + (G_KV + 3 * s + 3))
                    pe.wait_ge(sem("kv_rows"), 6 * i + (3 * s))
                    for t in range(NT):
                        mm = pe.transpose(PS[:, 6 + t // 4, (t % 4) * P:(t % 4) * P + P], STG[:, s, t * P:t * P + P],
                                          ident[:, :])
                        if t % 4 == 3:
                            mm.then_inc(sem("kv_turned"), 1)
                    pe.wait_ge(sem("kv_rows"), 6 * i + (3 * s + 1))
                    pe.transpose(PS[0:DEC, 6, 0:P], STG[:, s, SEQ:T], ident[:, :]).then_inc(sem("kv_turned"), 1)

            barrier(pe, PH["norm2"])
            barrier(pe, PH["q"])
            dense(KB, U_Q, G_Q)

            barrier(pe, PH["attn"])

            def settle(i):
                if i == NT:
                    pe.sem_inc(sem("sample_step"), 1)

            def scores(h, i):
                L, n, q0, k0 = (P, (i + 1) * P, i * P, 0) if i < NT else (DEC, PAST + DEC, SEQ, SEQ)
                if i == 0:
                    pe.wait_ge(sem("a_split"), h + 1)
                pe.wait_ge(sem("a_exp"), 18 * h + 2 * i)
                settle(i)
                for m in range(2):
                    r = slice(64 * m, 64 * m + 64)
                    for c in range(0, n, 512):
                        w = min(512, n - c)
                        diag = i < NT and c + w == n
                        out = PS[0:L, 2 * m + c // 512, 0:w]
                        kh, kl = KH[r, k0 + c:k0 + c + w], KL[r, k0 + c:k0 + c + w]
                        pe.matmul(out, QH[r, q0:q0 + L], kh, start=True, stop=False)
                        if diag:
                            pe.matmul(PS[0:L, 2 * m + c // 512, w - P:w], MA[r, :], MB[r, :], start=False,
                                      stop=False, skip_group_check=True)
                        pe.matmul(out, QH[r, q0:q0 + L], kl, start=False, stop=False)
                        mm = pe.matmul(out, QL[r, q0:q0 + L], kh, start=False, stop=True)
                mm.then_inc(sem("a_scores"), 1)

            def values(h, i):
                L, nk = (P, i + 1) if i < NT else (DEC, 5)
                f = slice(0, L)
                v0 = 0 if i < NT else NT
                pe.wait_ge(sem("a_comb"), 9 * h + (i + 1))
                pe.wait_ge(sem("a_tlo"), 9 * h + i)
                settle(i)
                for t in range(nk):
                    K = DEC if (i == NT and t == 4) else P
                    mm = pe.transpose(PS[0:K, 4 + t // 4, (t % 4) * L:(t % 4 + 1) * L], PR[f, 0, t * P:t * P + K],
                                      ident[f, f])
                mm.then_inc(sem("a_turned"), 1)
                pe.wait_ge(sem("a_tlo"), 9 * h + (i + 1))
                pe.wait_ge(sem("a_on"), 9 * h + i)
                for t in range(nk):
                    K = slice(0, DEC if (i == NT and t == 4) else P)
                    mm = three(PS[f, 6, 0:P], TH[K, t, f], TL[K, t, f], VH[K, v0 + t, :], VL[K, v0 + t, :],
                               t == 0, t == nk - 1)
                mm.then_inc(sem("a_out"), 1)
                pe.wait_ge(sem("a_on"), 9 * h + (i + 1))
                pe.wait_ge(sem("a_xlo"), 9 * h + i)
                settle(i)
                pe.transpose(PS[:, 7, 0:L], ON[f, :], ident[f, f]).then_inc(sem("a_oT"), 1)

            pe.wait_ge(sem("mask_r"), 1)
            with pe.Fori(0, H) as h:
                pe.wait_ge(sem("a_in"), 64 * h + 64)
                pe.wait_ge(sem("a_xlo"), 9 * h)
                for t in range(4):
                    mm = pe.transpose(PS[:, 7, t * P:t * P + P], CK[:, t, :], ident[:, :])
                mm.then_inc(sem("a_ckT"), 1)
                scores(h, 0)
                for i in range(NT + 1):
                    if i < NT:
                        scores(h, i + 1)
                    values(h, i)

            barrier(pe, PH["wo"])
            dense(KB, U_WO, G_WO)
            boundary("bound2", "b2")
            mlp(1, U_MLP1, G_MLP1)
            boundary("bound3", "b3", False)

            barrier(pe, PH["final"])
            for t in range(NCH):
                L = P if t < NT else DEC
                if t >= 2:
                    pe.wait_ge(sem("y_out_a"), t - 1)
                    pe.wait_ge(sem("y_out_d"), t - 1)
                for b in range(KB):
                    mm = pe.transpose(PS[0:L, 2 * (t % 2) + b // 4, (b % 4) * P:(b % 4) * P + P],
                                      X[:, b, t * P:t * P + L], ident[:, :])
                mm.then_inc(sem("y_turned"), 1)

        @block.scalar
        def _(act):
            mm_done, bank_free, w_hi = sem("mm_done"), sem("bank_free"), sem("w_hi")

            def split_hi(s, u, u2, g):
                act.wait_ge(sem(f"w_in{s}"), 16 * u2 + 16)
                if g is not None:
                    act.wait_ge(mm_done, g)
                act.activation(WH[:, s, :], WR[:, s, :], ACT.Copy).then_inc(w_hi, 1)

            def norm_sums(src, name):
                n = NORMS[name]
                for k in range(KB):
                    if k >= 2:
                        act.wait_ge(sem("sq_sum"), KB * n + k - 1)
                    act.activation(STG[:, k % 2, :], src[:, k, :], ACT.Square).then_inc(sem("squared"), 1)

            def norm_roots(name):
                for g in range(NG):
                    act.wait_ge(sem("tok_sum"), NG * NORMS[name] + g + 1)
                    act.activation(STG[:, 0, grp(g)], PS[:, 6 + g % 2, 0:G], ACT.Sqrt, bias=eps[:, 0:1], scale=1.0 / D)\
                        .then_inc(sem("root"), 1)

            barrier(act, PH["load"])
            act.wait_ge(sem("gains_turned"), 1)
            act.activation(GN[:, :], PS[:, 7, 0:88], ACT.Copy).then_inc(sem("gains"), 1)
            act.sem_inc(sem("x_cp_a"), 2)
            with act.Fori(0, NT // 2) as i:
                for j in range(2):
                    act.wait_ge(sem("x_turned"), 2 * i + (j + 1))
                    act.activation(X[:, 0:4, bass.ds(256 * i + P * j, P)],
                                   PS[:, 2 * j, :].rearrange("p (b t) -> p b t", b=4), ACT.Copy)\
                        .then_inc(sem("x_cp_a"), 1)
            act.wait_ge(sem("x_turned"), NT + 1)
            act.activation(X[:, :, SEQ:T], PS[:, 0, 0:KB * DEC].rearrange("p (b t) -> p b t", b=KB), ACT.Copy)\
                .then_inc(sem("x_cp_a"), 1)

            barrier(act, PH["norm0"])
            split_hi(0, 0, 0, None)
            for k in range(KB):
                act.activation(XH[:, k, :], X[:, k, :], ACT.Copy, scale=gcol("mix_pre0", k)).then_inc(sem("x_hi"), 1)
            norm_sums(X, "n0")
            act.wait_ge(sem("wg_in"), 16)
            act.wait_ge(sem("wg_zero"), 2)
            act.activation(WGH[:, :, 0:8], WG[:, :, 0:8], ACT.Copy).then_inc(sem("wg_hi"), 1)
            act.activation(WGH[:, :, 32:40], WG[:, :, 8:16], ACT.Copy).then_inc(sem("wg_hi"), 1)
            norm_roots("n0")

            def store(s, dst, src, name="stg"):
                act.dma_start(dst, src).then_inc(sem(f"{name}{s}"), 16)

            barrier(act, PH["proj"])
            with act.Fori(0, 8) as i:
                for s in range(2):
                    split_hi(1 - s, None, i + s, 6 * i + (G_PROJ + 3 * s))
                    act.wait_ge(bank_free, RING + 6 * i + (G_PROJ + 3 * s + 3))
                    store(s, proj_s[2 * i + s], STG[:, s, :])
            with act.Fori(8, 12) as i:
                for s in range(2):
                    split_hi(1 - s, None, i + s, 6 * i + (G_PROJ + 3 * s))
                    act.wait_ge(bank_free, RING + 6 * i + (G_PROJ + 3 * s + 3))
                    act.activation(STG[:, s, :], STG[:, s, :], ACT.Sigmoid).then_inc(sem("o_sig"), 1)
                    act.wait_ge(sem("o_gain"), 2 * i + (s + 1 - 16))
                    store(s, proj_s[2 * i + s], STG[:, s, :])

            barrier(act, PH["gates"])
            li, lf, m_, fc, u_ = (rows[0:H, r, :] for r in (R_LI, R_LF, R_M, R_FC, R_U))
            tmp = rows[0:H, R_EM, :]
            act.wait_ge(sem("g_abs"), 1)
            act.activation(tmp, tmp, ACT.Exp, scale=-1.0).then_inc(sem("g_exp"), 1)
            act.wait_ge(sem("g_one"), 1)
            act.activation(tmp, tmp, ACT.Ln).then_inc(sem("g_exp"), 1)
            act.wait_ge(sem("g_m"), 1)
            act.activation(tmp, m_, ACT.Exp, scale=-1.0).then_inc(sem("g_fin"), 1)
            act.wait_ge(sem("g_inter"), 1)
            act.activation(rows[0:H, R_INTER, :], rows[0:H, R_INTER, :], ACT.Exp).then_inc(sem("g_fin"), 1)

            barrier(act, PH["mlstm"])
            act.wait_ge(sem("stg0"), 16 * 12)
            act.wait_ge(sem("stg1"), 16 * 12)
            act.dma_start(m_prompt[0].rearrange("b h -> h b"), rows[0:H, R_M, SEQ - 1:SEQ]).then_inc(sem("m_st"), 16)
            act.dma_start(m_sample[0].rearrange("b h -> h b"), rows[0:H, R_M, T - 1:T]).then_inc(sem("m_st"), 16)

            def chunk_in(t0, L):
                act.dma_start(CH[:, :, 0:L], proj_s[:, :, bass.ds(t0, L)].rearrange("b p t -> p b t"))\
                    .then_inc(sem("ch_in"), 16)
                act.dma_start(RC[:, :, 0:L], rows[0:H, 0:4, bass.ds(t0, L)]).then_inc(sem("ch_in"), 16)

            def chunk(L, c1, xcol, nxt):
                f = slice(0, L)
                act.wait_ge(sem("c_turned"), c1)
                act.activation(KN[f, :], PS[f, 0, :], ACT.Copy, scale=K_SCALE).then_inc(sem("c_kn"), 1)
                act.activation(VC[f, 0:4, 0:DV], PS[f, 1, :].rearrange("p (h e) -> p h e", h=4), ACT.Copy)\
                    .then_inc(sem("c_vc"), 1)
                for h in range(H):
                    act.wait_ge(sem("c_cols"), c1)
                    act.wait_ge(sem("c_masked"), 2 * c1 - (1 - h // 4))
                    act.activation(DT[f, h, f], DT[f, h, f], ACT.Exp, bias=MS[f, 0, h:h + 1])\
                        .then_inc(sem("c_dt"), 1)
                act.wait_ge(sem("c_num"), c1)
                for p in range(NPAIR):
                    act.activation(HN[f, 2 * p:2 * p + 2, :], PS[f, p, 0:2 * (DV + 1)]
                                   .rearrange("p (a b) -> p a b", a=2), ACT.Copy).then_inc(sem("c_hn"), 1)
                act.wait_ge(sem("c_hn"), 4 * c1)
                act.wait_ge(sem("c_kw"), c1)
                act.activation(DT[f, :, :], HN[f, :, 0:DV], ACT.Square).then_inc(sem("c_sn"), 1)
                act.wait_ge(sem("c_hf"), 2 * c1)
                act.activation(XH[:, :, xcol], SD[:, :, f], ACT.Copy).then_inc(sem("c_xh"), 1)
                if nxt is not None:
                    nxt()

            chunk_in(0, LC)
            with act.Fori(0, NT - 1) as c:
                chunk(LC, c + 1, bass.ds(c * P, P), lambda: chunk_in(c * P + P, LC))
            chunk(LC, NT, slice(SEQ - P, SEQ), lambda: chunk_in(SEQ, DEC))
            act.wait_ge(sem("c_upd"), 3 * NT)

            def state_out(c_o, n_o):
                for a in range(2):
                    r = slice(64 * a, 64 * a + 64)
                    act.dma_start(c_o.rearrange("(q a) d e -> a d q e", a=2)[a], CB[r, :, a, 0:DV]).then_inc(sem("st_out"), 16)
                    with nc.allow_non_contiguous_dma(reason="one normaliser column"):
                        act.dma_start(n_o.rearrange("(q a) (d o) -> a d q o", a=2, o=1)[a], CB[r, :, a, DV:DV + 1])\
                            .then_inc(sem("st_out"), 16)
            state_out(c_prompt[0, 0], n_prompt[0, 0])
            act.wait_ge(sem("st_out"), 64)
            sc_, sn_ = state_c[0, 0], state_n[0, 0]
            for a in range(2):
                r = slice(64 * a, 64 * a + 64)
                act.dma_start(CB[r, :, a, 0:DV], sc_.rearrange("(q a) d e -> a d q e", a=2)[a]).then_inc(sem("c_state0"), 16)
                with nc.allow_non_contiguous_dma(reason="one normaliser column"):
                    act.dma_start(CB[r, :, a, DV:DV + 1], sn_.rearrange("(q a) (d o) -> a d q o", a=2, o=1)[a])\
                        .then_inc(sem("c_state0"), 16)
            act.wait_ge(sem("c_state0"), 64)
            act.sem_inc(sem("c_state"), 1)
            chunk(DEC, NCH, slice(SEQ, T), None)
            act.wait_ge(sem("c_upd"), 3 * NCH)
            state_out(c_sample[0, 0], n_sample[0, 0])
            act.wait_ge(sem("st_out"), 128)
            act.wait_ge(sem("m_st"), 32)

            def dense_hi(n, g0, u0):
                with act.Fori(0, n // 2) as i:
                    for s in range(2):
                        split_hi(1 - s, None, i + (u0 // 2 + s), 6 * i + (g0 + 3 * s))

            barrier(act, PH["out"])
            dense_hi(KB, G_OUT, U_OUT)

            def boundary(n, name, pre):
                barrier(act, PH[n])
                norm_sums(Y, name + "y")
                norm_roots(name + "y")
                if pre:
                    for k in range(KB):
                        act.wait_ge(sem("x_new"), KB * BOUNDS[name] + k + 1)
                        act.activation(XH[:, k, :], X[:, k, :], ACT.Copy, scale=gcol(pre, k)).then_inc(sem("x_hi"), 1)
                    act.wait_ge(sem("inverse"), NG * (NORMS[name + "y"] + 1))
                    norm_sums(X, name + "x")
                    norm_roots(name + "x")

            def mlp(l, u0, g0):
                barrier(act, PH[f"mlp{l}"])

                def group(j, last):
                    for m in range(4):
                        split_hi((m + 1) % 2, None, 4 * j + (u0 // 2 + (m + 1) // 2), 36 * j + (g0 + 3 * m))
                        for g in range(NG):
                            n = 3 * m + g
                            act.wait_ge(bank_free, RING + 36 * j + (g0 + n + 1))
                            act.activation(HH[:, m, grp(g)], MT[:, n % 2, :], ACT.Square).then_inc(sem("h_hi"), 1)
                    for d in range(4):
                        if not (last and d == 3):
                            split_hi((d + 1) % 2, None, 4 * j + (u0 // 2 + (d + 5) // 2), 36 * j + (g0 + 12 + 6 * d))
                if l == 0:
                    with act.Fori(0, FFG) as j:
                        group(j, False)
                else:
                    with act.Fori(0, FFG - 1) as j:
                        group(j, False)
                    group(FFG - 1, True)

            boundary("bound0", "b0", "ffn_pre0")
            mlp(0, U_MLP0, G_MLP0)
            boundary("bound1", "b1", "kv")

            barrier(act, PH["kv"])
            kp = k_prompt[0].rearrange("(t p) h a d -> h p t (a d)", p=P)
            ks = k_sample[0].rearrange("t h a d -> h t (a d)")
            vp = v_prompt[0].rearrange("(t p) h d -> h p t d", p=P)
            vs = v_sample[0].rearrange("t h d -> h t d")

            def kv_unit(i, s, h, dp, ds_, keys):
                split_hi(1 - s, None, i + (U_KV // 2 + s), 6 * i + (G_KV + 3 * s))
                act.wait_ge(bank_free, RING + 6 * i + (G_KV + 3 * s + 3))
                if keys:
                    store(s, kT_s[h], STG[:, s, :], "kt_st")
                act.wait_ge(sem(f"kv_st{s}"), 32 * i)
                for b in range(2):
                    act.wait_ge(sem("kv_turned"), 6 * i + (3 * s + b + 1))
                    act.activation(OT[:, s, 4 * b:4 * b + 4, :], PS[:, 6 + b, :].rearrange("p (t c) -> p t c", t=4),
                                   ACT.Copy).then_inc(sem("kv_rows"), 1)
                act.wait_ge(sem("kv_turned"), 6 * i + (3 * s + 3))
                act.activation(OT[0:DEC, s, NT, :], PS[0:DEC, 6, 0:P], ACT.Copy).then_inc(sem("kv_rows"), 1)
                act.wait_ge(sem("kv_rows"), 6 * i + (3 * s + 3))
                store(s, dp[h], OT[:, s, 0:NT, :], "kv_st")
                store(s, ds_[h], OT[0:DEC, s, NT, :], "kv_st")

            with act.Fori(0, 4) as i:
                for s in range(2):
                    kv_unit(i, s, 2 * i + s, kp, ks, True)
            with act.Fori(4, 8) as i:
                for s in range(2):
                    kv_unit(i, s, 2 * i + (s - 8), vp, vs, False)

            barrier(act, PH["norm2"])
            for k in range(KB):
                act.activation(XH[:, k, :], X[:, k, :], ACT.Copy, scale=gcol("mix_pre1", k)).then_inc(sem("x_hi"), 1)

            barrier(act, PH["q"])
            with act.Fori(0, 4) as i:
                for s in range(2):
                    split_hi(1 - s, None, i + (U_Q // 2 + s), 6 * i + (G_Q + 3 * s))
                    act.wait_ge(bank_free, RING + 6 * i + (G_Q + 3 * s + 3))
                    store(s, qT_s[2 * i + s], STG[:, s, :], "q_st")

            barrier(act, PH["attn"])
            for s in range(2):
                act.wait_ge(sem(f"kt_st{s}"), 16 * 4)
                act.wait_ge(sem(f"q_st{s}"), 16 * 4)
                act.wait_ge(sem(f"kv_st{s}"), 32 * 8)
            for a in range(2):
                act.activation(lam[:, 2 + a:3 + a], lam[:, a:a + 1], ACT.Exp).then_inc(sem("lam_exp"), 1)
            ck = cache_k[0].rearrange("(t p) h a d -> h p t (a d)", p=P)
            cv = cache_v[0].rearrange("(t p) h d -> h p t d", p=P)

            with act.Fori(0, H) as h:
                act.wait_ge(sem("a_split"), h)
                act.dma_start(KR[:, :], kT_s[h]).then_inc(sem("a_in"), 16)
                act.dma_start(QR[:, :], qT_s[h]).then_inc(sem("a_inq"), 16)
                act.dma_start(CK[:, :, :], ck[h]).then_inc(sem("a_in"), 16)
                act.dma_start(VR[:, 0:NT, :], vp[h]).then_inc(sem("a_inv"), 16)
                act.dma_start(VR[:, NT:NT + 4, :], cv[h]).then_inc(sem("a_in"), 16)
                act.dma_start(VR[0:DEC, NT + 4, :], vs[h]).then_inc(sem("a_in"), 16)
                act.wait_ge(sem("a_in"), 64 * h + 64)
                act.wait_ge(sem("a_inq"), 16 * h + 16)
                act.wait_ge(sem("a_inv"), 16 * h + 16)
                act.wait_ge(sem("a_out"), 9 * h)
                act.activation(KH[:, 0:SEQ], KR[:, 0:SEQ], ACT.Copy).then_inc(sem("a_khi"), 1)
                act.activation(KH[:, SCOL:NKEY], KR[:, SEQ:T], ACT.Copy).then_inc(sem("a_khi"), 1)
                act.activation(QH[:, :], QR[:, :], ACT.Copy).then_inc(sem("a_khi"), 1)
                act.activation(VH[:, 0:12, :], VR[:, 0:12, :], ACT.Copy).then_inc(sem("a_khi"), 1)
                act.activation(VH[0:DEC, 12, :], VR[0:DEC, 12, :], ACT.Copy).then_inc(sem("a_khi"), 1)
                act.wait_ge(sem("a_ckT"), h + 1)
                act.activation(KH[:, SEQ:SCOL], PS[:, 7, :], ACT.Copy).then_inc(sem("a_khi"), 1)

                def exps(i):
                    L, n = (P, (i + 1) * P) if i < NT else (DEC, PAST + DEC)
                    f = slice(0, L)
                    act.wait_ge(sem("a_max"), 9 * h + (i + 1))
                    act.wait_ge(sem("a_turned"), 9 * h + i)
                    for m in range(2):
                        act.activation(PR[f, m, 0:n], PS[f, 2 * m:2 * m + 2, :].rearrange("p a b -> p (a b)")[:, 0:n],
                                       ACT.Exp, bias=AS[f, 2 + m:3 + m], scale=ATT_SCALE, accum_out=AS[f, 4 + m:5 + m])\
                            .then_inc(sem("a_exp"), 1)

                def outs(i):
                    L, nk, x0 = (P, i + 1, i * P) if i < NT else (DEC, 5, SEQ)
                    f = slice(0, L)
                    act.wait_ge(sem("a_turned"), 9 * h + (i + 1))
                    act.wait_ge(sem("a_out"), 9 * h + i)
                    for b in range(0, nk, 4):
                        w = min(4, nk - b)
                        if i == NT and b == 4:
                            act.activation(TH[0:DEC, 4, f], PS[0:DEC, 5, 0:L], ACT.Copy).then_inc(sem("a_thi"), 1)
                        else:
                            act.activation(TH[:, b:b + w, f], PS[:, 4 + b // 4, 0:w * L]
                                           .rearrange("p (t q) -> p t q", t=w), ACT.Copy).then_inc(sem("a_thi"), 1)
                    act.wait_ge(sem("a_out"), 9 * h + (i + 1))
                    act.activation(OS[f, :], PS[f, 6, 0:P], ACT.Square, accum_out=AS[f, 8:9]).then_inc(sem("a_ss"), 1)
                    act.wait_ge(sem("a_oT"), 9 * h + (i + 1))
                    act.activation(XH[:, h, x0:x0 + L], PS[:, 7, 0:L], ACT.Copy, scale=gcol("sub", h))\
                        .then_inc(sem("a_xhi"), 1)

                for i in range(NT + 1):
                    exps(i)
                    outs(i)

            barrier(act, PH["wo"])
            dense_hi(KB, G_WO, U_WO)
            boundary("bound2", "b2", "ffn_pre1")
            mlp(1, U_MLP1, G_MLP1)
            boundary("bound3", "b3", None)

            barrier(act, PH["final"])
            for t in range(NCH):
                L, j = (P, t % 2) if t < NT else (DEC, 0)
                act.wait_ge(sem("y_turned"), t + 1)
                if t >= 2:
                    act.wait_ge(sem(f"y_st{j}"), 16 * (t // 2))
                act.activation(STG[0:L, j, 0:512], PS[0:L, 2 * j, :], ACT.Copy).then_inc(sem("y_out_a"), 1)

        @block.vector
        def _(dve):
            mm_done, bank_free, w_hi, w_lo = sem("mm_done"), sem("bank_free"), sem("w_hi"), sem("w_lo")

            def split_lo(s, u1):
                dve.wait_ge(w_hi, u1)
                dve.tensor_tensor(WL[:, s, :], WR[:, s, :], WH[:, s, :].bitcast(F32), ALU.subtract).then_inc(w_lo, 1)

            def norm_inverse(name, dst):
                for g in range(NG):
                    dve.wait_ge(sem("root"), NG * NORMS[name] + g + 1)
                    dve.reciprocal(dst[:, grp(g)], STG[:, 0, grp(g)]).then_inc(sem("inverse"), 1)

            def x_lo(k, gain, name):
                dve.wait_ge(sem("x_hi"), KB * SPLITS[name] + k + 1)
                dve.scalar_tensor_tensor(XL[:, k, :], X[:, k, :], gcol(gain, k), XH[:, k, :].bitcast(F32),
                                         ALU.mult, ALU.subtract).then_inc(sem("x_lo"), 1)

            dve.memset(eps[:, :], EPS)
            dve.memset(half[:, :], -0.5)
            dve.memset(ones[:, :], 1.0)
            dve.sem_inc(bank_free, RING)
            dve.sem_inc(sem("x_cp_d"), 2)
            barrier(dve, PH["load"])
            with dve.Fori(0, NT // 2) as i:
                for j in range(2):
                    dve.wait_ge(sem("x_turned"), 2 * i + (j + 1))
                    dve.tensor_copy(X[:, 4:8, bass.ds(256 * i + P * j, P)],
                                    PS[:, 2 * j + 1, :].rearrange("p (b t) -> p b t", b=4)).then_inc(sem("x_cp_d"), 1)
            dve.wait_ge(sem("gains"), 1)
            dve.tensor_scalar(GN[:, 80:88], GN[:, 80:88], 1.0 - LAM_INIT, None, ALU.mult)
            link = [0]

            def ln(ins):
                link[0] += 1
                ins.then_inc(sem("lam"), 1)
                dve.wait_ge(sem("lam"), link[0])
            dve.wait_ge(sem("consts"), 16 * 14)
            ln(dve.tensor_tensor(lam_in[:, 0, :], lam_in[:, 0, :], lam_in[:, 1, :], ALU.mult))
            ln(dve.tensor_tensor(lam_in[:, 2, :], lam_in[:, 2, :], lam_in[:, 3, :], ALU.mult))
            ln(dve.reduce_sum(lam[:, 0:1], lam_in[:, 0, :], AX))
            ln(dve.reduce_sum(lam[:, 1:2], lam_in[:, 2, :], AX))

            barrier(dve, PH["norm0"])
            split_lo(0, 1)
            for k in range(KB):
                x_lo(k, "mix_pre0", "n0")
            norm_inverse("n0", RB)
            dve.wait_ge(sem("wg_zero"), 2)
            dve.wait_ge(sem("wg_hi"), 2)
            dve.tensor_tensor(WGL[:, :, 0:8], WG[:, :, 0:8], WGH[:, :, 0:8].bitcast(F32), ALU.subtract)
            dve.tensor_tensor(WGL[:, :, 32:40], WG[:, :, 8:16], WGH[:, :, 32:40].bitcast(F32), ALU.subtract)\
                .then_inc(sem("wg_lo"), 1)

            barrier(dve, PH["proj"])
            dve.wait_ge(sem("rst"), 1)
            for g in range(NG):
                dve.wait_ge(sem("gates_mm"), g + 1)
                dve.tensor_tensor(rows[0:H, R_LI, grp(g)], PS[0:H, 5 + g, 0:G], RB[0:H, grp(g)], ALU.mult)\
                    .then_inc(sem("gates_read"), 1)
                dve.tensor_tensor(rows[0:H, R_LF, grp(g)], PS[32:40, 5 + g, 0:G], RB[0:H, grp(g)], ALU.mult)\
                    .then_inc(sem("gates_read"), 1)

            def take(s, g, n):
                dve.wait_ge(mm_done, n)
                dve.tensor_tensor(STG[:, s, grp(g)], PS[:, 3 * s + g, 0:G], RB[:, grp(g)], ALU.mult)\
                    .then_inc(bank_free, 1)

            with dve.Fori(0, N_PROJ // 2) as i:
                for s in range(2):
                    split_lo(1 - s, 2 * i + (s + 2))
                    dve.wait_ge(sem(f"stg{s}"), 16 * i)
                    for g in range(NG):
                        take(s, g, 6 * i + (3 * s + g + 1))

            barrier(dve, PH["gates"])
            row = lambda r: rows[0:H, r, :]
            li, lf, m_, fc, u_, inter, gg, tmp = (row(r) for r in (R_LI, R_LF, R_M, R_FC, R_U, R_INTER, R_G, R_EM))
            glink = [0]

            def gl(ins, other=None):
                glink[0] += 1
                ins.then_inc(sem("g_dve"), 1)
                dve.wait_ge(sem("g_dve"), glink[0])
            gl(dve.tensor_scalar(li, li, bg[:, 0:1], None, ALU.add))
            gl(dve.tensor_scalar(lf, lf, bg[:, 1:2], None, ALU.add))
            gl(dve.tensor_scalar(gg, lf, -1.0, None, ALU.mult))
            dve.tensor_tensor(tmp, lf, gg, ALU.max).then_inc(sem("g_abs"), 1)
            dve.wait_ge(sem("g_exp"), 1)
            dve.tensor_scalar(tmp, tmp, 1.0, None, ALU.add).then_inc(sem("g_one"), 1)
            gl(dve.tensor_scalar(lf, lf, 0.0, None, ALU.min))
            dve.wait_ge(sem("g_exp"), 2)
            gl(dve.tensor_tensor(lf, lf, tmp, ALU.subtract))
            gl(dve.tensor_tensor_scan(fc, RST[:, :], lf, 0.0, ALU.mult, ALU.add))
            gl(dve.tensor_tensor_scan(rows[0:H, R_M, 0:SEQ], rows[0:H, R_LF, 0:SEQ], rows[0:H, R_LI, 0:SEQ], 0.0,
                                      ALU.add, ALU.max))
            dve.tensor_tensor_scan(rows[0:H, R_M, SEQ:T], rows[0:H, R_LF, SEQ:T], rows[0:H, R_LI, SEQ:T], bg[:, 2:3],
                                   ALU.add, ALU.max).then_inc(sem("g_m"), 1)
            dve.wait_ge(sem("g_m"), 1)
            gl(dve.memset(MP[:, 0:1], 0.0))
            gl(dve.tensor_copy(MP[:, 1:NT], rows[0:H, R_M, LC - 1:SEQ - LC:LC]))
            gl(dve.tensor_copy(MP[:, NT:NCH], bg[:, 2:3]))
            gl(dve.tensor_tensor(gg, li, fc, ALU.subtract))
            gl(dve.tensor_tensor(u_, fc, m_, ALU.subtract))
            dve.tensor_tensor(rows[0:H, R_INTER, 0:SEQ].rearrange("h (c t) -> h c t", c=NT),
                              rows[0:H, R_U, 0:SEQ].rearrange("h (c t) -> h c t", c=NT),
                              MP[:, 0:NT].unsqueeze(2).to_broadcast([H, NT, LC]), ALU.add)
            dve.tensor_scalar(rows[0:H, R_INTER, SEQ:T], rows[0:H, R_U, SEQ:T], MP[:, NT:NCH], None, ALU.add)\
                .then_inc(sem("g_inter"), 1)

            barrier(dve, PH["mlstm"])
            dve.memset(VC[:, :, DV:DV + 1], 1.0).then_inc(sem("c_ones"), 1)
            dve.memset(CB[:, :, :, :], 0.0)
            dve.sem_inc(sem("c_prev"), 1)

            def chunk(L, c1, xcol):
                f = slice(0, L)
                w = lambda name, n: dve.wait_ge(sem(name), n)
                w("c_turned", c1)
                dve.tensor_copy(VC[f, 4:8, 0:DV], PS[f, 2, :].rearrange("p (h e) -> p h e", h=4)).then_inc(sem("c_vc2"), 1)
                dve.tensor_copy(MS[f, 0:2, :], PS[f, 7, 0:2 * H].rearrange("p (r h) -> p r h", r=2))\
                    .then_inc(sem("c_cols"), 1)
                w("c_spread", c1)
                for b in range(2):
                    dve.tensor_tensor(DT[f, 4 * b:4 * b + 4, f], PS[f, 3 + b, 0:4 * L].rearrange("p (h t) -> p h t", h=4),
                                      mask[f, f].unsqueeze(1).to_broadcast([L, 4, L]), ALU.add)\
                        .then_inc(sem("c_masked"), 1)
                dve.tensor_copy(DEC4[:, :], PS[:, 5, L - 1:4 * L:L]).then_inc(sem("c_dec"), 1)
                w("ch_in", 32 * c1)
                dve.tensor_tensor(QI[:, :, f], CH[:, 0:4, f], PS[:, 5, 0:4 * L].rearrange("p (a t) -> p a t", a=4),
                                  ALU.mult).then_inc(sem("c_qi"), 1)
                w("c_scores", c1)
                w("c_dt", 8 * c1)
                for a in range(2):
                    dve.scalar_tensor_tensor(SD[f, a:H:2, f], PS[f, 6 + a, 0:4 * L].rearrange("p (h t) -> p h t", h=4),
                                             K_SCALE, DT[f, a:H:2, f], ALU.mult, ALU.mult).then_inc(sem("c_sd"), 1)
                w("c_kn", c1)
                dve.tensor_tensor(KN[f, :].rearrange("p (h d) -> p h d", h=H), KN[f, :].rearrange("p (h d) -> p h d", h=H),
                                  DT[f, :, L - 1:L].to_broadcast([L, H, DK]), ALU.mult).then_inc(sem("c_kw"), 1)
                w("c_hn", 4 * c1)
                qn = HN[f, :, DV]
                n0 = 8 * (c1 - 1) if isinstance(c1, int) else c1 * 8 - 8

                def cl(k, ins):
                    ins.then_inc(sem("c_den"), 1)
                    dve.wait_ge(sem("c_den"), n0 + k)
                cl(1, dve.scalar_tensor_tensor(MS[f, 2, :], qn, -1.0, qn, ALU.mult, ALU.max))
                cl(2, dve.tensor_tensor(MS[f, 2, :], MS[f, 2, :], MS[f, 1, :], ALU.max))
                cl(3, dve.reciprocal(MS[f, 3, :], MS[f, 2, :]))
                w("c_sn", c1)
                cl(4, dve.reduce_sum(MS[f, 4, :], DT[f, :, :], AX))
                cl(5, dve.tensor_tensor(MS[f, 5, :], MS[f, 3, :], MS[f, 3, :], ALU.mult))
                cl(6, dve.tensor_tensor(MS[f, 5, :], MS[f, 5, :], MS[f, 4, :], ALU.mult))
                cl(7, dve.tensor_scalar(MS[f, 5, :], MS[f, 5, :], 1.0 / DV, EPS, ALU.mult, ALU.add))
                w("c_pow", c1)
                cl(8, dve.tensor_tensor(MS[f, 7, :], MS[f, 6, :], MS[f, 3, :], ALU.mult))
                dve.tensor_tensor(HN[f, :, 0:DV], HN[f, :, 0:DV], MS[f, 7, :].unsqueeze(2).to_broadcast([L, H, DV]),
                                  ALU.mult).then_inc(sem("c_hs"), 1)
                w("c_kv", c1)
                w("c_num", c1)
                cu = 3 * (c1 - 1) if isinstance(c1, int) else c1 * 3 - 3
                dve.tensor_tensor(CB[:, :, :, :].rearrange("p q a b -> p q (a b)"),
                                  CB[:, :, :, :].rearrange("p q a b -> p q (a b)"),
                                  DEC4[:, :].unsqueeze(2).to_broadcast([P, NPAIR, 2 * (DV + 1)]), ALU.mult)\
                    .then_inc(sem("c_upd"), 1)
                w("c_upd", cu + 1)
                for a in range(2):
                    r = slice(64 * a, 64 * a + 64)
                    dve.tensor_tensor(CB[r, :, a, :], CB[r, :, a, :], PS[r, 4:8, a * (DV + 1):(a + 1) * (DV + 1)],
                                      ALU.add).then_inc(sem("c_upd"), 1)
                w("c_hT", c1)
                for b in range(2):
                    dve.tensor_tensor(SD[:, 4 * b:4 * b + 4, f], PS[:, b, 0:4 * L].rearrange("p (h t) -> p h t", h=4),
                                      CH[:, 16 + 4 * b:20 + 4 * b, f], ALU.mult).then_inc(sem("c_hf"), 1)
                w("c_xh", c1)
                dve.tensor_tensor(XL[:, :, xcol], SD[:, :, f], XH[:, :, xcol].bitcast(F32), ALU.subtract)\
                    .then_inc(sem("c_prev"), 1)

            with dve.Fori(0, NT) as c:
                chunk(LC, c + 1, bass.ds(c * P, P))
            dve.wait_ge(sem("c_state"), 1)
            chunk(DEC, NCH, slice(SEQ, T))

            def dense_y(u0, g0):
                with dve.Fori(0, KB // 2) as i:
                    for s in range(2):
                        split_lo(1 - s, 2 * i + (u0 + s + 2))
                        for g in range(NG):
                            dve.wait_ge(mm_done, 6 * i + (g0 + 3 * s + g + 1))
                            dve.tensor_copy(Y[:, 2 * i + s, grp(g)], PS[:, 3 * s + g, 0:G]).then_inc(bank_free, 1)

            barrier(dve, PH["out"])
            dense_y(U_OUT, G_OUT)

            def boundary(n, name, post, pre):
                barrier(dve, PH[n])
                norm_inverse(name + "y", RB)
                for k in range(KB):
                    dve.wait_ge(sem("y_scaled"), KB * BOUNDS[name] + k + 1)
                    dve.scalar_tensor_tensor(X[:, k, :], Y[:, k, :], gcol(post, k), X[:, k, :], ALU.mult, ALU.add)\
                        .then_inc(sem("x_new"), 1)
                    if pre and k >= 1:
                        x_lo(k - 1, pre, name)
                if pre:
                    x_lo(KB - 1, pre, name)
                    norm_inverse(name + "x", RB)

            def mlp(l, u0, g0):
                barrier(dve, PH[f"mlp{l}"])
                dve.wait_ge(sem("y_zero"), l + 1)

                def group(j, last):
                    def low(n):
                        dve.wait_ge(sem("h_hi"), 12 * j + (96 * l + n + 1))
                        dve.wait_ge(sem("h_sq"), 12 * j + (96 * l + n + 1))
                        dve.tensor_tensor(HL[:, n // 3, grp(n % 3)], M2[:, n % 2, :],
                                          HH[:, n // 3, grp(n % 3)].bitcast(F32), ALU.subtract).then_inc(sem("h_lo"), 1)
                    for m in range(4):
                        split_lo((m + 1) % 2, 8 * j + (u0 + m + 2))
                        for g in range(NG):
                            n = 3 * m + g
                            dve.wait_ge(mm_done, 36 * j + (g0 + n + 1))
                            dve.scalar_tensor_tensor(MT[:, n % 2, :], PS[:, 3 * (m % 2) + g, 0:G], 0.0, RB[:, grp(g)],
                                                     ALU.max, ALU.mult).then_inc(bank_free, 1)
                            if n:
                                low(n - 1)
                    low(11)
                    for d in range(4):
                        if not (last and d == 3):
                            split_lo((d + 1) % 2, 8 * j + (u0 + d + 6))
                        for b in range(2):
                            for g in range(NG):
                                n = 12 + 6 * d + 3 * b + g
                                dve.wait_ge(mm_done, 36 * j + (g0 + n + 1))
                                y = Y[:, 2 * d + b, grp(g)]
                                dve.tensor_tensor(y, y, PS[:, 3 * b + g, 0:G], ALU.add).then_inc(bank_free, 1)
                if l == 0:
                    with dve.Fori(0, FFG) as j:
                        group(j, False)
                else:
                    with dve.Fori(0, FFG - 1) as j:
                        group(j, False)
                    group(FFG - 1, True)

            boundary("bound0", "b0", "mix_post0", "ffn_pre0")
            mlp(0, U_MLP0, G_MLP0)
            boundary("bound1", "b1", "ffn_post0", "kv")

            barrier(dve, PH["kv"])

            def kv_unit(i, s, stored):
                split_lo(1 - s, 2 * i + (U_KV + s + 2))
                dve.wait_ge(sem("kv_turned"), 6 * i + 3 * s)
                dve.wait_ge(sem(f"kt_st{s}"), stored)
                for g in range(NG):
                    take(s, g, 6 * i + (G_KV + 3 * s + g + 1))
            with dve.Fori(0, 4) as i:
                for s in range(2):
                    kv_unit(i, s, 16 * i)
            with dve.Fori(4, 8) as i:
                for s in range(2):
                    kv_unit(i, s, 16 * 4)

            barrier(dve, PH["norm2"])
            for k in range(KB):
                x_lo(k, "mix_pre1", "n2")

            barrier(dve, PH["q"])
            with dve.Fori(0, KB // 2) as i:
                for s in range(2):
                    split_lo(1 - s, 2 * i + (U_Q + s + 2))
                    dve.wait_ge(sem(f"kt_st{s}"), 16 * 4)
                    dve.wait_ge(sem(f"q_st{s}"), 16 * i)
                    for g in range(NG):
                        take(s, g, 6 * i + (G_Q + 3 * s + g + 1))

            barrier(dve, PH["attn"])
            dve.wait_ge(sem("lam_exp"), 2)
            ln(dve.tensor_tensor(lam[:, 4:5], lam[:, 3:4], lam[:, 2:3], ALU.subtract))
            ln(dve.tensor_scalar(lam[:, 5:6], lam[:, 4:5], LAM_INIT, None, ALU.subtract))
            dve.wait_ge(sem("mask_in"), 5)
            dve.tensor_copy(MA[:, :], MF[:, 0, :])
            dve.tensor_copy(MB[:, :], MF[:, 1, :]).then_inc(sem("mask_r"), 1)

            with dve.Fori(0, H) as h:
                sub = ALU.subtract
                dve.wait_ge(sem("a_khi"), 6 * h + 6)
                for o, a, b in ((KL[:, 0:SEQ], KR[:, 0:SEQ], KH[:, 0:SEQ]), (KL[:, SCOL:NKEY], KR[:, SEQ:T], KH[:, SCOL:NKEY]),
                                (QL[:, :], QR[:, :], QH[:, :]), (KL[:, SEQ:SCOL], PS[:, 7, :], KH[:, SEQ:SCOL]),
                                (VL[:, 0:12, :], VR[:, 0:12, :], VH[:, 0:12, :]),
                                (VL[0:DEC, 12, :], VR[0:DEC, 12, :], VH[0:DEC, 12, :])):
                    last = dve.tensor_tensor(o, a, b.bitcast(F32), sub)
                last.then_inc(sem("a_split"), 1)

                def chain(i, k, ins):
                    ins.then_inc(sem("a_small"), 1)
                    dve.wait_ge(sem("a_small"), 90 * h + (10 * i + k))

                def maxima(i):
                    L, n = (P, (i + 1) * P) if i < NT else (DEC, PAST + DEC)
                    f = slice(0, L)
                    dve.wait_ge(sem("a_scores"), 9 * h + (i + 1))
                    for m in range(2):
                        ins = dve.reduce_max(AS[f, m:m + 1], PS[f, 2 * m:2 * m + 2, :].rearrange("p a b -> p (a b)")[:, 0:n], AX)
                        chain(i, 1 + m, ins)
                    dve.tensor_scalar(AS[f, 2:4], AS[f, 0:2], -ATT_SCALE, None, ALU.mult).then_inc(sem("a_max"), 1)

                def rest(i):
                    L, n = (P, (i + 1) * P) if i < NT else (DEC, PAST + DEC)
                    nk = i + 1 if i < NT else 5
                    x0 = i * P if i < NT else SEQ
                    f = slice(0, L)
                    dve.wait_ge(sem("a_exp"), 18 * h + (2 * i + 2))
                    chain(i, 3, dve.reciprocal(AS[f, 6:8], AS[f, 4:6]))
                    chain(i, 4, dve.tensor_tensor(AS[f, 9:10], AS[f, 4:5], AS[f, 7:8], ALU.mult))
                    chain(i, 5, dve.tensor_tensor(AS[f, 10:11], AS[f, 9:10], lam[f, 5:6], ALU.mult))
                    dve.scalar_tensor_tensor(PR[f, 0, 0:n], PR[f, 1, 0:n], AS[f, 10:11], PR[f, 0, 0:n], ALU.mult, ALU.add)\
                        .then_inc(sem("a_comb"), 1)
                    nb = [(b, min(4, nk - b)) for b in range(0, nk, 4)]
                    hi0 = sum(((j + 1 if j < NT else 5) + 3) // 4 for j in range(i))
                    for q, (b, w) in enumerate(nb):
                        dve.wait_ge(sem("a_thi"), 14 * h + (hi0 + q + 1))
                        if i == NT and b == 4:
                            o, a, c = TL[0:DEC, 4, f], PS[0:DEC, 5, 0:L], TH[0:DEC, 4, f]
                        else:
                            o, c = TL[:, b:b + w, f], TH[:, b:b + w, f]
                            a = PS[:, 4 + b // 4, 0:w * L].rearrange("p (t q) -> p t q", t=w)
                        ins = dve.tensor_tensor(o, a, c.bitcast(F32), sub)
                    ins.then_inc(sem("a_tlo"), 1)
                    dve.wait_ge(sem("a_ss"), 9 * h + (i + 1))
                    chain(i, 6, dve.tensor_tensor(AS[f, 11:12], AS[f, 6:7], AS[f, 6:7], ALU.mult))
                    chain(i, 7, dve.tensor_tensor(AS[f, 12:13], AS[f, 11:12], AS[f, 8:9], ALU.mult))
                    chain(i, 8, dve.tensor_scalar(AS[f, 13:14], AS[f, 12:13], 1.0 / P, EPS, ALU.mult, ALU.add))
                    dve.wait_ge(sem("a_pow"), 9 * h + (i + 1))
                    chain(i, 9, dve.tensor_tensor(AS[f, 15:16], AS[f, 14:15], AS[f, 6:7], ALU.mult))
                    chain(i, 10, dve.tensor_scalar(ON[f, :], PS[f, 6, 0:P], AS[f, 15:16], None, ALU.mult))
                    dve.sem_inc(sem("a_on"), 1)
                    dve.wait_ge(sem("a_xhi"), 9 * h + (i + 1))
                    dve.scalar_tensor_tensor(XL[:, h, x0:x0 + L], PS[:, 7, 0:L], gcol("sub", h),
                                             XH[:, h, x0:x0 + L].bitcast(F32), ALU.mult, ALU.subtract)\
                        .then_inc(sem("a_xlo"), 1)

                for i in range(NT + 1):
                    maxima(i)
                    rest(i)

            barrier(dve, PH["wo"])
            dense_y(U_WO, G_WO)
            boundary("bound2", "b2", "mix_post1", "ffn_pre1")
            mlp(1, U_MLP1, G_MLP1)
            boundary("bound3", "b3", "ffn_post1", None)

            barrier(dve, PH["final"])
            for t in range(NCH):
                L, j = (P, t % 2) if t < NT else (DEC, 0)
                dve.wait_ge(sem("y_turned"), t + 1)
                if t >= 2:
                    dve.wait_ge(sem(f"y_st{j}"), 16 * (t // 2))
                dve.tensor_copy(STG[0:L, j, 512:D], PS[0:L, 2 * j + 1, :]).then_inc(sem("y_out_d"), 1)

        @block.gpsimd
        def _(pool):
            def add_squares(name):
                n = KB * NORMS[name]
                for k in range(KB):
                    pool.wait_ge(sem("squared"), n + k + 1)
                    if k == 0:
                        pool.tensor_copy(SQ[:, :], STG[:, 0, :]).then_inc(sem("sq_sum"), 1)
                    else:
                        pool.wait_ge(sem("sq_sum"), n + k)
                        pool.tensor_tensor(SQ[:, :], SQ[:, :], STG[:, k % 2, :], ALU.add).then_inc(sem("sq_sum"), 1)

            pool.memset(ident[:, :], 0.0).then_inc(sem("ident"), 1)
            pool.wait_ge(sem("ident"), 1)
            pool.affine_select(out=ident[:, :], in_=ident[:, :], compare_op=ALU.not_equal, fill=1.0, base=0,
                               pattern=[[-1, P]], channel_multiplier=1).then_inc(sem("ident"), 1)
            pool.memset(mask[:, :], 0.0).then_inc(sem("setup"), 1)
            pool.memset(WGH[:, :, :].bitcast(F32), 0.0).then_inc(sem("wg_zero"), 1)
            pool.memset(WGL[:, :, :].bitcast(F32), 0.0).then_inc(sem("wg_zero"), 1)
            pool.memset(RST[:, :], 1.0).then_inc(sem("setup"), 1)
            pool.wait_ge(sem("setup"), 2)
            pool.affine_select(out=mask[:, :], in_=mask[:, :], compare_op=ALU.is_ge, fill=NEG, base=0,
                               pattern=[[1, LC]], channel_multiplier=-1).then_inc(sem("setup"), 1)
            pool.memset(RST[:, 0:T:LC], 0.0).then_inc(sem("rst"), 1)
            barrier(pool, PH["load"])
            barrier(pool, PH["norm0"])
            add_squares("n0")
            barrier(pool, PH["proj"])
            for h in range(H):
                pool.wait_ge(sem("o_sig"), h + 1)
                pool.tensor_scalar(STG[:, h % 2, :], STG[:, h % 2, :], gcol("h", h), 1.0, ALU.mult, ALU.mult)\
                    .then_inc(sem("o_gain"), 1)
            barrier(pool, PH["gates"])
            barrier(pool, PH["mlstm"])

            def mlstm_consts():
                pool.memset(SEL[:, :, :], 0.0).then_inc(sem("sel"), 1)
                pool.memset(SELP[:, :, :], 0.0).then_inc(sem("sel"), 1)
                pool.wait_ge(sem("sel"), 2)
                pool.affine_select(out=SEL[:, :, :], in_=SEL[:, :, :], compare_op=ALU.not_equal, fill=1.0, base=0,
                                   pattern=[[-1, H], [0, P]], channel_multiplier=1).then_inc(sem("sel"), 1)
                pool.affine_select(out=SELP[:, :, :].rearrange("h q (a d) -> h q a d", a=2),
                                   in_=SELP[:, :, :].rearrange("h q (a d) -> h q a d", a=2),
                                   compare_op=ALU.not_equal, fill=1.0, base=0,
                                   pattern=[[-2, NPAIR], [-1, 2], [0, 64]], channel_multiplier=1).then_inc(sem("sel"), 1)
            mlstm_consts()
            c_pow = sem("c_pow")
            with pool.Fori(0, NT) as c:
                pool.wait_ge(sem("c_den"), 8 * c + 7)
                pool.tensor_tensor(MS[:, 6, :], MS[:, 5, :], half[:, :], ALU.pow).then_inc(c_pow, 1)
            pool.wait_ge(sem("c_den"), 8 * NT + 7)
            pool.tensor_tensor(MS[0:DEC, 6, :], MS[0:DEC, 5, :], half[0:DEC, :], ALU.pow).then_inc(c_pow, 1)

            def boundary(n, name, pre=True):
                barrier(pool, PH[n])
                add_squares(name + "y")
                for k in range(KB):
                    pool.wait_ge(sem("inverse"), NG * (NORMS[name + "y"] + 1))
                    pool.tensor_tensor(Y[:, k, :], Y[:, k, :], RB[:, :], ALU.mult).then_inc(sem("y_scaled"), 1)
                if pre:
                    add_squares(name + "x")

            def mlp(l, u0, g0):
                barrier(pool, PH[f"mlp{l}"])
                pool.memset(Y[:, :, :], 0.0).then_inc(sem("y_zero"), 1)
                with pool.Fori(0, FFG) as j:
                    for n in range(12):
                        pool.wait_ge(sem("bank_free"), RING + 36 * j + (g0 + n + 1))
                        pool.tensor_tensor(M2[:, n % 2, :], MT[:, n % 2, :], MT[:, n % 2, :], ALU.mult)\
                            .then_inc(sem("h_sq"), 1)

            barrier(pool, PH["out"])
            boundary("bound0", "b0")
            mlp(0, U_MLP0, G_MLP0)
            boundary("bound1", "b1")
            barrier(pool, PH["kv"])
            barrier(pool, PH["norm2"])
            barrier(pool, PH["q"])
            barrier(pool, PH["attn"])
            pool.memset(MF[:, :, :], 0.0).then_inc(sem("mask_in"), 1)
            pool.wait_ge(sem("mask_in"), 1)
            for r in (0, 64):
                pool.memset(MF[r:r + 1, 0, 0:64], 1.0).then_inc(sem("mask_in"), 1)
                pool.memset(MF[r:r + 1, 1, 64:P], NEG).then_inc(sem("mask_in"), 1)
            with pool.Fori(0, H) as h:
                for i in range(NT + 1):
                    f = slice(0, P if i < NT else DEC)
                    pool.wait_ge(sem("a_small"), 90 * h + (10 * i + 8))
                    pool.tensor_tensor(AS[f, 14:15], AS[f, 13:14], half[f, 0:1], ALU.pow).then_inc(sem("a_pow"), 1)
            barrier(pool, PH["wo"])
            boundary("bound2", "b2")
            mlp(1, U_MLP1, G_MLP1)
            boundary("bound3", "b3", False)
            barrier(pool, PH["final"])


_INS = ['x_prompt', 'x_sample', 'cache_k', 'cache_v', 'state_c', 'state_n', 'state_m', 'w_in_a', 'b_i_a', 'b_f_a',
        'g_h_a', 'w_out_a', 'g_kv', 'w_kv', 'w_q_b', 'lambda_q1', 'lambda_k1', 'lambda_q2', 'lambda_k2', 'g_sub_b',
        'w_o_b', 'g_mix_pre', 'g_mix_post', 'g_ffn_pre', 'g_ffn_post', 'w_up', 'w_down']
_OUTS = [(1, SEQ, D), (1, DEC, D), (1, 1, H, DK, DV), (1, 1, H, DK), (1, 1, H), (1, SEQ, H, 2, 64), (1, SEQ, H, 128),
         (1, 1, H, DK, DV), (1, 1, H, DK), (1, 1, H), (1, DEC, H, 2, 64), (1, DEC, H, 128)]


def kernel(**inputs):
    import numpy as _np
    import concourse.bacc as _bacc
    from concourse import mybir as _mybir
    from concourse.bass_utils import run_bass_kernel_spmd as _run

    nc = _bacc.Bacc("TRN2", target_bir_lowering=False, num_devices=1, dynamic_dma_scratch_size=1024)
    arrays, args = {}, []
    for name in _INS:
        a = _np.ascontiguousarray(inputs[name])
        arrays[f"in_{name}"] = a
        args.append(nc.dram_tensor(f"in_{name}", a.shape, _mybir.dt.from_np(a.dtype), kind="ExternalInput").ap())
    for i, shape in enumerate(_OUTS):
        args.append(nc.dram_tensor(f"out_{i}", shape, _mybir.dt.float32, kind="ExternalOutput").ap())
    for name, n in (("proj_s", 24), ("kT_s", H), ("qT_s", H)):
        args.append(nc.dram_tensor(name, (n, P, T), _mybir.dt.float32).ap())
    stream_step(nc, *args)
    r = _run(nc, [arrays], core_ids=[0])
    return tuple(r.results[0][f"out_{i}"] for i in range(len(_OUTS)))
```

```python
from contextlib import ExitStack
import math

import concourse.bass as bass
from concourse import mybir

F32 = mybir.dt.float32
F32R = mybir.dt.float32r
ALU = mybir.AluOpType
ACT = mybir.ActivationFunctionType
AX = mybir.AxisListType.X

P = 128
D = 1024
KB = D // P
SEQ, DEC = 1024, 32
T = SEQ + DEC
NG = 3
G = T // NG
PAST = 512
H = 8
DK, DV = 64, 128
LC = 128
NT = SEQ // P
NCH = NT + 1
NPAIR = H // 2
DFF = 4 * D
FFG = DFF // 512
EPS = 1e-6
NEG = -1e30
LAM_INIT = 0.8 - 0.6 * math.exp(-0.3)
ATT_SCALE = 64 ** -0.5
K_SCALE = DK ** -0.5
SCOL = SEQ + PAST
NKEY = SCOL + DEC

U_PROJ, N_PROJ = 0, 24
U_OUT = U_PROJ + N_PROJ
U_MLP0 = U_OUT + KB
U_KV, N_KV = U_MLP0 + 8 * FFG, 16
U_Q = U_KV + N_KV
U_WO = U_Q + KB
U_MLP1 = U_WO + KB
G_PROJ = 0
G_OUT = G_PROJ + NG * N_PROJ
G_MLP0 = G_OUT + NG * KB
G_KV = G_MLP0 + 36 * FFG
G_Q = G_KV + NG * N_KV
G_WO = G_Q + NG * KB
G_MLP1 = G_WO + NG * KB
RING = 6

GAINS = ["mix_pre0", "mix_pre1", "mix_post0", "mix_post1", "ffn_pre0", "ffn_pre1", "ffn_post0", "ffn_post1",
         "kv", "h", "sub"]
R_U, R_INTER, R_G, R_EM, R_LI, R_LF, R_M, R_FC = range(8)


def stream_step(nc, x_prompt, x_sample, cache_k, cache_v, state_c, state_n, state_m, w_in, b_i, b_f, g_h, w_out,
                g_kv, w_kv, w_q, lq1, lk1, lq2, lk2, g_sub, w_o, g_mix_pre, g_mix_post, g_ffn_pre, g_ffn_post,
                w_up, w_down, y_prompt, y_sample, c_prompt, n_prompt, m_prompt, k_prompt, v_prompt,
                c_sample, n_sample, m_sample, k_sample, v_sample, proj_s, kT_s, o_s):
    with ExitStack() as ctx:
        def sb(name, shape, dt=F32, scope=ctx):
            return scope.enter_context(nc.sbuf_tensor(name, shape, dt))

        sems = {}

        def sem(name):
            if name not in sems:
                sems[name] = ctx.enter_context(nc.semaphore(name))
            return sems[name]

        X = sb("X", [P, KB, T])
        XH = sb("XH", [P, KB, T], F32R)
        XL = sb("XL", [P, KB, T], F32R)
        WR = sb("WR", [P, 2, D])
        WH = sb("WH", [P, 2, D], F32R)
        WL = sb("WL", [P, 2, D], F32R)
        RB = sb("RB", [P, T])
        STG = sb("STG", [P, 2, T])
        SQ = sb("SQ", [P, T])
        TV = sb("TV", [P, 3, NCH])
        ident = sb("ident", [P, P])
        ones = sb("ones", [P, P])
        GN = sb("GN", [P, len(GAINS) * KB])
        lam = sb("lam", [P, 8])
        half = sb("half", [P, NCH])
        mean_eps = sb("mean_eps", [P, 2])
        bg = sb("bg", [H, 4])
        MP = sb("MP", [H, NCH])
        with ExitStack() as sc:
            VR = sb("VR", [P, 13, P], F32, sc)
            CK = sb("CK", [P, 4, P], F32, sc)
            KH = sb("KH", [P, NKEY], F32R, sc)
            KL = sb("KL", [P, NKEY], F32R, sc)
            QH = sb("QH", [P, 2, T], F32R, sc)
            QL = sb("QL", [P, 2, T], F32R, sc)
            VH = sb("VH", [P, 13, P], F32R, sc)
            VL = sb("VL", [P, 13, P], F32R, sc)
            P0 = sb("P0", [P, 2, D], F32, sc)
            P1 = sb("P1", [P, D], F32, sc)
            TH = sb("TH", [P, 2, KB, P], F32R, sc)
            TL = sb("TL", [P, 2, KB, P], F32R, sc)
            OC = sb("OC", [P, 2, P], F32, sc)
            ON = sb("ON", [P, 2, P], F32, sc)
            AS = sb("AS", [P, 6, 16], F32, sc)
            MA = sb("MA", [P, P], F32R, sc)
            MB = sb("MB", [P, P], F32R, sc)
        QR, KR, OTS = STG[:, 0, :], STG[:, 1, :], SQ[:, :]
        with ExitStack() as sc:
            OT = sb("OT", [P, 2, NCH, P], F32, sc)
        Y = sb("Y", [P, KB, T])
        rows = Y
        XG = Y[:, :, :].rearrange("p k t -> p (k t)")[:, 0:2 * D].rearrange("p (j b t) -> p j b t", j=2, b=KB)
        with ExitStack() as sc:
            HH = sb("HH", [P, 4, T], F32R, sc)
            HL = sb("HL", [P, 4, T], F32R, sc)
            MT = sb("MT", [P, 2, G], F32, sc)
            M2 = sb("M2", [P, 2, G], F32, sc)
        with ExitStack() as sc:
            WG = sb("WG", [P, KB, 16], F32, sc)
            WGH = sb("WGH", [P, KB, 40], F32R, sc)
            WGL = sb("WGL", [P, KB, 40], F32R, sc)
            RST = sb("RST", [H, T], F32, sc)
            gain_rows = sb("gain_rows", [len(GAINS) * KB, P], F32, sc)
            lam_in = sb("lam_in", [P, 4, DK], F32, sc)
        with ExitStack() as sc:
            CH = sb("CH", [P, 24, LC], F32, sc)
            RC = sb("RC", [H, 4, LC], F32, sc)
            KN = sb("KN", [P, 4 * P], F32, sc)
            VC = sb("VC", [P, H, DV + 1], F32, sc)
            DT = sb("DT", [P, H, LC], F32, sc)
            SD = sb("SD", [P, H, LC], F32, sc)
            QI = sb("QI", [P, NPAIR, LC], F32, sc)
            CB = sb("CB", [P, NPAIR, 2, DV + 1], F32, sc)
            HN = sb("HN", [P, H, DV + 1], F32, sc)
            MS = sb("MS", [P, 8, H], F32, sc)
            DEC4 = sb("DEC4", [P, NPAIR], F32, sc)
            mask = sb("mask", [P, LC], F32, sc)
            SEL = sb("SEL", [H, H, P], F32, sc)
            SELP = sb("SELP", [H, NPAIR, P], F32, sc)
        PS = ctx.enter_context(nc.psum_tensor("PS", [P, 8, 512], F32))
        KN3 = KN[:, :].rearrange("p (a b) -> p a b", b=P)

        def gcol(name, k):
            j = GAINS.index(name) * KB
            return GN[:, j + k:j + k + 1] if isinstance(k, int) else GN[:, bass.ds(k + j, 1)]

        def grp(g):
            return slice(g * G, (g + 1) * G)

        def tok(t, L=P):
            return bass.ds(t * P, L)

        def y_half(t, b):
            if t < NT:
                return Y[:, :, :].rearrange("p k t -> p (k t)")[:, t * D + 512 * b:t * D + 512 * b + 512]
            return STG[0:DEC, 0, 512 * b:512 * b + 512]

        block = ctx.enter_context(nc.Block())
        w_in2, w_out2 = w_in[0], w_out[0]

        def weight_cols(w, c):
            return w[:, bass.ds(c * P, P)].rearrange("(k p) n -> p k n", p=P)

        def barrier(e, n):
            e.drain().then_inc(sem("phase"), 1)
            e.wait_ge(sem("phase"), 4 * n)

        PHASES = ["load", "proj", "gates", "mlstm", "out"]
        TPT = 2 * (NT + 1)

        class Tile:
            def __init__(self, q, m):
                self.hp, self.i = (m % TPT) // (NT + 1), m % (NT + 1)
                self.n = TPT * q + m
                self.h = 2 * q + m // (NT + 1)
                self.par, self.slot = m % 2, m % 6
                s = self.i == NT
                self.L = DEC if s else P
                self.keys = PAST + DEC if s else (self.i + 1) * P
                self.q0, self.k0 = (SEQ, SEQ) if s else (self.i * P, 0)
                self.blocks = [(b, P if b < 4 or not s else DEC) for b in range(-(-self.keys // P))]
                self.v0 = NT if s else 0
                self.f = slice(0, self.L)
                self.sample = s

            def bank(self, m, c):
                return 2 * m + (self.i % 2 if self.i < 4 else c // 512)

            def score(self, m):
                if self.keys <= 512:
                    return PS[self.f, self.bank(m, 0), 0:self.keys]
                return PS[self.f, 2 * m:2 * m + 2, :].rearrange("p a b -> p (a b)")[:, 0:self.keys]

            def turned(self, T4, par=None):
                out = []
                for b in range(0, len(self.blocks), 4):
                    w = min(4, len(self.blocks) - b)
                    if self.sample and b == 4:
                        out.append((PS[0:DEC, 5, 0:self.L], T4[0:DEC, self.par, 4, self.f]))
                    else:
                        out.append((PS[:, 4 + b // 4, 0:w * self.L].rearrange("p (t q) -> p t q", t=w),
                                    T4[:, self.par, b:b + w, self.f]))
                return out

            def number(self, c, w=1):
                return AS[self.f, self.slot, c:c + w]

        FILL = range(1, 7)
        PH = {n: i + 1 for i, n in enumerate(PHASES)}

        NORMS = {n: i for i, n in enumerate(["n0", "b0y", "b0x", "b1y", "b1x", "b2y", "b2x", "b3y"])}
        SPLITS = {n: i for i, n in enumerate(["b0", "b1", "n2", "wo", "b2"])}
        SUMS = {"b0y": 24, "b0x": 31, "b1y": 55, "b1x": 62, "b2y": 86, "b2x": 93, "b3y": 117}
        POOL_Y = 5
        BOUNDS = {n: i for i, n in enumerate(["b0", "b1", "b2", "b3"])}

        @block.sync
        def _(sp):
            consts = sem("consts")
            for j, (w, r) in enumerate([(g_mix_pre, 0), (g_mix_post, 16), (g_ffn_pre, 32), (g_ffn_post, 48)]):
                sp.dma_start(gain_rows[r:r + 16, :], w.rearrange("l (k p) -> (l k) p", p=P)).then_inc(consts, 16)
            sp.dma_start(gain_rows[64:72, :], g_kv.rearrange("(k p) -> k p", p=P)).then_inc(consts, 16)
            sp.dma_start(gain_rows[72:80, :], g_h.rearrange("l (k p) -> (l k) p", p=P)).then_inc(consts, 16)
            sp.dma_start(gain_rows[80:88, :], g_sub.rearrange("l (k p) -> (l k) p", p=P)).then_inc(consts, 16)
            x_t = x_prompt[0].rearrange("(t p) n -> t p n", p=P)
            for j in range(2):
                sp.dma_start(STG[:, j, 0:D], x_t[j]).then_inc(sem(f"x_in{j}"), 16)
            for s in range(2):
                sp.dma_start(WR[:, s, :].rearrange("p (k n) -> p k n", k=KB),
                             weight_cols(w_in2, s)).then_inc(sem(f"w_in{s}"), 16)
            for j, v in enumerate([b_i, b_f, state_m[0]]):
                sp.dma_start(bg[:, j:j + 1], v.rearrange("l h -> h l")).then_inc(consts, 16)
            for j, v in enumerate([lq1, lk1, lq2, lk2]):
                sp.dma_start(lam_in[:, j, :], v.to_broadcast([P, DK])).then_inc(consts, 16)
            sp.dma_start(WG[:, :, :], w_in2[:, 3072:3088].rearrange("(k p) n -> p k n", p=P)).then_inc(sem("wg_in"), 16)
            with sp.Fori(0, 3) as i:
                for j in range(2):
                    sp.wait_ge(sem("x_turned"), 2 * i + j + 1)
                    sp.wait_ge(sem("x_sumsq"), 2 * i + j + 1)
                    sp.dma_start(STG[:, j, 0:D], x_t[2 * i + j + 2]).then_inc(sem(f"x_in{j}"), 16)
            sp.wait_ge(sem("x_turned"), 7)
            sp.wait_ge(sem("x_sumsq"), 7)
            sp.dma_start(STG[0:DEC, 0, 0:D], x_sample[0]).then_inc(sem("x_in0"), 16)

            def load(w, s, src, k=KB):
                sp.wait_ge(sem("w_lo"), w - 1)
                sp.dma_start(WR[:, s, :].rearrange("p (k n) -> p k n", k=k), src).then_inc(sem(f"w_in{s}"), 16)

            def load_cols(w, u0, n, i0=0):
                with sp.Fori(i0, n // 2) as i:
                    for s in range(2):
                        load(2 * i + (u0 + s), s, weight_cols(w, 2 * i + s))

            def load_mlp(l, u0):
                up = w_up[l]
                down = w_down[l]
                with sp.Fori(0, FFG) as j:
                    for m in range(4):
                        load(8 * j + (u0 + m), m % 2, weight_cols(up, 4 * j + m))
                    for d in range(4):
                        src = down[bass.ds(j * 512, 512), 256 * d:256 * d + 256].rearrange("(k p) n -> p k n", p=P)
                        load(8 * j + (u0 + 4 + d), d % 2, src, 4)

            load_cols(w_in2, U_PROJ, N_PROJ, 1)
            load_cols(w_out2, U_OUT, KB)
            load_mlp(0, U_MLP0)
            load_cols(w_kv, U_KV, N_KV)
            load_cols(w_q[0], U_Q, KB)
            load_cols(w_o[0], U_WO, KB)
            load_mlp(1, U_MLP1)

            y_t = y_prompt[0].rearrange("(t p) n -> t p n", p=P)
            for t in range(NCH):
                sp.wait_ge(sem("y_out_a"), t + 1)
                sp.wait_ge(sem("y_out_d"), t + 1)
                src = Y[:, :, :].rearrange("p k t -> p (k t)")[:, t * D:(t + 1) * D] if t < NT else STG[0:DEC, 0, 0:D]
                sp.dma_start(y_t[t] if t < NT else y_sample[0], src).then_inc(sem("y_st"), 16)
            sp.wait_ge(sem("y_st"), 16 * NCH)

        @block.tensor
        def _(pe):
            mm_done, bank_free, w_lo = sem("mm_done"), sem("bank_free"), sem("w_lo")

            def three(out, lh, ll, rh, rl, start, stop):
                pe.matmul(out, lh, rh, start=start, stop=False)
                pe.matmul(out, lh, rl, start=False, stop=False)
                return pe.matmul(out, ll, rh, start=False, stop=stop)

            def unit(s, w_count, g0):
                pe.wait_ge(w_lo, w_count)
                for g in range(NG):
                    bank = PS[:, 3 * s + g, 0:G]
                    pe.wait_ge(bank_free, g0 + (g + 1))
                    for k in range(KB):
                        ws = slice(k * P, k * P + P)
                        mm = three(bank, WH[:, s, ws], WL[:, s, ws], XH[:, k, grp(g)], XL[:, k, grp(g)],
                                   k == 0, k == KB - 1)
                    mm.then_inc(mm_done, 1)

            def dense(n, u0, g0):
                with pe.Fori(0, n // 2) as i:
                    for s in range(2):
                        unit(s, 2 * i + (u0 + s + 1), 6 * i + (g0 + 3 * s))

            def first_pair(u0, g0, split, n=2):
                pe.wait_ge(w_lo, u0 + n)
                pe.wait_ge(bank_free, g0 + RING)
                for k in range(KB):
                    pe.wait_ge(sem("x_lo"), KB * SPLITS[split] + k + 1)
                    ws = slice(k * P, k * P + P)
                    for s in range(n):
                        for g in range(NG):
                            mm = three(PS[:, 3 * s + g, 0:G], WH[:, s, ws], WL[:, s, ws], XH[:, k, grp(g)],
                                       XL[:, k, grp(g)], k == 0, k == KB - 1)
                            if k == KB - 1:
                                mm.then_inc(mm_done, 1)

            def token_sums(name):
                pe.wait_ge(sem("sq_sum"), SUMS[name])
                for t in range(NCH):
                    L = P if t < NT else DEC
                    mm = pe.matmul(PS[0:L, 7, t:t + 1], SQ[:, t * P:t * P + L], ones[:, 0:1], start=True, stop=True)
                mm.then_inc(sem("tok_sum"), 1)

            def spread_rms(name):
                n = NORMS[name]
                pe.wait_ge(sem("tok_diag"), n + 1)
                for b in range(2):
                    pe.matmul(PS[:, 6 + b, :], ones[:, :], STG[:, 1, 512 * b:512 * b + 512], start=True, stop=True)\
                        .then_inc(sem("tok_spread"), 1)
                pe.wait_ge(sem("rb"), 3 * n + 1)
                pe.matmul(PS[:, 6, 0:DEC], ones[0:DEC, :], STG[0:DEC, 1, SEQ:T], start=True, stop=True)\
                    .then_inc(sem("tok_spread"), 1)

            barrier(pe, PH["load"])
            pe.wait_ge(sem("consts"), 16 * 14)
            pe.wait_ge(sem("ident"), 2)
            pe.transpose(PS[:, 7, 0:88], gain_rows[:, :], ident[0:88, 0:88]).then_inc(sem("gains_turned"), 1)
            with pe.Fori(0, NT // 2) as i:
                for j in range(2):
                    pe.wait_ge(sem(f"x_in{j}"), 16 * i + 16)
                    pe.wait_ge(sem("x_cp_a"), 4 * i + 2 * j)
                    for b in range(KB):
                        mm = pe.transpose(PS[:, 2 * j + b // 4, (b % 4) * P:(b % 4) * P + P],
                                          STG[:, j, b * P:b * P + P], ident[:, :])
                    mm.then_inc(sem("x_turned"), 1)
            pe.wait_ge(sem("x_in0"), 16 * (NT // 2 + 1))
            pe.wait_ge(sem("x_cp_a"), 2 * NT)
            for b in range(KB):
                mm = pe.transpose(PS[:, b // 4, (b % 4) * DEC:(b % 4 + 1) * DEC], STG[0:DEC, 0, b * P:b * P + P], ident[0:DEC, 0:DEC])
            mm.then_inc(sem("x_turned"), 1)

            spread_rms("n0")

            barrier(pe, PH["proj"])
            pe.wait_ge(sem("wg_lo"), 1)
            for g in range(NG):
                pe.wait_ge(bank_free, 1)
                for k in range(KB):
                    mm = three(PS[0:40, 5 + g, 0:G], WGH[:, k, :], WGL[:, k, :], XH[:, k, grp(g)], XL[:, k, grp(g)],
                               k == 0, k == KB - 1)
                mm.then_inc(sem("gates_mm"), 1)
            pe.wait_ge(sem("gates_read"), 6)
            dense(N_PROJ, U_PROJ, G_PROJ)

            barrier(pe, PH["gates"])
            barrier(pe, PH["mlstm"])
            pe.wait_ge(sem("sel"), 6)

            def chunk(L, c1):
                f = slice(0, L)
                c9 = lambda name: pe.wait_ge(sem(name), c1)
                pe.wait_ge(sem("ch_in"), c1 * 32)
                for b in range(4):
                    pe.transpose(PS[f, 0, b * P:b * P + P], CH[:, 4 + b, f], ident[:, :])
                for b in range(H):
                    mm = pe.transpose(PS[f, 1 + b // 4, (b % 4) * P:(b % 4) * P + P], CH[:, 8 + b, f], ident[:, :])
                pe.transpose(PS[f, 7, 0:H], RC[:, 2, f], ident[0:H, 0:H])
                pe.transpose(PS[f, 7, H:2 * H], RC[:, 3, f], ident[0:H, 0:H])\
                    .then_inc(sem("c_turned"), 1)
                for h in range(H):
                    pe.matmul(PS[f, 3 + h // 4, (h % 4) * L:(h % 4 + 1) * L], SEL[:, h, f], RC[:, 0, f],
                              start=True, stop=True)
                for p in range(NPAIR):
                    mm = pe.matmul(PS[:, 5, p * L:(p + 1) * L], SELP[:, p, :], RC[:, 1, f], start=True, stop=True)
                mm.then_inc(sem("c_spread"), 1)
                c9("c_cols")
                for h in range(H):
                    r = slice(64 * (h % 2), 64 * (h % 2) + 64)
                    mm = pe.matmul(PS[f, 6 + h % 2, (h // 2) * L:(h // 2 + 1) * L], CH[r, 4 + h // 2, f],
                                   CH[r, h // 2, f], start=True, stop=True)
                mm.then_inc(sem("c_scores"), 1)
                c9("c_kn")
                c9("c_vc")
                c9("c_vc2")
                pe.wait_ge(sem("c_sd"), 2 * c1)
                c9("c_qi")
                for p in range(NPAIR):
                    pe.matmul(PS[f, p, 0:2 * (DV + 1)], QI[:, p, f], CB[:, p, :, :].rearrange("p a b -> p (a b)"),
                              start=True, stop=False, skip_group_check=True)
                    for a in range(2):
                        h = 2 * p + a
                        mm = pe.matmul(PS[f, p, a * (DV + 1):(a + 1) * (DV + 1)], SD[f, h, f], VC[f, h, :],
                                       start=False, stop=True, skip_group_check=True)
                mm.then_inc(sem("c_num"), 1)
                c9("c_kw")
                for p in range(NPAIR):
                    mm = pe.matmul(PS[:, 4 + p, 0:2 * (DV + 1)], KN[f, p * P:p * P + P],
                                   VC[f, 2 * p:2 * p + 2, :].rearrange("p a b -> p (a b)"), start=True, stop=True)
                mm.then_inc(sem("c_kv"), 1)
                c9("c_hs")
                for h in range(H):
                    mm = pe.transpose(PS[:, h // 4, (h % 4) * L:(h % 4 + 1) * L], HN[f, h, 0:DV], ident[f, f])
                mm.then_inc(sem("c_hT"), 1)

            with pe.Fori(0, NT) as c:
                pe.wait_ge(sem("c_prev"), c + 1)
                chunk(LC, c + 1)
            pe.wait_ge(sem("c_prev"), NT + 1)
            pe.wait_ge(sem("c_state"), 1)
            chunk(DEC, NCH)

            barrier(pe, PH["out"])
            dense(KB, U_OUT, G_OUT)

            def boundary(name, u0, g0):
                token_sums(name + "y")
                spread_rms(name + "y")
                if u0 is not None:
                    first_pair(u0, g0, name)
                    token_sums(name + "x")
                    spread_rms(name + "x")

            def mlp(l, u0, g0):
                def group(j, first=False):
                    for m in range(2 if first else 0, 4):
                        unit(m % 2, 8 * j + (u0 + m + 1), 36 * j + (g0 + 3 * m))
                    for d in range(4):
                        s = d % 2
                        pe.wait_ge(w_lo, 8 * j + (u0 + 5 + d))
                        for b in range(2):
                            for g in range(NG):
                                pe.wait_ge(bank_free, 36 * j + (g0 + 12 + 6 * d + 3 * b + g + 1))
                                for k in range(4):
                                    if d == 0 and b == 0:
                                        pe.wait_ge(sem("h_lo"), 12 * j + (96 * l + 3 * k + g + 1))
                                    ws = slice(k * 256 + b * P, k * 256 + b * P + P)
                                    mm = three(PS[:, 3 * b + g, 0:G], WH[:, s, ws], WL[:, s, ws],
                                               HH[:, k, grp(g)], HL[:, k, grp(g)], k == 0, k == 3)
                                mm.then_inc(mm_done, 1)

                group(0, True)
                with pe.Fori(1, FFG) as j:
                    group(j)

            boundary("b0", U_MLP0, G_MLP0)
            mlp(0, U_MLP0, G_MLP0)
            boundary("b1", U_KV, G_KV)

            def rows_of(s, v3):
                pe.wait_ge(bank_free, RING + G_KV + 3 + v3)
                pe.wait_ge(sem("kv_rows"), v3)
                for t in range(NT):
                    mm = pe.transpose(PS[:, 6 + t // 4, (t % 4) * P:(t % 4) * P + P], STG[:, s, t * P:t * P + P],
                                      ident[:, :])
                    if t % 4 == 3:
                        mm.then_inc(sem("kv_turned"), 1)
                pe.wait_ge(sem("kv_rows"), v3 + 1)
                pe.transpose(PS[0:DEC, 6, 0:P], STG[:, s, SEQ:T], ident[:, :]).then_inc(sem("kv_turned"), 1)

            rows_of(0, 0)
            with pe.Fori(1, N_KV // 2) as i:
                for s in range(2):
                    unit(s, 2 * i + (U_KV + s + 1), 6 * i + (G_KV + 3 * s))
                    rows_of(1 - s, 6 * i + 3 * (s - 1))
            rows_of(1, 3 * (N_KV - 1))

            first_pair(U_Q, G_Q, "n2", 1)

            def att_scores(t, first):
                for m in range(2):
                    r = slice(64 * m, 64 * m + 64)
                    back = 1 if t.i in (0, 4, 5, 6, 7, 8) else 2
                    if not (first and t.i < back and t.hp == 0):
                        pe.wait_ge(sem("a_exp"), 2 * t.n + (m + 1 - 2 * back))
                    if t.i == 0 and m == 0:
                        pe.wait_ge(sem("q_lo"), 3 * t.h + 3)
                        pe.wait_ge(sem("k_lo"), t.h + 1)
                    if t.sample:
                        if m == 0:
                            pe.wait_ge(sem("kc_lo"), t.h + 1)
                        pe.sem_inc(sem("sample_step"), 1)
                    for c in range(0, t.keys, 512):
                        w = min(512, t.keys - c)
                        out = PS[t.f, t.bank(m, c), 0:w]
                        kh, kl = KH[r, t.k0 + c:t.k0 + c + w], KL[r, t.k0 + c:t.k0 + c + w]
                        qs = slice(t.q0, t.q0 + t.L)
                        pe.matmul(out, QH[r, t.hp, qs], kh, start=True, stop=False)
                        if not t.sample and c + w == t.keys:
                            pe.matmul(PS[t.f, t.bank(m, c), w - P:w], MA[r, :], MB[r, :], start=False, stop=False,
                                      skip_group_check=True)
                        pe.matmul(out, QH[r, t.hp, qs], kl, start=False, stop=False)
                        mm = pe.matmul(out, QL[r, t.hp, qs], kh, start=False, stop=True)
                    mm.then_inc(sem("a_scores"), 1)

            def att_turn(t):
                pe.wait_ge(sem("a_tlo"), t.n)
                pe.wait_ge(sem("a_comb"), t.n + 1)
                if t.sample:
                    pe.sem_inc(sem("sample_step"), 1)
                for b, K in t.blocks:
                    mm = pe.transpose(PS[0:K, 4 + b // 4, (b % 4) * t.L:(b % 4 + 1) * t.L],
                                      P0[t.f, t.par, b * P:b * P + K], ident[t.f, t.f])
                mm.then_inc(sem("a_turned"), 1)

            def att_values(t, first):
                pe.wait_ge(sem("a_tlo"), t.n + 1)
                if not first:
                    pe.wait_ge(sem("a_otc"), t.n - 1)
                elif t.n >= 1:
                    pe.wait_ge(sem("a_oc"), t.n)
                if t.i == 0:
                    pe.wait_ge(sem("v_lo"), t.h + 1)
                if t.sample:
                    pe.wait_ge(sem("vc_lo"), t.h + 1)
                    pe.sem_inc(sem("sample_step"), 1)
                for b, K in t.blocks:
                    k = slice(0, K)
                    mm = three(PS[t.f, 6, 0:P], TH[k, t.par, b, t.f], TL[k, t.par, b, t.f], VH[k, t.v0 + b, :],
                               VL[k, t.v0 + b, :], b == 0, b == len(t.blocks) - 1)
                mm.then_inc(sem("a_out"), 1)

            def att_out(t, end):
                pe.wait_ge(sem("a_oc"), t.n + (1 if end else 2))
                pe.wait_ge(sem("a_on"), t.n + 1)
                if t.sample:
                    pe.sem_inc(sem("sample_step"), 1)
                pe.transpose(PS[:, 6, P:P + t.L], ON[t.f, t.par, :], ident[t.f, t.f]).then_inc(sem("a_oT"), 1)

            def att_fill(q, t):
                s = (t.hp + 1) % 2
                i0 = 12 * (t.i - 1)
                g = i0 // 24
                unit0 = G_Q + 3 * (t.hp + 1)
                if i0 == 0:
                    pe.wait_ge(w_lo, 2 * q + (U_Q + t.hp + 2))
                if i0 % 24 == 0:
                    pe.wait_ge(bank_free, 6 * q + (RING + unit0 + g))
                for k in range((i0 % 24) // 3, (i0 % 24) // 3 + 4):
                    ws = slice(k * P, k * P + P)
                    mm = three(PS[:, 7, 0:G], WH[:, s, ws], WL[:, s, ws], XH[:, k, grp(g)], XL[:, k, grp(g)],
                               k == 0, k == KB - 1)
                if i0 % 24 == 12:
                    mm.then_inc(mm_done, 1)

            def att_cache(q, t):
                pe.wait_ge(sem("ck_in"), 32 * q + (16 * t.hp + 16))
                pe.wait_ge(bank_free, 6 * q + (RING + G_Q + 3 * (t.hp + 1)))
                for b in range(4):
                    mm = pe.transpose(PS[:, 7, b * P:b * P + P], CK[:, b, :], ident[:, :])
                mm.then_inc(sem("a_ckT"), 1)

            def att_turn_of_loop(q, first=False, last=False):
                for m in range(TPT + (4 if last else 0)):
                    t = Tile(q, m)
                    fill = m < TPT and t.i in FILL and not (last and t.hp == 1)
                    if m < TPT:
                        att_scores(t, first)
                    if m - 1 < TPT and not (first and m < 1):
                        att_turn(Tile(q, m - 1))
                    if not (first and m < 4):
                        att_out(Tile(q, m - 4), m - 4 == TPT - 1)
                    if m < TPT and t.i == 0:
                        att_cache(q, t)
                    if fill:
                        if t.i == 1:
                            pe.wait_ge(sem("kc_lo"), t.h + 1)
                        att_fill(q, t)
                    if m - 2 < TPT and not (first and m < 2):
                        att_values(Tile(q, m - 2), first and m < 4)

            pe.wait_ge(sem("mask_r"), 1)
            att_turn_of_loop(0, first=True)
            with pe.Fori(1, NPAIR - 1) as q:
                att_turn_of_loop(q)
            att_turn_of_loop(NPAIR - 1, last=True)

            first_pair(U_WO, G_WO, "wo")
            with pe.Fori(1, KB // 2) as i:
                for s in range(2):
                    unit(s, 2 * i + (U_WO + s + 1), 6 * i + (G_WO + 3 * s))
            boundary("b2", U_MLP1, G_MLP1)
            mlp(1, U_MLP1, G_MLP1)
            boundary("b3", None, None)

            pe.wait_ge(sem("x_new"), KB * 4)
            for t in range(NCH):
                L = P if t < NT else DEC
                if t >= 4:
                    pe.wait_ge(sem("y_out_a"), t - 3)
                    pe.wait_ge(sem("y_out_d"), t - 3)
                for b in range(KB):
                    mm = pe.transpose(PS[0:L, 2 * (t % 4) + b // 4, (b % 4) * P:(b % 4) * P + P],
                                      X[:, b, t * P:t * P + L], ident[:, :])
                mm.then_inc(sem("y_turned"), 1)

        @block.scalar
        def _(act):
            mm_done, bank_free, w_hi = sem("mm_done"), sem("bank_free"), sem("w_hi")

            def split_hi(s, u, u2, g):
                act.wait_ge(sem(f"w_in{s}"), 16 * u2 + 16)
                if g is not None:
                    act.wait_ge(mm_done, g)
                act.activation(WH[:, s, :], WR[:, s, :], ACT.Copy).then_inc(w_hi, 1)

            def square(src, s, g):
                act.activation(STG[:, s, grp(g)], src, ACT.Square).then_inc(sem("squared"), 1)

            def take_rms(name):
                n = NORMS[name]
                for b, c in enumerate((slice(0, 512), slice(512, SEQ), slice(SEQ, T))):
                    act.wait_ge(sem("tok_spread"), 3 * n + b + 1)
                    act.activation(RB[:, c], PS[:, 6 + b % 2, 0:c.stop - c.start], ACT.Copy).then_inc(sem("rb"), 1)

            barrier(act, PH["load"])
            act.wait_ge(sem("gains_turned"), 1)
            act.activation(GN[:, :], PS[:, 7, 0:88], ACT.Copy).then_inc(sem("gains"), 1)
            act.sem_inc(sem("x_cp_a"), 2)
            split_hi(0, 0, 0, None)
            act.wait_ge(sem("wg_in"), 16)
            act.wait_ge(sem("wg_zero"), 2)
            act.activation(WGH[:, :, 0:8], WG[:, :, 0:8], ACT.Copy).then_inc(sem("wg_hi"), 1)
            act.activation(WGH[:, :, 32:40], WG[:, :, 8:16], ACT.Copy).then_inc(sem("wg_hi"), 1)

            def x_tile(t1, j, i, c, L=P):
                act.wait_ge(sem(f"x_in{j}"), i)
                act.activation(SQ[0:L, 0:D], STG[0:L, j, 0:D], ACT.Square, accum_out=TV[0:L, 0, bass.ds(t1 - 1, 1)])\
                    .then_inc(sem("x_sumsq"), 1)
                act.wait_ge(sem("x_turned"), t1)
                for b in range(2):
                    act.activation(X[:, 4 * b:4 * b + 4, c], PS[:, 2 * j + b, 0:4 * L].rearrange("p (b t) -> p b t", b=4),
                                   ACT.Copy).then_inc(sem("x_cp_a"), 1)
                act.wait_ge(sem("x_scaled"), t1)
                act.activation(XH[:, :, c], XG[:, j, :, 0:L], ACT.Copy).then_inc(sem("x_hi0"), 1)

            with act.Fori(0, NT // 2) as i:
                for j in range(2):
                    x_tile(2 * i + (j + 1), j, 16 * i + 16, bass.ds(256 * i + P * j, P))
            x_tile(NCH, 0, 16 * (NT // 2 + 1), slice(SEQ, T), DEC)
            take_rms("n0")

            def store(s, dst, src, name="stg"):
                act.dma_start(dst, src).then_inc(sem(f"{name}{s}"), 16)

            barrier(act, PH["proj"])
            with act.Fori(0, 8) as i:
                for s in range(2):
                    split_hi(1 - s, None, i + s, 6 * i + (G_PROJ + 3 * s))
                    act.wait_ge(bank_free, RING + 6 * i + (G_PROJ + 3 * s + 3))
                    store(s, proj_s[2 * i + s], STG[:, s, :])
            with act.Fori(8, 12) as i:
                for s in range(2):
                    split_hi(1 - s, None, i + s, 6 * i + (G_PROJ + 3 * s))
                    act.wait_ge(bank_free, RING + 6 * i + (G_PROJ + 3 * s + 3))
                    act.activation(STG[:, s, :], STG[:, s, :], ACT.Sigmoid).then_inc(sem("o_sig"), 1)
                    act.wait_ge(sem("o_gain"), 2 * i + (s + 1 - 16))
                    store(s, proj_s[2 * i + s], STG[:, s, :])

            barrier(act, PH["gates"])
            li, lf, m_, fc, u_ = (rows[0:H, r, :] for r in (R_LI, R_LF, R_M, R_FC, R_U))
            tmp = rows[0:H, R_EM, :]
            act.wait_ge(sem("g_abs"), 1)
            act.activation(tmp, tmp, ACT.Exp, scale=-1.0).then_inc(sem("g_exp"), 1)
            act.wait_ge(sem("g_one"), 1)
            act.activation(tmp, tmp, ACT.Ln).then_inc(sem("g_exp"), 1)
            act.wait_ge(sem("g_m"), 1)
            act.activation(tmp, m_, ACT.Exp, scale=-1.0).then_inc(sem("g_fin"), 1)
            act.wait_ge(sem("g_inter"), 1)
            act.activation(rows[0:H, R_INTER, :], rows[0:H, R_INTER, :], ACT.Exp).then_inc(sem("g_fin"), 1)

            barrier(act, PH["mlstm"])
            act.wait_ge(sem("stg0"), 16 * 12)
            act.wait_ge(sem("stg1"), 16 * 12)
            act.dma_start(m_prompt[0].rearrange("b h -> h b"), rows[0:H, R_M, SEQ - 1:SEQ]).then_inc(sem("m_st"), 16)
            act.dma_start(m_sample[0].rearrange("b h -> h b"), rows[0:H, R_M, T - 1:T]).then_inc(sem("m_st"), 16)

            def chunk_in(t0, L):
                act.dma_start(CH[:, :, 0:L], proj_s[:, :, bass.ds(t0, L)].rearrange("b p t -> p b t"))\
                    .then_inc(sem("ch_in"), 16)
                act.dma_start(RC[:, :, 0:L], rows[0:H, 0:4, bass.ds(t0, L)]).then_inc(sem("ch_in"), 16)

            def chunk(L, c1, xcol, nxt):
                f = slice(0, L)
                act.wait_ge(sem("c_turned"), c1)
                act.activation(KN[f, :], PS[f, 0, :], ACT.Copy, scale=K_SCALE).then_inc(sem("c_kn"), 1)
                act.activation(VC[f, 0:4, 0:DV], PS[f, 1, :].rearrange("p (h e) -> p h e", h=4), ACT.Copy)\
                    .then_inc(sem("c_vc"), 1)
                for h in range(H):
                    act.wait_ge(sem("c_cols"), c1)
                    act.wait_ge(sem("c_masked"), 2 * c1 - (1 - h // 4))
                    act.activation(DT[f, h, f], DT[f, h, f], ACT.Exp, bias=MS[f, 0, h:h + 1])\
                        .then_inc(sem("c_dt"), 1)
                act.wait_ge(sem("c_num"), c1)
                for p in range(NPAIR):
                    act.activation(HN[f, 2 * p:2 * p + 2, :], PS[f, p, 0:2 * (DV + 1)]
                                   .rearrange("p (a b) -> p a b", a=2), ACT.Copy).then_inc(sem("c_hn"), 1)
                act.wait_ge(sem("c_hn"), 4 * c1)
                act.wait_ge(sem("c_kw"), c1)
                act.activation(DT[f, :, :], HN[f, :, 0:DV], ACT.Square).then_inc(sem("c_sn"), 1)
                act.wait_ge(sem("c_hf"), 2 * c1)
                act.activation(XH[:, :, xcol], SD[:, :, f], ACT.Copy).then_inc(sem("c_xh"), 1)
                if nxt is not None:
                    nxt()

            chunk_in(0, LC)
            with act.Fori(0, NT - 1) as c:
                chunk(LC, c + 1, bass.ds(c * P, P), lambda: chunk_in(c * P + P, LC))
            chunk(LC, NT, slice(SEQ - P, SEQ), lambda: chunk_in(SEQ, DEC))
            act.wait_ge(sem("c_upd"), 3 * NT)

            def state_out(c_o, n_o):
                for a in range(2):
                    r = slice(64 * a, 64 * a + 64)
                    act.dma_start(c_o.rearrange("(q a) d e -> a d q e", a=2)[a], CB[r, :, a, 0:DV]).then_inc(sem("st_out"), 16)
                    with nc.allow_non_contiguous_dma(reason="one normaliser column"):
                        act.dma_start(n_o.rearrange("(q a) (d o) -> a d q o", a=2, o=1)[a], CB[r, :, a, DV:DV + 1])\
                            .then_inc(sem("st_out"), 16)
            state_out(c_prompt[0, 0], n_prompt[0, 0])
            act.wait_ge(sem("st_out"), 64)
            sc_, sn_ = state_c[0, 0], state_n[0, 0]
            for a in range(2):
                r = slice(64 * a, 64 * a + 64)
                act.dma_start(CB[r, :, a, 0:DV], sc_.rearrange("(q a) d e -> a d q e", a=2)[a]).then_inc(sem("c_state0"), 16)
                with nc.allow_non_contiguous_dma(reason="one normaliser column"):
                    act.dma_start(CB[r, :, a, DV:DV + 1], sn_.rearrange("(q a) (d o) -> a d q o", a=2, o=1)[a])\
                        .then_inc(sem("c_state0"), 16)
            act.wait_ge(sem("c_state0"), 64)
            act.sem_inc(sem("c_state"), 1)
            chunk(DEC, NCH, slice(SEQ, T), None)
            act.wait_ge(sem("c_upd"), 3 * NCH)
            state_out(c_sample[0, 0], n_sample[0, 0])
            act.wait_ge(sem("st_out"), 128)
            act.wait_ge(sem("m_st"), 32)

            def dense_hi(n, g0, u0, first=0):
                def one(i, s, ahead=True):
                    if ahead:
                        split_hi(1 - s, None, i + (u0 // 2 + s), 6 * i + (g0 + 3 * s))
                    for g in range(NG):
                        act.wait_ge(bank_free, RING + 6 * i + (g0 + 3 * s + g + 1))
                        square(Y[:, 2 * i + s, grp(g)], s, g)
                if first:
                    one(0, 0, False)
                    one(0, 1)
                with act.Fori(first, n // 2) as i:
                    for s in range(2):
                        one(i, s)

            barrier(act, PH["out"])
            dense_hi(KB, G_OUT, U_OUT)

            def boundary(name, pre, u0, g0):
                if pre:
                    split_hi(1, None, u0 // 2, g0)
                take_rms(name + "y")
                if pre:
                    for k in range(KB):
                        act.wait_ge(sem("x_new"), KB * BOUNDS[name] + k + 1)
                        act.activation(XH[:, k, :], X[:, k, :], ACT.Copy, scale=gcol(pre, k)).then_inc(sem("x_hi"), 1)
                        if k >= 2:
                            act.wait_ge(sem("sq_sum"), SUMS[name + "y"] + k - 1)
                        act.activation(SQ[:, :] if k == 0 else STG[:, k % 2, :], X[:, k, :], ACT.Square)\
                            .then_inc(sem("squared_x"), 1)
                    take_rms(name + "x")

            def mlp(l, u0, g0):
                def group(j, first=False, last=False):
                    for m in range(4):
                        if not (first and m == 0):
                            split_hi((m + 1) % 2, None, 4 * j + (u0 // 2 + (m + 1) // 2), 36 * j + (g0 + 3 * m))
                        for g in range(NG):
                            n = 3 * m + g
                            act.wait_ge(bank_free, RING + 36 * j + (g0 + n + 1))
                            act.activation(HH[:, m, grp(g)], MT[:, n % 2, :], ACT.Square).then_inc(sem("h_hi"), 1)
                    for d in range(4):
                        if not (last and l == 1 and d == 3):
                            split_hi((d + 1) % 2, None, 4 * j + (u0 // 2 + (d + 5) // 2), 36 * j + (g0 + 12 + 6 * d))
                        for b in range(2 if last else 0):
                            for g in range(NG):
                                act.wait_ge(bank_free, RING + 36 * j + (g0 + 12 + 6 * d + 3 * b + g + 1))
                                square(Y[:, 2 * d + b, grp(g)], b, g)
                group(0, first=True)
                with act.Fori(1, FFG - 1) as j:
                    group(j)
                group(FFG - 1, last=True)

            boundary("b0", "ffn_pre0", U_MLP0, G_MLP0)
            mlp(0, U_MLP0, G_MLP0)
            boundary("b1", "kv", U_KV, G_KV)

            kp = k_prompt[0].rearrange("(t p) h a d -> h p t (a d)", p=P)
            ks = k_sample[0].rearrange("t h a d -> h t (a d)")
            vp = v_prompt[0].rearrange("(t p) h d -> h p t d", p=P)
            vs = v_sample[0].rearrange("t h d -> h t d")

            def kv_unit(i, s, h, dp, ds_, keys):
                act.wait_ge(bank_free, RING + 6 * i + (G_KV + 3 * s + 3))
                if keys:
                    store(s, kT_s[h], STG[:, s, :], "kt_st")
                split_hi(s, None, i + (U_KV // 2 + 1), 6 * i + (G_KV + 3 * s + 3))
                act.wait_ge(sem(f"kv_st{s}"), 32 * i)
                for b in range(2):
                    act.wait_ge(sem("kv_turned"), 6 * i + (3 * s + b + 1))
                    act.activation(OT[:, s, 4 * b:4 * b + 4, :], PS[:, 6 + b, :].rearrange("p (t c) -> p t c", t=4),
                                   ACT.Copy).then_inc(sem("kv_rows"), 1)
                act.wait_ge(sem("kv_turned"), 6 * i + (3 * s + 3))
                act.activation(OT[0:DEC, s, NT, :], PS[0:DEC, 6, 0:P], ACT.Copy).then_inc(sem("kv_rows"), 1)
                act.wait_ge(sem("kv_rows"), 6 * i + (3 * s + 3))
                store(s, dp[h], OT[:, s, 0:NT, :], "kv_st")
                store(s, ds_[h], OT[0:DEC, s, NT, :], "kv_st")

            kv_unit(0, 0, 0, kp, ks, True)
            kv_unit(0, 1, 1, kp, ks, True)
            with act.Fori(1, 4) as i:
                for s in range(2):
                    kv_unit(i, s, 2 * i + s, kp, ks, True)
            with act.Fori(4, 8) as i:
                for s in range(2):
                    kv_unit(i, s, 2 * i + (s - 8), vp, vs, False)

            for k in range(KB):
                act.activation(XH[:, k, :], X[:, k, :], ACT.Copy, scale=gcol("mix_pre1", k)).then_inc(sem("x_hi"), 1)

            for s in range(2):
                act.wait_ge(sem(f"kt_st{s}"), 16 * 4)
                act.wait_ge(sem(f"kv_st{s}"), 32 * 8)
            for a in range(2):
                act.activation(lam[:, 2 + a:3 + a], lam[:, a:a + 1], ACT.Exp).then_inc(sem("lam_exp"), 1)
            ck = cache_k[0].rearrange("(t p) h a d -> h p t (a d)", p=P)
            cv = cache_v[0].rearrange("(t p) h d -> h p t d", p=P)

            def load_k(h):
                act.dma_start(KR, kT_s[h]).then_inc(sem("k_in"), 16)

            def load_ck(h):
                act.dma_start(CK[:, :, :], ck[h]).then_inc(sem("ck_in"), 16)

            def load_v(h):
                act.dma_start(VR[:, 0:NT, :], vp[h]).then_inc(sem("v_in"), 16)
                act.dma_start(VR[:, NT:NT + 4, :], cv[h]).then_inc(sem("vc_in"), 16)
                act.dma_start(VR[0:DEC, NT + 4, :], vs[h]).then_inc(sem("vs_in"), 16)

            def split_k(h1, a_scores):
                act.wait_ge(sem("k_in"), 16 * h1)
                if a_scores is not None:
                    act.wait_ge(sem("a_scores"), a_scores)
                act.activation(KH[:, 0:SEQ], KR[:, 0:SEQ], ACT.Copy).then_inc(sem("k_hi"), 1)

            def split_q(h, s, g):
                act.wait_ge(bank_free, 3 * h + (RING + G_Q + g + 1))
                act.activation(QH[:, s, grp(g)], QR[:, grp(g)], ACT.Copy).then_inc(sem("q_hi"), 1)

            def att_extras(q, t, first, last):
                h, more = t.h, not (last and t.hp == 1)
                if t.i == 0:
                    act.wait_ge(sem("a_ckT"), h + 1)
                    act.wait_ge(sem("a_scores"), 2 * t.n)
                    act.activation(KH[:, SCOL:NKEY], KR[:, SEQ:T], ACT.Copy)
                    act.activation(KH[:, SEQ:SCOL], PS[:, 7, :], ACT.Copy).then_inc(sem("kc_hi"), 1)
                    if more:
                        split_hi(t.hp, None, q + (U_Q // 2 + 1), 6 * q + (G_Q + 3 * (t.hp + 1)))
                if t.i == 1:
                    act.wait_ge(sem("v_in"), 16 * h + 16)
                    if not (first and t.hp == 0):
                        act.wait_ge(sem("a_out"), t.n - 2)
                    act.activation(VH[:, 0:NT, :], VR[:, 0:NT, :], ACT.Copy).then_inc(sem("v_hi"), 1)
                if t.i == 2 and more:
                    act.wait_ge(sem("kc_lo"), h + 1)
                    load_k(h + 1)
                    load_ck(h + 1)
                if t.i == 3:
                    act.wait_ge(sem("vc_in"), 16 * h + 16)
                    act.wait_ge(sem("vs_in"), 16 * h + 16)
                    if not (first and t.hp == 0):
                        act.wait_ge(sem("a_out"), t.n - 3)
                    act.activation(VH[:, NT:NT + 4, :], VR[:, NT:NT + 4, :], ACT.Copy)
                    act.activation(VH[0:DEC, NT + 4, :], VR[0:DEC, NT + 4, :], ACT.Copy).then_inc(sem("vc_hi"), 1)
                if t.i == 5 and more:
                    act.wait_ge(sem("v_lo"), h + 1)
                    act.wait_ge(sem("vc_lo"), h + 1)
                    load_v(h + 1)
                if t.i == 8 and more:
                    split_k(h + 2, 2 * t.n)
                if t.i in (4, 6, 8) and more:
                    split_q(h + 1, (t.hp + 1) % 2, (t.i - 4) // 2)

            def att_sumsq(t):
                act.wait_ge(sem("a_oc"), t.n + 1)
                act.activation(ON[t.f, t.par, :], OC[t.f, t.par, :], ACT.Square, scale=t.number(6), accum_out=t.number(8))\
                    .then_inc(sem("a_ss"), 1)

            def att_exp(t, m, first):
                act.wait_ge(sem("a_max"), 2 * t.n + (m + 1))
                if m == 0 and not (first and t.n < 2):
                    act.wait_ge(sem("a_turned"), t.n - 1)
                if m == 1:
                    act.wait_ge(sem("a_comb"), t.n)
                dst = P0[t.f, t.par, 0:t.keys] if m == 0 else P1[t.f, 0:t.keys]
                act.activation(dst, t.score(m), ACT.Exp, bias=t.number(m),
                               accum_out=t.number(4 + m)).then_inc(sem("a_exp"), 1)

            def att_take_out(t, first):
                if t.i == 0 and not (first and t.hp == 0):
                    act.wait_ge(sem("o_st"), 32 * t.h)
                act.wait_ge(sem("a_oT"), t.n + 1)
                act.activation(OTS[:, t.q0:t.q0 + t.L], PS[:, 6, P:P + t.L], ACT.Copy)\
                    .then_inc(sem("a_otc"), 1)
                if t.i in (NT - 1, NT):
                    act.wait_ge(sem("a_otc"), t.n + 1)
                    c = slice(0, SEQ) if t.i == NT - 1 else slice(SEQ, T)
                    act.dma_start(o_s[t.h][:, c], OTS[:, c]).then_inc(sem("o_st"), 16)

            def att_turned_hi(t, first):
                act.wait_ge(sem("a_turned"), t.n + 1)
                if not (first and t.n < 2):
                    act.wait_ge(sem("a_out"), t.n - 1)
                for src, dst in t.turned(TH):
                    ins = act.activation(dst, src, ACT.Copy)
                ins.then_inc(sem("a_thi"), 1)

            load_k(0)
            load_ck(0)
            load_v(0)
            split_k(1, None)
            for g in range(NG):
                split_q(0, 0, g)

            def att_turn_of_loop(q, first=False, last=False):
                for m in range(TPT + (4 if last else 0)):
                    t = Tile(q, m)
                    if m < TPT:
                        att_exp(t, 0, first)
                    if m - 1 < TPT and not (first and m < 1):
                        att_turned_hi(Tile(q, m - 1), first)
                    if not (first and m < 4):
                        att_take_out(Tile(q, m - 4), first)
                    if m < TPT:
                        att_exp(t, 1, first)
                    if m - 3 < TPT and not (first and m < 3):
                        att_sumsq(Tile(q, m - 3))
                    if m < TPT:
                        att_extras(q, t, first, last)

            att_turn_of_loop(0, first=True)
            with act.Fori(1, NPAIR - 1) as q:
                att_turn_of_loop(q)
            att_turn_of_loop(NPAIR - 1, last=True)

            act.wait_ge(sem("o_st"), 32 * H)
            for k in range(KB):
                act.dma_start(Y[:, k, :], o_s[k]).then_inc(sem(f"o_in{k}"), 16)
            split_hi(1, None, U_WO // 2, G_WO)
            for k in range(KB):
                act.wait_ge(sem(f"o_in{k}"), 16)
                act.activation(XH[:, k, :], Y[:, k, :], ACT.Copy, scale=gcol("sub", k)).then_inc(sem("x_hi"), 1)
            dense_hi(KB, G_WO, U_WO, 1)
            boundary("b2", "ffn_pre1", U_MLP1, G_MLP1)
            mlp(1, U_MLP1, G_MLP1)
            boundary("b3", None, None, None)

            for t in range(NCH):
                act.wait_ge(sem("y_turned"), t + 1)
                act.activation(y_half(t, 0), PS[0:P if t < NT else DEC, 2 * (t % 4), :], ACT.Copy).then_inc(sem("y_out_a"), 1)

        @block.vector
        def _(dve):
            mm_done, bank_free, w_hi, w_lo = sem("mm_done"), sem("bank_free"), sem("w_hi"), sem("w_lo")

            def split_lo(s, u1):
                dve.wait_ge(w_hi, u1)
                dve.tensor_tensor(WL[:, s, :], WR[:, s, :], WH[:, s, :].bitcast(F32), ALU.subtract).then_inc(w_lo, 1)

            def add_square(s, g, n):
                dve.wait_ge(sem("squared"), n)
                dve.tensor_tensor(SQ[:, grp(g)], SQ[:, grp(g)], STG[:, s, grp(g)], ALU.add).then_inc(sem("sq_sum"), 1)

            def token_rms(name):
                n = NORMS[name]
                if name != "n0":
                    dve.wait_ge(sem("tok_sum"), n)
                    dve.tensor_copy(TV[:, 0, 0:NT], PS[:, 7, 0:NT])
                    dve.tensor_copy(TV[0:DEC, 0, NT:NCH], PS[0:DEC, 7, NT:NCH]).then_inc(sem("tok_var"), 1)
                else:
                    dve.wait_ge(sem("x_sumsq"), NCH)
                    dve.sem_inc(sem("tok_var"), 1)
                dve.wait_ge(sem("tok_var"), 2 * n + 1)
                dve.tensor_scalar(TV[:, 1, :], TV[:, 0, :], 1.0 / D, EPS, ALU.mult, ALU.add).then_inc(sem("tok_var"), 1)
                dve.wait_ge(sem("tok_pow"), n + 1)
                dve.tensor_tensor(STG[:, 1, 0:SEQ].rearrange("p (t c) -> p t c", t=NT),
                                  ident[:, :].unsqueeze(1).to_broadcast([P, NT, P]),
                                  TV[:, 2, 0:NT].unsqueeze(2).to_broadcast([P, NT, P]), ALU.mult)
                dve.tensor_scalar(STG[0:DEC, 1, SEQ:T], ident[0:DEC, 0:DEC], TV[0:DEC, 2, NT:NCH], None, ALU.mult)\
                    .then_inc(sem("tok_diag"), 1)

            def x_lo(k, gain, name):
                dve.wait_ge(sem("x_hi"), KB * SPLITS[name] + k + 1)
                src = Y if name == "wo" else X
                dve.scalar_tensor_tensor(XL[:, k, :], src[:, k, :], gcol(gain, k), XH[:, k, :].bitcast(F32),
                                         ALU.mult, ALU.subtract).then_inc(sem("x_lo"), 1)

            dve.memset(TV[:, :, :], 1.0).then_inc(sem("tv_init"), 1)
            dve.memset(half[:, :], -0.5)
            dve.memset(mean_eps[:, 0:1], 1.0 / P)
            dve.memset(mean_eps[:, 1:2], EPS)
            dve.memset(ones[:, :], 1.0)
            dve.sem_inc(bank_free, RING)
            barrier(dve, PH["load"])
            dve.wait_ge(sem("gains"), 1)
            dve.tensor_scalar(GN[:, 80:88], GN[:, 80:88], 1.0 - LAM_INIT, None, ALU.mult)
            split_lo(0, 1)
            dve.wait_ge(sem("wg_zero"), 2)
            dve.wait_ge(sem("wg_hi"), 2)
            dve.tensor_tensor(WGL[:, :, 0:8], WG[:, :, 0:8], WGH[:, :, 0:8].bitcast(F32), ALU.subtract)
            dve.tensor_tensor(WGL[:, :, 32:40], WG[:, :, 8:16], WGH[:, :, 32:40].bitcast(F32), ALU.subtract)\
                .then_inc(sem("wg_lo"), 1)

            def x_tile(t1, j, c, L=P):
                dve.wait_ge(sem("x_cp_a"), 2 * t1 + 2)
                g0 = GAINS.index("mix_pre0") * KB
                dve.tensor_tensor(XG[:, j, :, 0:L], X[:, :, c], GN[:, g0:g0 + KB].unsqueeze(2).to_broadcast([P, KB, L]),
                                  ALU.mult).then_inc(sem("x_scaled"), 1)
                dve.wait_ge(sem("x_scaled"), t1)
                dve.wait_ge(sem("x_hi0"), t1)
                dve.tensor_tensor(XL[:, :, c], XG[:, j, :, 0:L], XH[:, :, c].bitcast(F32), ALU.subtract)\
                    .then_inc(sem("x_lo0"), 1)
            with dve.Fori(0, NT // 2) as i:
                for j in range(2):
                    x_tile(2 * i + (j + 1), j, bass.ds(256 * i + P * j, P))
            x_tile(NCH, 0, slice(SEQ, T), DEC)
            token_rms("n0")
            link = [0]

            def ln(ins):
                link[0] += 1
                ins.then_inc(sem("lam"), 1)
                dve.wait_ge(sem("lam"), link[0])
            dve.wait_ge(sem("consts"), 16 * 14)
            ln(dve.tensor_tensor(lam_in[:, 0, :], lam_in[:, 0, :], lam_in[:, 1, :], ALU.mult))
            ln(dve.tensor_tensor(lam_in[:, 2, :], lam_in[:, 2, :], lam_in[:, 3, :], ALU.mult))
            ln(dve.reduce_sum(lam[:, 0:1], lam_in[:, 0, :], AX))
            ln(dve.reduce_sum(lam[:, 1:2], lam_in[:, 2, :], AX))

            barrier(dve, PH["proj"])
            dve.wait_ge(sem("rst"), 1)
            for g in range(NG):
                dve.wait_ge(sem("gates_mm"), g + 1)
                dve.tensor_tensor(rows[0:H, R_LI, grp(g)], PS[0:H, 5 + g, 0:G], RB[0:H, grp(g)], ALU.mult)\
                    .then_inc(sem("gates_read"), 1)
                dve.tensor_tensor(rows[0:H, R_LF, grp(g)], PS[32:40, 5 + g, 0:G], RB[0:H, grp(g)], ALU.mult)\
                    .then_inc(sem("gates_read"), 1)

            def take(s, g, n):
                dve.wait_ge(mm_done, n)
                dve.tensor_tensor(STG[:, s, grp(g)], PS[:, 3 * s + g, 0:G], RB[:, grp(g)], ALU.mult)\
                    .then_inc(bank_free, 1)

            with dve.Fori(0, N_PROJ // 2) as i:
                for s in range(2):
                    split_lo(1 - s, 2 * i + (s + 2))
                    dve.wait_ge(sem(f"stg{s}"), 16 * i)
                    for g in range(NG):
                        take(s, g, 6 * i + (3 * s + g + 1))

            barrier(dve, PH["gates"])
            row = lambda r: rows[0:H, r, :]
            li, lf, m_, fc, u_, inter, gg, tmp = (row(r) for r in (R_LI, R_LF, R_M, R_FC, R_U, R_INTER, R_G, R_EM))
            glink = [0]

            def gl(ins, other=None):
                glink[0] += 1
                ins.then_inc(sem("g_dve"), 1)
                dve.wait_ge(sem("g_dve"), glink[0])
            gl(dve.tensor_scalar(li, li, bg[:, 0:1], None, ALU.add))
            gl(dve.tensor_scalar(lf, lf, bg[:, 1:2], None, ALU.add))
            gl(dve.tensor_scalar(gg, lf, -1.0, None, ALU.mult))
            dve.tensor_tensor(tmp, lf, gg, ALU.max).then_inc(sem("g_abs"), 1)
            dve.wait_ge(sem("g_exp"), 1)
            dve.tensor_scalar(tmp, tmp, 1.0, None, ALU.add).then_inc(sem("g_one"), 1)
            gl(dve.tensor_scalar(lf, lf, 0.0, None, ALU.min))
            dve.wait_ge(sem("g_exp"), 2)
            gl(dve.tensor_tensor(lf, lf, tmp, ALU.subtract))
            gl(dve.tensor_tensor_scan(fc, RST[:, :], lf, 0.0, ALU.mult, ALU.add))
            gl(dve.tensor_tensor_scan(rows[0:H, R_M, 0:SEQ], rows[0:H, R_LF, 0:SEQ], rows[0:H, R_LI, 0:SEQ], 0.0,
                                      ALU.add, ALU.max))
            dve.tensor_tensor_scan(rows[0:H, R_M, SEQ:T], rows[0:H, R_LF, SEQ:T], rows[0:H, R_LI, SEQ:T], bg[:, 2:3],
                                   ALU.add, ALU.max).then_inc(sem("g_m"), 1)
            dve.wait_ge(sem("g_m"), 1)
            gl(dve.memset(MP[:, 0:1], 0.0))
            gl(dve.tensor_copy(MP[:, 1:NT], rows[0:H, R_M, LC - 1:SEQ - LC:LC]))
            gl(dve.tensor_copy(MP[:, NT:NCH], bg[:, 2:3]))
            gl(dve.tensor_tensor(gg, li, fc, ALU.subtract))
            gl(dve.tensor_tensor(u_, fc, m_, ALU.subtract))
            dve.tensor_tensor(rows[0:H, R_INTER, 0:SEQ].rearrange("h (c t) -> h c t", c=NT),
                              rows[0:H, R_U, 0:SEQ].rearrange("h (c t) -> h c t", c=NT),
                              MP[:, 0:NT].unsqueeze(2).to_broadcast([H, NT, LC]), ALU.add)
            dve.tensor_scalar(rows[0:H, R_INTER, SEQ:T], rows[0:H, R_U, SEQ:T], MP[:, NT:NCH], None, ALU.add)\
                .then_inc(sem("g_inter"), 1)

            barrier(dve, PH["mlstm"])
            dve.memset(VC[:, :, DV:DV + 1], 1.0).then_inc(sem("c_ones"), 1)
            dve.memset(CB[:, :, :, :], 0.0)
            dve.sem_inc(sem("c_prev"), 1)

            def chunk(L, c1, xcol):
                f = slice(0, L)
                w = lambda name, n: dve.wait_ge(sem(name), n)
                w("c_turned", c1)
                dve.tensor_copy(VC[f, 4:8, 0:DV], PS[f, 2, :].rearrange("p (h e) -> p h e", h=4)).then_inc(sem("c_vc2"), 1)
                dve.tensor_copy(MS[f, 0:2, :], PS[f, 7, 0:2 * H].rearrange("p (r h) -> p r h", r=2))\
                    .then_inc(sem("c_cols"), 1)
                w("c_spread", c1)
                for b in range(2):
                    dve.tensor_tensor(DT[f, 4 * b:4 * b + 4, f], PS[f, 3 + b, 0:4 * L].rearrange("p (h t) -> p h t", h=4),
                                      mask[f, f].unsqueeze(1).to_broadcast([L, 4, L]), ALU.add)\
                        .then_inc(sem("c_masked"), 1)
                dve.tensor_copy(DEC4[:, :], PS[:, 5, L - 1:4 * L:L]).then_inc(sem("c_dec"), 1)
                w("ch_in", 32 * c1)
                dve.tensor_tensor(QI[:, :, f], CH[:, 0:4, f], PS[:, 5, 0:4 * L].rearrange("p (a t) -> p a t", a=4),
                                  ALU.mult).then_inc(sem("c_qi"), 1)
                w("c_scores", c1)
                w("c_dt", 8 * c1)
                for a in range(2):
                    dve.scalar_tensor_tensor(SD[f, a:H:2, f], PS[f, 6 + a, 0:4 * L].rearrange("p (h t) -> p h t", h=4),
                                             K_SCALE, DT[f, a:H:2, f], ALU.mult, ALU.mult).then_inc(sem("c_sd"), 1)
                w("c_kn", c1)
                dve.tensor_tensor(KN[f, :].rearrange("p (h d) -> p h d", h=H), KN[f, :].rearrange("p (h d) -> p h d", h=H),
                                  DT[f, :, L - 1:L].to_broadcast([L, H, DK]), ALU.mult).then_inc(sem("c_kw"), 1)
                w("c_hn", 4 * c1)
                qn = HN[f, :, DV]
                n0 = 8 * (c1 - 1) if isinstance(c1, int) else c1 * 8 - 8

                def cl(k, ins):
                    ins.then_inc(sem("c_den"), 1)
                    dve.wait_ge(sem("c_den"), n0 + k)
                cl(1, dve.scalar_tensor_tensor(MS[f, 2, :], qn, -1.0, qn, ALU.mult, ALU.max))
                cl(2, dve.tensor_tensor(MS[f, 2, :], MS[f, 2, :], MS[f, 1, :], ALU.max))
                cl(3, dve.reciprocal(MS[f, 3, :], MS[f, 2, :]))
                w("c_sn", c1)
                cl(4, dve.reduce_sum(MS[f, 4, :], DT[f, :, :], AX))
                cl(5, dve.tensor_tensor(MS[f, 5, :], MS[f, 3, :], MS[f, 3, :], ALU.mult))
                cl(6, dve.tensor_tensor(MS[f, 5, :], MS[f, 5, :], MS[f, 4, :], ALU.mult))
                cl(7, dve.tensor_scalar(MS[f, 5, :], MS[f, 5, :], 1.0 / DV, EPS, ALU.mult, ALU.add))
                w("c_pow", c1)
                cl(8, dve.tensor_tensor(MS[f, 7, :], MS[f, 6, :], MS[f, 3, :], ALU.mult))
                dve.tensor_tensor(HN[f, :, 0:DV], HN[f, :, 0:DV], MS[f, 7, :].unsqueeze(2).to_broadcast([L, H, DV]),
                                  ALU.mult).then_inc(sem("c_hs"), 1)
                w("c_kv", c1)
                w("c_num", c1)
                cu = 3 * (c1 - 1) if isinstance(c1, int) else c1 * 3 - 3
                dve.tensor_tensor(CB[:, :, :, :].rearrange("p q a b -> p q (a b)"),
                                  CB[:, :, :, :].rearrange("p q a b -> p q (a b)"),
                                  DEC4[:, :].unsqueeze(2).to_broadcast([P, NPAIR, 2 * (DV + 1)]), ALU.mult)\
                    .then_inc(sem("c_upd"), 1)
                w("c_upd", cu + 1)
                for a in range(2):
                    r = slice(64 * a, 64 * a + 64)
                    dve.tensor_tensor(CB[r, :, a, :], CB[r, :, a, :], PS[r, 4:8, a * (DV + 1):(a + 1) * (DV + 1)],
                                      ALU.add).then_inc(sem("c_upd"), 1)
                w("c_hT", c1)
                for b in range(2):
                    dve.tensor_tensor(SD[:, 4 * b:4 * b + 4, f], PS[:, b, 0:4 * L].rearrange("p (h t) -> p h t", h=4),
                                      CH[:, 16 + 4 * b:20 + 4 * b, f], ALU.mult).then_inc(sem("c_hf"), 1)
                w("c_xh", c1)
                dve.tensor_tensor(XL[:, :, xcol], SD[:, :, f], XH[:, :, xcol].bitcast(F32), ALU.subtract)\
                    .then_inc(sem("c_prev"), 1)

            with dve.Fori(0, NT) as c:
                chunk(LC, c + 1, bass.ds(c * P, P))
            dve.wait_ge(sem("c_state"), 1)
            chunk(DEC, NCH, slice(SEQ, T))

            def dense_y(u0, g0, q0, first=0):
                dve.memset(SQ[:, :], 0.0)

                def one(i, s, ahead=True):
                    if ahead:
                        split_lo(1 - s, 2 * i + (u0 + s + 2))
                    for g in range(NG):
                        dve.wait_ge(mm_done, 6 * i + (g0 + 3 * s + g + 1))
                        dve.tensor_copy(Y[:, 2 * i + s, grp(g)], PS[:, 3 * s + g, 0:G]).then_inc(bank_free, 1)
                        if g:
                            add_square(s, g - 1, 6 * i + (q0 + 3 * s + g))
                    add_square(s, 2, 6 * i + (q0 + 3 * s + 3))
                if first:
                    one(0, 0, False)
                    one(0, 1)
                with dve.Fori(first, KB // 2) as i:
                    for s in range(2):
                        one(i, s)

            barrier(dve, PH["out"])
            dense_y(U_OUT, G_OUT, 0)

            def boundary(name, post, pre, u0=None):
                if pre:
                    split_lo(1, u0 + 2)
                token_rms(name + "y")
                dve.wait_ge(sem("rb"), 3 * (NORMS[name + "y"] + 1))
                for k in range(KB):
                    if k < POOL_Y:
                        dve.tensor_tensor(Y[:, k, :], Y[:, k, :], RB[:, :], ALU.mult).then_inc(sem("y_scaled_d"), 1)
                        dve.wait_ge(sem("y_scaled_d"), POOL_Y * BOUNDS[name] + k + 1)
                    else:
                        dve.wait_ge(sem("y_scaled"), (KB - POOL_Y) * BOUNDS[name] + k - POOL_Y + 1)
                    dve.scalar_tensor_tensor(X[:, k, :], Y[:, k, :], gcol(post, k), X[:, k, :], ALU.mult, ALU.add)\
                        .then_inc(sem("x_new"), 1)
                    if pre and k >= 1:
                        x_lo(k - 1, pre, name)
                if pre:
                    x_lo(KB - 1, pre, name)
                    token_rms(name + "x")
                    dve.wait_ge(sem("rb"), 3 * (NORMS[name + "x"] + 1))

            def mlp(l, u0, g0):
                def group(j, first=False, last=False):
                    if last:
                        dve.memset(SQ[:, :], 0.0)
                    def low(n):
                        dve.wait_ge(sem("h_hi"), 12 * j + (96 * l + n + 1))
                        dve.wait_ge(sem("h_sq"), 12 * j + (96 * l + n + 1))
                        dve.tensor_tensor(HL[:, n // 3, grp(n % 3)], M2[:, n % 2, :],
                                          HH[:, n // 3, grp(n % 3)].bitcast(F32), ALU.subtract).then_inc(sem("h_lo"), 1)
                    for m in range(4):
                        if not (first and m == 0):
                            split_lo((m + 1) % 2, 8 * j + (u0 + m + 2))
                        for g in range(NG):
                            n = 3 * m + g
                            dve.wait_ge(mm_done, 36 * j + (g0 + n + 1))
                            dve.scalar_tensor_tensor(MT[:, n % 2, :], PS[:, 3 * (m % 2) + g, 0:G], 0.0, RB[:, grp(g)],
                                                     ALU.max, ALU.mult).then_inc(bank_free, 1)
                            if n:
                                low(n - 1)
                    low(11)
                    if first:
                        dve.wait_ge(sem("y_zero"), KB * (l + 1))
                    q0 = 24 + 48 * l + 1
                    for d in range(4):
                        if not (last and l == 1 and d == 3):
                            split_lo((d + 1) % 2, 8 * j + (u0 + d + 6))
                        for b in range(2):
                            for g in range(NG):
                                n = 12 + 6 * d + 3 * b + g
                                dve.wait_ge(mm_done, 36 * j + (g0 + n + 1))
                                y = Y[:, 2 * d + b, grp(g)]
                                dve.tensor_tensor(y, y, PS[:, 3 * b + g, 0:G], ALU.add).then_inc(bank_free, 1)
                                q = n - 12
                                if last and q:
                                    add_square((q - 1) // 3 % 2, (q - 1) % 3, q0 + q - 1)
                    if last:
                        add_square(1, 2, q0 + 23)
                group(0, first=True)
                with dve.Fori(1, FFG - 1) as j:
                    group(j)
                group(FFG - 1, last=True)

            boundary("b0", "mix_post0", "ffn_pre0", U_MLP0)
            mlp(0, U_MLP0, G_MLP0)
            boundary("b1", "ffn_post0", "kv", U_KV)

            def kv_unit(i, s, stored, first=False):
                if not first:
                    dve.wait_ge(sem("kv_turned"), 6 * i + (3 * s - 3))
                dve.wait_ge(sem(f"kt_st{s}"), stored)
                for g in range(NG):
                    take(s, g, 6 * i + (G_KV + 3 * s + g + 1))
                split_lo(s, 2 * i + (U_KV + s + 3))
            for s in range(2):
                kv_unit(0, s, 0, True)
            with dve.Fori(1, 4) as i:
                for s in range(2):
                    kv_unit(i, s, 16 * i)
            with dve.Fori(4, 8) as i:
                for s in range(2):
                    kv_unit(i, s, 16 * 4)

            for k in range(KB):
                x_lo(k, "mix_pre1", "n2")
            dve.wait_ge(sem("lam_exp"), 2)
            ln(dve.tensor_tensor(lam[:, 4:5], lam[:, 3:4], lam[:, 2:3], ALU.subtract))
            ln(dve.tensor_scalar(lam[:, 5:6], lam[:, 4:5], LAM_INIT, None, ALU.subtract))
            dve.wait_ge(sem("mask_in"), 5)
            dve.tensor_copy(MA[:, :], P0[:, 0, 0:P])
            dve.tensor_copy(MB[:, :], P0[:, 0, P:2 * P]).then_inc(sem("mask_r"), 1)

            def take_q(g, n, bank=None):
                dve.wait_ge(mm_done, n)
                dve.scalar_tensor_tensor(QR[:, grp(g)], PS[:, 7 if bank is None else bank, 0:G], ATT_SCALE, RB[:, grp(g)],
                                         ALU.mult, ALU.mult).then_inc(bank_free, 1)

            for g in range(NG):
                take_q(g, G_Q + g + 1, g)

            def lower(o, a, hi):
                return dve.tensor_tensor(o, a, hi.bitcast(F32), ALU.subtract)

            def split_k(h1):
                dve.wait_ge(sem("k_hi"), h1)
                lower(KL[:, 0:SEQ], KR[:, 0:SEQ], KH[:, 0:SEQ]).then_inc(sem("k_lo"), 1)

            def split_q(h, s, g):
                dve.wait_ge(sem("q_hi"), 3 * h + (g + 1))
                lower(QL[:, s, grp(g)], QR[:, grp(g)], QH[:, s, grp(g)]).then_inc(sem("q_lo"), 1)

            split_k(1)
            for g in range(NG):
                split_q(0, 0, g)

            def att_extras(q, t, last):
                h, more = t.h, not (last and t.hp == 1)
                if t.i == 0:
                    dve.wait_ge(sem("kc_hi"), h + 1)
                    lower(KL[:, SCOL:NKEY], KR[:, SEQ:T], KH[:, SCOL:NKEY])
                    lower(KL[:, SEQ:SCOL], PS[:, 7, :], KH[:, SEQ:SCOL]).then_inc(sem("kc_lo"), 1)
                    if more:
                        split_lo(t.hp, 2 * q + (U_Q + t.hp + 3))
                if t.i == 1:
                    dve.wait_ge(sem("v_hi"), h + 1)
                    lower(VL[:, 0:NT, :], VR[:, 0:NT, :], VH[:, 0:NT, :]).then_inc(sem("v_lo"), 1)
                if t.i == 8 and more:
                    split_k(h + 2)
                if t.i in (4, 6, 8) and more:
                    split_q(h + 1, (t.hp + 1) % 2, (t.i - 4) // 2)

            def att_take(t):
                dve.wait_ge(sem("a_out"), t.n + 1)
                dve.tensor_copy(OC[t.f, t.par, :], PS[t.f, 6, 0:P]).then_inc(sem("a_oc"), 1)

            def att_combine(t):
                dve.wait_ge(sem("a_exp"), 2 * t.n + 2)
                dve.reciprocal(t.number(6, 2), t.number(4, 2)).then_inc(sem("a_c"), 1)
                dve.wait_ge(sem("a_c"), 2 * t.n + 1)
                dve.scalar_tensor_tensor(t.number(10), t.number(4), t.number(7), lam[t.f, 5:6], ALU.mult, ALU.mult)\
                    .then_inc(sem("a_c"), 1)
                dve.wait_ge(sem("a_c"), 2 * t.n + 2)
                w = P0[t.f, t.par, 0:t.keys]
                dve.scalar_tensor_tensor(w, P1[t.f, 0:t.keys], t.number(10), w, ALU.mult, ALU.add)\
                    .then_inc(sem("a_comb"), 1)

            def att_turned_lo(t):
                dve.wait_ge(sem("a_thi"), t.n + 1)
                for (src, dst), (_, hi) in zip(t.turned(TL), t.turned(TH)):
                    ins = lower(dst, src, hi)
                ins.then_inc(sem("a_tlo"), 1)

            def att_norm(t):
                dve.wait_ge(sem("a_pow"), t.n + 1)
                dve.tensor_scalar(ON[t.f, t.par, :], OC[t.f, t.par, :], t.number(14), t.number(6), ALU.mult, ALU.mult)\
                    .then_inc(sem("a_on"), 1)

            def att_max(t, m):
                dve.wait_ge(sem("a_scores"), 2 * t.n + (m + 1))
                dve.tensor_reduce(t.number(m), t.score(m), AX, ALU.max, negate=True).then_inc(sem("a_max"), 1)

            def att_turn_of_loop(q, first=False, last=False):
                for m in range(TPT + (4 if last else 0)):
                    t = Tile(q, m)
                    if m - 1 < TPT and not (first and m < 1):
                        att_combine(Tile(q, m - 1))
                    if m - 3 < TPT and not (first and m < 3):
                        att_take(Tile(q, m - 3))
                    if not (first and m < 4):
                        att_norm(Tile(q, m - 4))
                    if m < TPT:
                        if t.i in (3, 5, 7) and not (last and t.hp == 1):
                            g = (t.i - 3) // 2
                            take_q(g, 6 * q + (G_Q + 3 * (t.hp + 1) + g + 1))
                        att_max(t, 0)
                        att_max(t, 1)
                    if m - 1 < TPT and not (first and m < 1):
                        att_turned_lo(Tile(q, m - 1))
                    if m < TPT:
                        att_extras(q, t, last)

            att_turn_of_loop(0, first=True)
            with dve.Fori(1, NPAIR - 1) as q:
                att_turn_of_loop(q)
            att_turn_of_loop(NPAIR - 1, last=True)

            split_lo(1, U_WO + 2)
            for k in range(KB):
                x_lo(k, "sub", "wo")
            dense_y(U_WO, G_WO, 48, 1)
            boundary("b2", "mix_post1", "ffn_pre1", U_MLP1)
            mlp(1, U_MLP1, G_MLP1)
            boundary("b3", "ffn_post1", None)

            for t in range(NCH):
                dve.wait_ge(sem("y_turned"), t + 1)
                dve.tensor_copy(y_half(t, 1), PS[0:P if t < NT else DEC, 2 * (t % 4) + 1, :]).then_inc(sem("y_out_d"), 1)

        @block.gpsimd
        def _(pool):
            def token_pow(name):
                pool.wait_ge(sem("tok_var"), 2 * NORMS[name] + 2)
                pool.tensor_tensor(TV[:, 2, :], TV[:, 1, :], half[:, :], ALU.pow).then_inc(sem("tok_pow"), 1)

            pool.memset(ident[:, :], 0.0).then_inc(sem("ident"), 1)
            pool.wait_ge(sem("ident"), 1)
            pool.affine_select(out=ident[:, :], in_=ident[:, :], compare_op=ALU.not_equal, fill=1.0, base=0,
                               pattern=[[-1, P]], channel_multiplier=1).then_inc(sem("ident"), 1)
            pool.memset(WGH[:, :, :].bitcast(F32), 0.0).then_inc(sem("wg_zero"), 1)
            pool.memset(WGL[:, :, :].bitcast(F32), 0.0).then_inc(sem("wg_zero"), 1)
            pool.memset(RST[:, :], 1.0).then_inc(sem("setup"), 1)
            pool.wait_ge(sem("setup"), 1)
            pool.memset(RST[:, 0:T:LC], 0.0).then_inc(sem("rst"), 1)
            barrier(pool, PH["load"])
            token_pow("n0")
            barrier(pool, PH["proj"])
            for h in range(H):
                pool.wait_ge(sem("o_sig"), h + 1)
                pool.tensor_scalar(STG[:, h % 2, :], STG[:, h % 2, :], gcol("h", h), 1.0, ALU.mult, ALU.mult)\
                    .then_inc(sem("o_gain"), 1)
            barrier(pool, PH["gates"])
            barrier(pool, PH["mlstm"])

            def mlstm_consts():
                pool.memset(SEL[:, :, :], 0.0).then_inc(sem("sel"), 1)
                pool.memset(SELP[:, :, :], 0.0).then_inc(sem("sel"), 1)
                pool.memset(mask[:, :], 0.0).then_inc(sem("sel"), 1)
                pool.wait_ge(sem("sel"), 3)
                pool.affine_select(out=mask[:, :], in_=mask[:, :], compare_op=ALU.is_ge, fill=NEG, base=0,
                                   pattern=[[1, LC]], channel_multiplier=-1).then_inc(sem("sel"), 1)
                pool.affine_select(out=SEL[:, :, :], in_=SEL[:, :, :], compare_op=ALU.not_equal, fill=1.0, base=0,
                                   pattern=[[-1, H], [0, P]], channel_multiplier=1).then_inc(sem("sel"), 1)
                pool.affine_select(out=SELP[:, :, :].rearrange("h q (a d) -> h q a d", a=2),
                                   in_=SELP[:, :, :].rearrange("h q (a d) -> h q a d", a=2),
                                   compare_op=ALU.not_equal, fill=1.0, base=0,
                                   pattern=[[-2, NPAIR], [-1, 2], [0, 64]], channel_multiplier=1).then_inc(sem("sel"), 1)
            mlstm_consts()
            c_pow = sem("c_pow")
            with pool.Fori(0, NT) as c:
                pool.wait_ge(sem("c_den"), 8 * c + 7)
                pool.tensor_tensor(MS[:, 6, :], MS[:, 5, :], half[:, 0:H], ALU.pow).then_inc(c_pow, 1)
            pool.wait_ge(sem("c_den"), 8 * NT + 7)
            pool.tensor_tensor(MS[0:DEC, 6, :], MS[0:DEC, 5, :], half[0:DEC, 0:H], ALU.pow).then_inc(c_pow, 1)

            def boundary(name, l=None, pre=True):
                token_pow(name + "y")
                pool.wait_ge(sem("rb"), 3 * (NORMS[name + "y"] + 1))
                for k in range(POOL_Y, KB):
                    pool.tensor_tensor(Y[:, k, :], Y[:, k, :], RB[:, :], ALU.mult).then_inc(sem("y_scaled"), 1)
                if not pre:
                    return
                for k in range(1, KB):
                    pool.wait_ge(sem("squared_x"), KB * BOUNDS[name] + k + 1)
                    pool.wait_ge(sem("sq_sum"), SUMS[name + "y"] + k - 1)
                    pool.tensor_tensor(SQ[:, :], SQ[:, :], STG[:, k % 2, :], ALU.add).then_inc(sem("sq_sum"), 1)
                token_pow(name + "x")
                if l is not None:
                    for k in range(KB):
                        pool.wait_ge(sem("x_new"), KB * BOUNDS[name] + k + 1)
                        pool.memset(Y[:, k, :], 0.0).then_inc(sem("y_zero"), 1)

            def mlp(l, g0):
                with pool.Fori(0, FFG) as j:
                    for n in range(12):
                        pool.wait_ge(sem("bank_free"), RING + 36 * j + (g0 + n + 1))
                        pool.tensor_tensor(M2[:, n % 2, :], MT[:, n % 2, :], MT[:, n % 2, :], ALU.mult)\
                            .then_inc(sem("h_sq"), 1)

            barrier(pool, PH["out"])
            boundary("b0", 0)
            mlp(0, G_MLP0)
            boundary("b1")
            pool.wait_ge(sem("kv_st0"), 32 * 8)
            pool.wait_ge(sem("kv_st1"), 32 * 8)
            pool.memset(P0[:, 0, 0:2 * P], 0.0).then_inc(sem("mask_in"), 1)
            pool.wait_ge(sem("mask_in"), 1)
            for r in (0, 64):
                pool.memset(P0[r:r + 1, 0, 0:64], 1.0).then_inc(sem("mask_in"), 1)
                pool.memset(P0[r:r + 1, 0, P + 64:2 * P], NEG).then_inc(sem("mask_in"), 1)

            def att_turn_of_loop(q, first=False, last=False):
                for m in range(TPT + (3 if last else 0)):
                    t = Tile(q, m)
                    if not (first and m < 3):
                        o = Tile(q, m - 3)
                        pool.wait_ge(sem("a_ss"), o.n + 1)
                        pool.tensor_tensor(o.number(11), o.number(8), mean_eps[o.f, 0:1], ALU.mult)\
                            .then_inc(sem("a_var"), 1)
                        pool.wait_ge(sem("a_var"), 2 * o.n + 1)
                        pool.tensor_tensor(o.number(13), o.number(11), mean_eps[o.f, 1:2], ALU.add)\
                            .then_inc(sem("a_var"), 1)
                        pool.wait_ge(sem("a_var"), 2 * o.n + 2)
                        pool.tensor_tensor(o.number(14), o.number(13), half[o.f, 0:1], ALU.pow).then_inc(sem("a_pow"), 1)
                    if m < TPT and t.i == 3:
                        pool.wait_ge(sem("vc_hi"), t.h + 1)
                        pool.tensor_tensor(VL[:, NT:NT + 4, :], VR[:, NT:NT + 4, :], VH[:, NT:NT + 4, :].bitcast(F32),
                                           ALU.subtract)
                        pool.tensor_tensor(VL[0:DEC, NT + 4, :], VR[0:DEC, NT + 4, :],
                                           VH[0:DEC, NT + 4, :].bitcast(F32), ALU.subtract).then_inc(sem("vc_lo"), 1)
            att_turn_of_loop(0, first=True)
            with pool.Fori(1, NPAIR - 1) as q:
                att_turn_of_loop(q)
            att_turn_of_loop(NPAIR - 1, last=True)
            boundary("b2", 1)
            mlp(1, G_MLP1)
            boundary("b3", None, False)


_INS = ['x_prompt', 'x_sample', 'cache_k', 'cache_v', 'state_c', 'state_n', 'state_m', 'w_in_a', 'b_i_a', 'b_f_a',
        'g_h_a', 'w_out_a', 'g_kv', 'w_kv', 'w_q_b', 'lambda_q1', 'lambda_k1', 'lambda_q2', 'lambda_k2', 'g_sub_b',
        'w_o_b', 'g_mix_pre', 'g_mix_post', 'g_ffn_pre', 'g_ffn_post', 'w_up', 'w_down']
_OUTS = [(1, SEQ, D), (1, DEC, D), (1, 1, H, DK, DV), (1, 1, H, DK), (1, 1, H), (1, SEQ, H, 2, 64), (1, SEQ, H, 128),
         (1, 1, H, DK, DV), (1, 1, H, DK), (1, 1, H), (1, DEC, H, 2, 64), (1, DEC, H, 128)]


def kernel(**inputs):
    import numpy as _np
    import concourse.bacc as _bacc
    from concourse import mybir as _mybir
    from concourse.bass_utils import run_bass_kernel_spmd as _run

    nc = _bacc.Bacc("TRN2", target_bir_lowering=False, num_devices=1, dynamic_dma_scratch_size=1024)
    arrays, args = {}, []
    for name in _INS:
        a = _np.ascontiguousarray(inputs[name])
        arrays[f"in_{name}"] = a
        args.append(nc.dram_tensor(f"in_{name}", a.shape, _mybir.dt.from_np(a.dtype), kind="ExternalInput").ap())
    for i, shape in enumerate(_OUTS):
        args.append(nc.dram_tensor(f"out_{i}", shape, _mybir.dt.float32, kind="ExternalOutput").ap())
    for name, n in (("proj_s", 24), ("kT_s", H), ("o_s", H)):
        args.append(nc.dram_tensor(name, (n, P, T), _mybir.dt.float32).ap())
    stream_step(nc, *args)
    r = _run(nc, [arrays], core_ids=[0])
    return tuple(r.results[0][f"out_{i}"] for i in range(len(_OUTS)))
```

```python
from contextlib import ExitStack
import math

import concourse.bass as bass
from concourse import mybir

F32 = mybir.dt.float32
F32R = mybir.dt.float32r
ALU = mybir.AluOpType
ACT = mybir.ActivationFunctionType
AX = mybir.AxisListType.X

P = 128
D = 1024
KB = D // P
SEQ, DEC = 1024, 32
T = SEQ + DEC
NG = 3
G = T // NG
PAST = 512
H = 8
DK, DV = 64, 128
LC = 128
NT = SEQ // P
NCH = NT + 1
NPAIR = H // 2
DFF = 4 * D
FFG = DFF // 512
EPS = 1e-6
NEG = -1e30
LAM_INIT = 0.8 - 0.6 * math.exp(-0.3)
ATT_SCALE = 64 ** -0.5
K_SCALE = DK ** -0.5
SCOL = SEQ + PAST
NKEY = SCOL + DEC

U_PROJ, N_PROJ = 0, 24
U_OUT = U_PROJ + N_PROJ
U_MLP0 = U_OUT + KB
U_KV, N_KV = U_MLP0 + 8 * FFG, 16
U_Q = U_KV + N_KV
U_WO = U_Q + KB
U_MLP1 = U_WO + KB
G_PROJ = 0
G_OUT = G_PROJ + NG * N_PROJ
G_MLP0 = G_OUT + NG * KB
G_KV = G_MLP0 + 36 * FFG
G_Q = G_KV + NG * N_KV
G_WO = G_Q + NG * KB
G_MLP1 = G_WO + NG * KB
RING = 6

GAINS = ["mix_pre0", "mix_pre1", "mix_post0", "mix_post1", "ffn_pre0", "ffn_pre1", "ffn_post0", "ffn_post1",
         "kv", "h", "sub"]
R_U, R_INTER, R_G, R_EM, R_LI, R_LF, R_M, R_FC = range(8)


def stream_step(nc, x_prompt, x_sample, cache_k, cache_v, state_c, state_n, state_m, w_in, b_i, b_f, g_h, w_out,
                g_kv, w_kv, w_q, lq1, lk1, lq2, lk2, g_sub, w_o, g_mix_pre, g_mix_post, g_ffn_pre, g_ffn_post,
                w_up, w_down, y_prompt, y_sample, c_prompt, n_prompt, m_prompt, k_prompt, v_prompt,
                c_sample, n_sample, m_sample, k_sample, v_sample, proj_s, kT_s, o_s, gate_s):
    with ExitStack() as ctx:
        def sb(name, shape, dt=F32, scope=ctx):
            return scope.enter_context(nc.sbuf_tensor(name, shape, dt))

        sems = {}

        def sem(name):
            if name not in sems:
                sems[name] = ctx.enter_context(nc.semaphore(name))
            return sems[name]

        X = sb("X", [P, KB, T])
        XH = sb("XH", [P, KB, T], F32R)
        XL = sb("XL", [P, KB, T], F32R)
        WR = sb("WR", [P, 2, D])
        WH = sb("WH", [P, 2, D], F32R)
        WL = sb("WL", [P, 2, D], F32R)
        RB = sb("RB", [P, T])
        STG = sb("STG", [P, 2, T])
        SQ = sb("SQ", [P, T])
        TV = sb("TV", [P, 3, NCH])
        ident = sb("ident", [P, P])
        ones = sb("ones", [P, 1])
        GN = sb("GN", [P, len(GAINS) * KB])
        lam = sb("lam", [P, 8])
        half = sb("half", [P, NCH])
        mean_eps = sb("mean_eps", [P, 2])
        bg = sb("bg", [H, 4])
        MP = sb("MP", [H, NCH])
        with ExitStack() as sc:
            VR = sb("VR", [P, 13, P], F32, sc)
            CK = sb("CK", [P, 4, P], F32, sc)
            KH = sb("KH", [P, NKEY], F32R, sc)
            KL = sb("KL", [P, NKEY], F32R, sc)
            QH = sb("QH", [P, 2, T], F32R, sc)
            QL = sb("QL", [P, 2, T], F32R, sc)
            VH = sb("VH", [P, 13, P], F32R, sc)
            VL = sb("VL", [P, 13, P], F32R, sc)
            P0 = sb("P0", [P, 2, D], F32, sc)
            P1 = sb("P1", [P, D], F32, sc)
            TH = sb("TH", [P, 2, KB, P], F32R, sc)
            TL = sb("TL", [P, 2, KB, P], F32R, sc)
            OC = sb("OC", [P, 2, P], F32, sc)
            ON = sb("ON", [P, 2, P], F32, sc)
            AS = sb("AS", [P, 6, 16], F32, sc)
            MA = sb("MA", [P, P], F32R, sc)
            MB = sb("MB", [P, P], F32R, sc)
        QR, KR, OTS = STG[:, 0, :], STG[:, 1, :], SQ[:, :]
        with ExitStack() as sc:
            OT = sb("OT", [P, 2, NCH, P], F32, sc)
        Y = sb("Y", [P, KB, T])
        rows = Y
        XG = Y[:, :, :].rearrange("p k t -> p (k t)")[:, 0:2 * D].rearrange("p (j b t) -> p j b t", j=2, b=KB)
        with ExitStack() as sc:
            HH = sb("HH", [P, 4, T], F32R, sc)
            with ExitStack() as under:
                RAW = sb("RAW", [P, 2, T], F32, under)
            HL = sb("HL", [P, 4, T], F32R, sc)
            MT = sb("MT", [P, 2, G], F32, sc)
            M2 = sb("M2", [P, 2, G], F32, sc)
        with ExitStack() as sc:
            WG = sb("WG", [P, KB, 16], F32, sc)
            WGH = sb("WGH", [P, KB, 40], F32R, sc)
            WGL = sb("WGL", [P, KB, 40], F32R, sc)
            RST = sb("RST", [H, T], F32, sc)
            gain_rows = sb("gain_rows", [len(GAINS) * KB, P], F32, sc)
            lam_in = sb("lam_in", [P, 4, DK], F32, sc)
            XT = sb("XT", [P, 4, D], F32, sc)
        with ExitStack() as sc:
            CH = sb("CH", [P, 2, 16, LC], F32, sc)
            RC = sb("RC", [H, 2, LC], F32, sc)
            KN = sb("KN", [P, 4 * P], F32, sc)
            VC = sb("VC", [P, H, DV + 1], F32, sc)
            DT = sb("DT", [P, H, LC], F32, sc)
            SD = sb("SD", [P, H, LC], F32, sc)
            QI = sb("QI", [P, NPAIR, LC], F32, sc)
            CB = sb("CB", [P, NPAIR, 2, DV + 1], F32, sc)
            CS = sb("CS", [P, NPAIR, 2, DV + 1], F32, sc)
            HN = sb("HN", [P, H, DV], F32, sc)
            MS = sb("MS", [P, 2, 8, H], F32, sc)
            DEC4 = sb("DEC4", [P, NPAIR], F32, sc)
            mask = sb("mask", [P, LC], F32, sc)
        SN = SQ[:, 0:H * DV].rearrange("p (h e) -> p h e", h=H)
        with ExitStack() as sc:
            OG = sb("OG", [P, 4, T], F32, sc)
        PS = ctx.enter_context(nc.psum_tensor("PS", [P, 8, 512], F32))

        def gcol(name, k):
            j = GAINS.index(name) * KB
            return GN[:, j + k:j + k + 1] if isinstance(k, int) else GN[:, bass.ds(k + j, 1)]

        def grp(g):
            return slice(g * G, (g + 1) * G)

        def y_half(t, b):
            if t < NT:
                return Y[:, :, :].rearrange("p k t -> p (k t)")[:, t * D + 512 * b:t * D + 512 * b + 512]
            return STG[0:DEC, 0, 512 * b:512 * b + 512]

        block = ctx.enter_context(nc.Block())
        w_in2, w_out2 = w_in[0], w_out[0]

        def weight_cols(w, c):
            return w[:, bass.ds(c * P, P)].rearrange("(k p) n -> p k n", p=P)

        def barrier(e, n):
            e.drain().then_inc(sem("phase"), 1)
            e.wait_ge(sem("phase"), 4 * n)

        PHASES = ["load"]
        WEIGHTS_AT = 5

        class Chunk:
            def __init__(self, i, m):
                self.n, self.par, self.half = 2 * i + m, m % 2, i + m // 2
                self.sample = isinstance(i, int) and self.n == NT
                self.L = DEC if self.sample else LC
                self.f = slice(0, self.L)
                self.cols = slice(SEQ, T) if self.sample else bass.ds(self.n * LC, LC)
                self.state = CS if self.sample else CB

            def number(self, c):
                return MS[self.f, self.par, c, :]

        FILL0 = U_PROJ + 17
        TPT = 2 * (NT + 1)

        class Tile:
            def __init__(self, q, m):
                self.hp, self.i = (m % TPT) // (NT + 1), m % (NT + 1)
                self.n = TPT * q + m
                self.h = 2 * q + m // (NT + 1)
                self.par, self.slot = m % 2, m % 6
                s = self.i == NT
                self.L = DEC if s else P
                self.keys = PAST + DEC if s else (self.i + 1) * P
                self.q0, self.k0 = (SEQ, SEQ) if s else (self.i * P, 0)
                self.blocks = [(b, P if b < 4 or not s else DEC) for b in range(-(-self.keys // P))]
                self.v0 = NT if s else 0
                self.f = slice(0, self.L)
                self.sample = s

            def bank(self, m, c):
                return 2 * m + (self.i % 2 if self.i < 4 else c // 512)

            def score(self, m):
                if self.keys <= 512:
                    return PS[self.f, self.bank(m, 0), 0:self.keys]
                return PS[self.f, 2 * m:2 * m + 2, :].rearrange("p a b -> p (a b)")[:, 0:self.keys]

            def turned(self, T4):
                out = []
                for b in range(0, len(self.blocks), 4):
                    w = min(4, len(self.blocks) - b)
                    if self.sample and b == 4:
                        out.append((PS[0:DEC, 5, 0:self.L], T4[0:DEC, self.par, 4, self.f]))
                    else:
                        out.append((PS[:, 4 + b // 4, 0:w * self.L].rearrange("p (t q) -> p t q", t=w),
                                    T4[:, self.par, b:b + w, self.f]))
                return out

            def number(self, c, w=1):
                return AS[self.f, self.slot, c:c + w]

        FILL = (2, 3, 4, 5, 6, 7)
        TAKE = (4, 6, 8)
        SPLIT = (5, 7, 8)
        PH = {n: i + 1 for i, n in enumerate(PHASES)}

        NORMS = {n: i for i, n in enumerate(["n0", "b0y", "b0x", "b1y", "b1x", "b2y", "b2x", "b3y"])}
        SPLITS = {n: i for i, n in enumerate(["h", "b0", "b1", "n2", "wo", "b2"])}
        SUMS = {"b0y": 24, "b0x": 31, "b1y": 55, "b1x": 62, "b2y": 86, "b2x": 93, "b3y": 117}
        POOL_Y = 6
        RAW_PAIR = {"b0": 0, "b2": 1}
        BOUNDS = {n: i for i, n in enumerate(["b0", "b1", "b2", "b3"])}

        @block.sync
        def _(sp):
            gains_in, consts = sem("gains_in"), sem("consts")
            for j, (w, r) in enumerate([(g_mix_pre, 0), (g_mix_post, 16), (g_ffn_pre, 32), (g_ffn_post, 48)]):
                sp.dma_start(gain_rows[r:r + 16, :], w.rearrange("l (k p) -> (l k) p", p=P)).then_inc(gains_in, 16)
            sp.dma_start(gain_rows[64:72, :], g_kv.rearrange("(k p) -> k p", p=P)).then_inc(gains_in, 16)
            sp.dma_start(gain_rows[72:80, :], g_h.rearrange("l (k p) -> (l k) p", p=P)).then_inc(gains_in, 16)
            sp.dma_start(gain_rows[80:88, :], g_sub.rearrange("l (k p) -> (l k) p", p=P)).then_inc(gains_in, 16)
            x_t = x_prompt[0].rearrange("(t p) n -> t p n", p=P)
            for j in range(4):
                sp.dma_start(XT[:, j, :], x_t[j]).then_inc(sem(f"x_in{j}"), 16)
            for s in range(2):
                sp.dma_start(WR[:, s, :].rearrange("p (k n) -> p k n", k=KB),
                             weight_cols(w_in2, s)).then_inc(sem(f"w_in{s}"), 16)
            sp.dma_start(WG[:, :, :], w_in2[:, 3072:3088].rearrange("(k p) n -> p k n", p=P)).then_inc(sem("wg_in"), 16)
            for j, v in enumerate([b_i, b_f, state_m[0]]):
                sp.dma_start(bg[:, j:j + 1], v.rearrange("l h -> h l")).then_inc(consts, 16)
            for j, v in enumerate([lq1, lk1, lq2, lk2]):
                sp.dma_start(lam_in[:, j, :], v.to_broadcast([P, DK])).then_inc(consts, 16)
            for t in range(4, NCH):
                sp.wait_ge(sem("x_turned"), t - 3)
                sp.wait_ge(sem("x_sumsq"), t - 3)
                sp.dma_start(XT[:, t % 4, :] if t < NT else XT[0:DEC, 0, :], x_t[t] if t < NT else x_sample[0])\
                    .then_inc(sem(f"x_in{t % 4}"), 16)

            def load(w, s, src, k=KB):
                sp.wait_ge(sem("w_lo"), w - 1)
                sp.dma_start(WR[:, s, :].rearrange("p (k n) -> p k n", k=k), src).then_inc(sem(f"w_in{s}"), 16)

            def load_cols(w, u0, n, i0=0):
                with sp.Fori(i0, n // 2) as i:
                    for s in range(2):
                        load(2 * i + (u0 + s), s, weight_cols(w, 2 * i + s))

            def load_mlp(l, u0):
                up = w_up[l]
                down = w_down[l]
                with sp.Fori(0, FFG) as j:
                    for m in range(4):
                        load(8 * j + (u0 + m), m % 2, weight_cols(up, 4 * j + m))
                    for d in range(4):
                        src = down[bass.ds(j * 512, 512), 256 * d:256 * d + 256].rearrange("(k p) n -> p k n", p=P)
                        load(8 * j + (u0 + 4 + d), d % 2, src, 4)

            load_cols(w_in2, U_PROJ, N_PROJ, 1)
            load_cols(w_out2, U_OUT, KB)
            load_mlp(0, U_MLP0)
            load_cols(w_kv, U_KV, N_KV)
            load_cols(w_q[0], U_Q, KB)
            load_cols(w_o[0], U_WO, KB)
            load_mlp(1, U_MLP1)

            y_t = y_prompt[0].rearrange("(t p) n -> t p n", p=P)
            for t in range(NCH):
                sp.wait_ge(sem("y_out_a"), t + 1)
                sp.wait_ge(sem("y_out_d"), t + 1)
                src = Y[:, :, :].rearrange("p k t -> p (k t)")[:, t * D:(t + 1) * D] if t < NT else STG[0:DEC, 0, 0:D]
                sp.dma_start(y_t[t] if t < NT else y_sample[0], src).then_inc(sem("y_st"), 16)
            sp.wait_ge(sem("y_st"), 16 * NCH)

        @block.tensor
        def _(pe):
            mm_done, bank_free, w_lo = sem("mm_done"), sem("bank_free"), sem("w_lo")

            def three(out, lh, ll, rh, rl, start, stop):
                pe.matmul(out, lh, rh, start=start, stop=False)
                pe.matmul(out, lh, rl, start=False, stop=False)
                return pe.matmul(out, ll, rh, start=False, stop=stop)

            def unit(s, w_count, g0):
                pe.wait_ge(w_lo, w_count)
                for g in range(NG):
                    bank = PS[:, 3 * s + g, 0:G]
                    pe.wait_ge(bank_free, g0 + (g + 1))
                    for k in range(KB):
                        ws = slice(k * P, k * P + P)
                        mm = three(bank, WH[:, s, ws], WL[:, s, ws], XH[:, k, grp(g)], XL[:, k, grp(g)],
                                   k == 0, k == KB - 1)
                    mm.then_inc(mm_done, 1)

            def dense(u0, g0, n=KB):
                with pe.Fori(1, n // 2) as i:
                    for s in range(2):
                        unit(s, 2 * i + (u0 + s + 1), 6 * i + (g0 + 3 * s))

            def first_pair(u0, g0, split, n=2):
                pe.wait_ge(w_lo, u0 + n)
                pe.wait_ge(bank_free, g0 + RING)
                for k in range(KB):
                    pe.wait_ge(sem("x_lo"), KB * SPLITS[split] + k + 1)
                    ws = slice(k * P, k * P + P)
                    for s in range(n):
                        for g in range(NG):
                            mm = three(PS[:, 3 * s + g, 0:G], WH[:, s, ws], WL[:, s, ws], XH[:, k, grp(g)],
                                       XL[:, k, grp(g)], k == 0, k == KB - 1)
                            if k == KB - 1:
                                mm.then_inc(mm_done, 1)

            def token_sums(name):
                pe.wait_ge(sem("sq_sum"), SUMS[name])
                for t in range(NCH):
                    L = P if t < NT else DEC
                    mm = pe.matmul(PS[0:L, 7, t:t + 1], SQ[:, t * P:t * P + L], ones[:, :], start=True, stop=True)
                mm.then_inc(sem("tok_sum"), 1)

            def spread_rms(name):
                n = NORMS[name]
                pe.wait_ge(sem("tok_pow"), n + 1)
                for t in range(NCH):
                    L = P if t < NT else DEC
                    if t == NT:
                        pe.wait_ge(sem("rb"), 3 * n + 1)
                    mm = pe.matmul(PS[:, 6 + t // 4 % 2, (t % 4) * P:(t % 4) * P + L],
                                   TV[0:L, 2, t:t + 1].to_broadcast([L, P]), ident[0:L, 0:L], start=True, stop=True)
                    if t % 4 == 3 or t == NT:
                        mm.then_inc(sem("tok_spread"), 1)

            barrier(pe, PH["load"])
            pe.wait_ge(sem("gains_in"), 16 * 7)
            pe.wait_ge(sem("ident"), 2)
            pe.transpose(PS[:, 7, 0:88], gain_rows[:, :], ident[0:88, 0:88]).then_inc(sem("gains_turned"), 1)
            with pe.Fori(0, NT // 4) as i:
                for j in range(4):
                    pe.wait_ge(sem(f"x_in{j}"), 16 * i + 16)
                    pe.wait_ge(sem("x_cp_a"), 4 * i + (j + 1))
                    pe.wait_ge(sem("x_cp_d"), 4 * i + (j + 1))
                    for b in range(KB):
                        mm = pe.transpose(PS[:, 2 * (j % 2) + b // 4, (b % 4) * P:(b % 4) * P + P],
                                          XT[:, j, b * P:b * P + P], ident[:, :])
                    mm.then_inc(sem("x_turned"), 1)
            pe.wait_ge(sem("x_in0"), 16 * (NT // 4 + 1))
            pe.wait_ge(sem("x_cp_a"), NT + 1)
            pe.wait_ge(sem("x_cp_d"), NT + 1)
            for b in range(KB):
                mm = pe.transpose(PS[:, b // 4, (b % 4) * DEC:(b % 4 + 1) * DEC], XT[0:DEC, 0, b * P:b * P + P], ident[0:DEC, 0:DEC])
            mm.then_inc(sem("x_turned"), 1)

            pe.wait_ge(sem("wg_lo"), 1)
            for g in range(NG):
                pe.wait_ge(sem("x_lo0"), -(-(g + 1) * G // P))
                for k in range(KB):
                    mm = three(PS[0:40, 5 - g, 0:G], WGH[:, k, :], WGL[:, k, :], XH[:, k, grp(g)], XL[:, k, grp(g)],
                               k == 0, k == KB - 1)
                mm.then_inc(sem("gates_mm"), 1)
            spread_rms("n0")
            unit(0, 1, 0)
            pe.wait_ge(sem("gates_read"), 6)
            unit(1, 2, 3)
            dense(U_PROJ, G_PROJ, 16)
            unit(0, FILL0, 3 * (FILL0 - 1))

            def turn_in(C):
                pe.wait_ge(sem(f"ch_in{C.par}"), 16 * C.half + 16)
                pe.wait_ge(sem("rc_in"), 16 * C.n + 16)
                pe.wait_ge(sem("c_hn"), 2 * C.n + 2)
                pe.wait_ge(sem("c_qn"), C.n + 1)
                pe.wait_ge(sem("c_y"), C.n + 1)
                for b in range(4):
                    pe.transpose(PS[C.f, 6, b * P:b * P + P], CH[:, C.par, 4 + b, C.f], ident[:, :])
                for b in range(H):
                    pe.transpose(PS[C.f, b // 4, (b % 4) * P:(b % 4) * P + P], CH[:, C.par, 8 + b, C.f], ident[:, :])
                pe.transpose(PS[C.f, 2, 0:H], RC[:, 0, C.f], ident[0:H, 0:H])
                pe.transpose(PS[C.f, 2, H:2 * H], RC[:, 1, C.f], ident[0:H, 0:H]).then_inc(sem("c_turned"), 1)

            def scores(C):
                pe.wait_ge(sem("c_upd"), 5 * C.n + 5)
                for h in range(H):
                    r = slice(64 * (h % 2), 64 * (h % 2) + 64)
                    mm = pe.matmul(PS[C.f, 3 + h % 2, (h // 2) * C.L:(h // 2 + 1) * C.L], CH[r, C.par, 4 + h // 2, C.f],
                                   CH[r, C.par, h // 2, C.f], start=True, stop=True)
                mm.then_inc(sem("c_scores"), 1)

            def numerator(C):
                pe.wait_ge(sem("c_vc"), C.n + 1)
                pe.wait_ge(sem("c_vc2"), C.n + 1)
                pe.wait_ge(sem("c_cols"), C.n + 1)
                pe.wait_ge(sem("c_qi"), C.n + 1)
                pe.wait_ge(sem("c_sd"), 2 * C.n + 2)
                S = C.state
                for p in range(NPAIR):
                    b, o = p // 2, 256 * (p % 2)
                    pe.matmul(PS[C.f, b, o:o + 256], QI[:, p, C.f], S[:, p, :, 0:DV], start=True, stop=False,
                              skip_group_check=True)
                    pe.matmul(PS[C.f, 2, 2 * p:2 * p + 2], QI[:, p, C.f], S[:, p, :, DV], start=True, stop=False,
                              skip_group_check=True)
                    for a in range(2):
                        h = 2 * p + a
                        pe.matmul(PS[C.f, b, o + a * P:o + a * P + P], SD[C.f, h, C.f], VC[C.f, h, 0:DV],
                                  start=False, stop=True, skip_group_check=True)
                        mm = pe.matmul(PS[C.f, 2, h:h + 1], SD[C.f, h, C.f], VC[C.f, h, DV:DV + 1],
                                       start=False, stop=True, skip_group_check=True)
                mm.then_inc(sem("c_num"), 1)

            def contribution(C):
                pe.wait_ge(sem("c_y"), C.n + 2)
                pe.wait_ge(sem("c_kw"), C.n + 1)
                for p in range(NPAIR):
                    k = KN[C.f, p * P:p * P + P]
                    pe.matmul(PS[:, 3 + p // 2, 256 * (p % 2):256 * (p % 2) + 256], k, VC[C.f, 2 * p:2 * p + 2, 0:DV],
                              start=True, stop=True)
                    mm = pe.matmul(PS[:, 5, p:p + 1], k, VC[C.f, 2 * p, DV:DV + 1], start=True, stop=True)
                mm.then_inc(sem("c_kv"), 1)

            def turn_out(C, last=False):
                if last:
                    pe.wait_ge(sem("c_upd"), 5 * C.n + 10)
                else:
                    pe.wait_ge(sem("c_kn"), C.n + 2)
                pe.wait_ge(sem("c_hs"), C.n + 1)
                for h in range(H):
                    mm = pe.transpose(PS[:, 5 + h // 4, (h % 4) * C.L:(h % 4 + 1) * C.L], HN[C.f, h, :], ident[C.f, C.f])
                mm.then_inc(sem("c_hT"), 1)

            def fill(C, g):
                s = (C.par + 1) % 2
                pe.wait_ge(w_lo, C.n + (FILL0 + 1))
                pe.wait_ge(bank_free, 3 * C.n + (RING + 3 * FILL0 + g))
                for k in range(KB):
                    ws = slice(k * P, k * P + P)
                    mm = three(PS[:, 7, 0:G], WH[:, s, ws], WL[:, s, ws], XH[:, k, grp(g)], XL[:, k, grp(g)],
                               k == 0, k == KB - 1)
                mm.then_inc(mm_done, 1)

            def step(C, N, filled):
                numerator(C)
                contribution(C)
                if filled:
                    fill(C, 0)
                turn_in(N)
                if filled:
                    fill(C, 1)
                scores(N)
                turn_out(C)
                if filled:
                    fill(C, 2)

            pe.sem_inc(sem("c_hT"), 1)
            pe.wait_ge(bank_free, RING + 3 * FILL0)
            turn_in(Chunk(0, 0))
            scores(Chunk(0, 0))
            with pe.Fori(0, NT // 2 - 1) as i:
                for m in range(2):
                    step(Chunk(i, m), Chunk(i, m + 1), True)
            step(Chunk(NT // 2 - 1, 0), Chunk(NT // 2 - 1, 1), True)
            step(Chunk(NT // 2 - 1, 1), Chunk(NT // 2, 0), False)
            pe.wait_ge(sem("cs_in"), 64)
            numerator(Chunk(NT // 2, 0))
            contribution(Chunk(NT // 2, 0))
            turn_out(Chunk(NT // 2, 0), True)

            first_pair(U_OUT, G_OUT, "h")
            dense(U_OUT, G_OUT)

            def boundary(name, u0, g0):
                token_sums(name + "y")
                spread_rms(name + "y")
                if u0 is not None:
                    first_pair(u0, g0, name)
                    token_sums(name + "x")
                    if name in RAW_PAIR:
                        unit(0, u0 + 3, g0 + 6)
                    spread_rms(name + "x")

            def mlp(l, u0, g0):
                def group(j, first=False):
                    for m in range(3 if first else 0, 4):
                        unit(m % 2, 8 * j + (u0 + m + 1), 36 * j + (g0 + 3 * m))
                    for d in range(4):
                        s = d % 2
                        pe.wait_ge(w_lo, 8 * j + (u0 + 5 + d))
                        for b in range(2):
                            for g in range(NG):
                                pe.wait_ge(bank_free, 36 * j + (g0 + 12 + 6 * d + 3 * b + g + 1))
                                for k in range(4):
                                    if d == 0 and b == 0:
                                        pe.wait_ge(sem("h_lo"), 12 * j + (96 * l + 3 * k + g + 1))
                                    ws = slice(k * 256 + b * P, k * 256 + b * P + P)
                                    mm = three(PS[:, 3 * b + g, 0:G], WH[:, s, ws], WL[:, s, ws],
                                               HH[:, k, grp(g)], HL[:, k, grp(g)], k == 0, k == 3)
                                mm.then_inc(mm_done, 1)

                group(0, True)
                with pe.Fori(1, FFG) as j:
                    group(j)

            boundary("b0", U_MLP0, G_MLP0)
            mlp(0, U_MLP0, G_MLP0)
            boundary("b1", U_KV, G_KV)

            def rows_of(s, v3):
                pe.wait_ge(bank_free, RING + G_KV + 3 + v3)
                pe.wait_ge(sem("kv_rows"), v3)
                for t in range(NT):
                    mm = pe.transpose(PS[:, 6 + t // 4, (t % 4) * P:(t % 4) * P + P], STG[:, s, t * P:t * P + P],
                                      ident[:, :])
                    if t % 4 == 3:
                        mm.then_inc(sem("kv_turned"), 1)
                pe.wait_ge(sem("kv_rows"), v3 + 1)
                pe.transpose(PS[0:DEC, 6, 0:P], STG[:, s, SEQ:T], ident[:, :]).then_inc(sem("kv_turned"), 1)

            rows_of(0, 0)
            with pe.Fori(1, N_KV // 2) as i:
                for s in range(2):
                    unit(s, 2 * i + (U_KV + s + 1), 6 * i + (G_KV + 3 * s))
                    rows_of(1 - s, 6 * i + 3 * (s - 1))
            rows_of(1, 3 * (N_KV - 1))

            first_pair(U_Q, G_Q, "n2", 1)

            def att_scores(t, first):
                for m in range(2):
                    r = slice(64 * m, 64 * m + 64)
                    back = 1 if t.i in (0, 4, 5, 6, 7, 8) else 2
                    if not (first and t.i < back and t.hp == 0):
                        pe.wait_ge(sem("a_exp"), 2 * t.n + (m + 1 - 2 * back))
                    if first and t.hp == 0 and m == 0:
                        pe.wait_ge(sem("q_lo"), (t.q0 + t.L - 1) // G + 1)
                    elif t.i == 0 and m == 0:
                        pe.wait_ge(sem("q_lo"), 3 * t.h + 3)
                    if t.i == 0 and m == 0:
                        pe.wait_ge(sem("k_lo"), t.h + 1)
                    if t.sample:
                        if m == 0:
                            pe.wait_ge(sem("kc_lo"), t.h + 1)
                        pe.sem_inc(sem("sample_step"), 1)
                    for c in range(0, t.keys, 512):
                        w = min(512, t.keys - c)
                        out = PS[t.f, t.bank(m, c), 0:w]
                        kh, kl = KH[r, t.k0 + c:t.k0 + c + w], KL[r, t.k0 + c:t.k0 + c + w]
                        qs = slice(t.q0, t.q0 + t.L)
                        pe.matmul(out, QH[r, t.hp, qs], kh, start=True, stop=False)
                        if not t.sample and c + w == t.keys:
                            pe.matmul(PS[t.f, t.bank(m, c), w - P:w], MA[r, :], MB[r, :], start=False, stop=False,
                                      skip_group_check=True)
                        pe.matmul(out, QH[r, t.hp, qs], kl, start=False, stop=False)
                        mm = pe.matmul(out, QL[r, t.hp, qs], kh, start=False, stop=True)
                    mm.then_inc(sem("a_scores"), 1)

            def att_turn(t):
                pe.wait_ge(sem("a_tlo"), t.n)
                pe.wait_ge(sem("a_comb"), t.n + 1)
                if t.sample:
                    pe.sem_inc(sem("sample_step"), 1)
                for b, K in t.blocks:
                    mm = pe.transpose(PS[0:K, 4 + b // 4, (b % 4) * t.L:(b % 4 + 1) * t.L],
                                      P0[t.f, t.par, b * P:b * P + K], ident[t.f, t.f])
                mm.then_inc(sem("a_turned"), 1)

            def att_values(t, first):
                pe.wait_ge(sem("a_tlo"), t.n + 1)
                if not first:
                    pe.wait_ge(sem("a_otc"), t.n - 1)
                elif t.n >= 1:
                    pe.wait_ge(sem("a_oc"), t.n)
                if t.i == 0:
                    pe.wait_ge(sem("v_lo"), t.h + 1)
                if t.sample:
                    pe.wait_ge(sem("vc_lo"), t.h + 1)
                    pe.sem_inc(sem("sample_step"), 1)
                for b, K in t.blocks:
                    k = slice(0, K)
                    mm = three(PS[t.f, 6, 0:P], TH[k, t.par, b, t.f], TL[k, t.par, b, t.f], VH[k, t.v0 + b, :],
                               VL[k, t.v0 + b, :], b == 0, b == len(t.blocks) - 1)
                mm.then_inc(sem("a_out"), 1)

            def att_out(t, end):
                pe.wait_ge(sem("a_oc"), t.n + (1 if end else 2))
                pe.wait_ge(sem("a_on"), t.n + 1)
                if t.sample:
                    pe.sem_inc(sem("sample_step"), 1)
                pe.transpose(PS[:, 6, P:P + t.L], ON[t.f, t.par, :], ident[t.f, t.f]).then_inc(sem("a_oT"), 1)

            def att_fill(q, t):
                s = (t.hp + 1) % 2
                i0 = 12 * FILL.index(t.i)
                g = i0 // 24
                unit0 = G_Q + 3 * (t.hp + 1)
                if i0 == 0:
                    pe.wait_ge(w_lo, 2 * q + (U_Q + t.hp + 2))
                if i0 % 24 == 0:
                    pe.wait_ge(bank_free, 6 * q + (RING + unit0 + g))
                for k in range((i0 % 24) // 3, (i0 % 24) // 3 + 4):
                    ws = slice(k * P, k * P + P)
                    mm = three(PS[:, 7, 0:G], WH[:, s, ws], WL[:, s, ws], XH[:, k, grp(g)], XL[:, k, grp(g)],
                               k == 0, k == KB - 1)
                if i0 % 24 == 12:
                    mm.then_inc(mm_done, 1)

            def att_cache(q, t):
                pe.wait_ge(sem("ck_in"), 32 * q + (16 * t.hp + 16))
                pe.wait_ge(bank_free, 6 * q + (RING + G_Q + 3 * (t.hp + 1)))
                for b in range(4):
                    mm = pe.transpose(PS[:, 7, b * P:b * P + P], CK[:, b, :], ident[:, :])
                mm.then_inc(sem("a_ckT"), 1)

            def att_turn_of_loop(q, first=False, last=False):
                for m in range(TPT + (4 if last else 0)):
                    t = Tile(q, m)
                    fill = m < TPT and t.i in FILL and not (last and t.hp == 1)
                    if m < TPT:
                        att_scores(t, first)
                    if m - 1 < TPT and not (first and m < 1):
                        att_turn(Tile(q, m - 1))
                    if not (first and m < 4):
                        att_out(Tile(q, m - 4), m - 4 == TPT - 1)
                    if m < TPT and t.i == 0:
                        att_cache(q, t)
                    if fill:
                        if t.i == 1:
                            pe.wait_ge(sem("kc_lo"), t.h + 1)
                        att_fill(q, t)
                    if m - 2 < TPT and not (first and m < 2):
                        att_values(Tile(q, m - 2), first and m < 4)

            pe.wait_ge(sem("mask_r"), 1)
            att_turn_of_loop(0, first=True)
            with pe.Fori(1, NPAIR - 1) as q:
                att_turn_of_loop(q)
            att_turn_of_loop(NPAIR - 1, last=True)

            first_pair(U_WO, G_WO, "wo")
            dense(U_WO, G_WO)
            boundary("b2", U_MLP1, G_MLP1)
            mlp(1, U_MLP1, G_MLP1)
            boundary("b3", None, None)

            pe.wait_ge(sem("x_new"), KB * 4)
            for t in range(NCH):
                L = P if t < NT else DEC
                if t >= 4:
                    pe.wait_ge(sem("y_out_a"), t - 3)
                    pe.wait_ge(sem("y_out_d"), t - 3)
                for b in range(KB):
                    mm = pe.transpose(PS[0:L, 2 * (t % 4) + b // 4, (b % 4) * P:(b % 4) * P + P],
                                      X[:, b, t * P:t * P + L], ident[:, :])
                mm.then_inc(sem("y_turned"), 1)

        @block.scalar
        def _(act):
            mm_done, bank_free, w_hi = sem("mm_done"), sem("bank_free"), sem("w_hi")

            def split_hi(s, u2, g):
                act.wait_ge(sem(f"w_in{s}"), 16 * u2 + 16)
                if g is not None:
                    act.wait_ge(mm_done, g)
                act.activation(WH[:, s, :], WR[:, s, :], ACT.Copy).then_inc(w_hi, 1)

            def square(src, s, g):
                act.activation(STG[:, s, grp(g)], src, ACT.Square).then_inc(sem("squared"), 1)

            def take_rms(name):
                n = NORMS[name]
                for b, c in enumerate((slice(0, 512), slice(512, SEQ), slice(SEQ, T))):
                    act.wait_ge(sem("tok_spread"), 3 * n + b + 1)
                    act.activation(RB[:, c], PS[:, 6 + b % 2, 0:c.stop - c.start], ACT.Copy).then_inc(sem("rb"), 1)

            act.sem_inc(sem("x_cp_a"), 2)
            barrier(act, PH["load"])
            act.wait_ge(sem("gains_turned"), 1)
            act.activation(GN[:, :], PS[:, 7, 0:88], ACT.Copy).then_inc(sem("gains"), 1)
            def weights_hi():
                split_hi(0, 0, None)
                act.wait_ge(sem("wg_in"), 16)
                act.wait_ge(sem("wg_zero"), 2)
                act.activation(WGH[:, :, 0:8], WG[:, :, 0:8], ACT.Copy).then_inc(sem("wg_hi"), 1)
                act.activation(WGH[:, :, 32:40], WG[:, :, 8:16], ACT.Copy).then_inc(sem("wg_hi"), 1)

            def tile(t):
                return (slice(t * P, t * P + P), P) if t < NT else (slice(SEQ, T), DEC)

            def x_tile(t):
                c, L = tile(t)
                act.wait_ge(sem(f"x_in{t % 4}"), 16 * (t // 4) + 16)
                if t:
                    act.wait_ge(sem("x_sumsq"), t)
                act.activation(SQ[0:L, 0:D], XT[0:L, t % 4, :], ACT.Square, accum_out=TV[0:L, 0, t:t + 1])\
                    .then_inc(sem("x_sumsq"), 1)
                act.wait_ge(sem("x_turned"), t + 1)
                act.activation(X[:, 0:4, c], PS[:, 2 * (t % 2), 0:4 * L].rearrange("p (b t) -> p b t", b=4), ACT.Copy)\
                    .then_inc(sem("x_cp_a"), 1)

            def x_hi(t):
                c, L = tile(t)
                act.wait_ge(sem("x_scaled"), t + 1)
                act.activation(XH[:, :, c], XG[:, t % 2, :, 0:L], ACT.Copy).then_inc(sem("x_hi0"), 1)

            for t in range(NCH + 1):
                if t < NCH:
                    x_tile(t)
                if t >= 1:
                    x_hi(t - 1)
                if t == WEIGHTS_AT:
                    weights_hi()
            take_rms("n0")

            def store(s, dst, src, name="stg"):
                act.dma_start(dst, src).then_inc(sem(f"{name}{s}"), 16)


            def stored_unit(i, s, n3, dst, sigmoid=False):
                act.wait_ge(bank_free, n3 + (RING + 3))
                if sigmoid:
                    act.activation(STG[:, s, :], STG[:, s, :], ACT.Sigmoid).then_inc(sem("o_sig"), 1)
                    act.wait_ge(sem("o_sig"), 2 * i + (s - 15))
                store(s, dst, STG[:, s, :])
                split_hi(s, i + 1, n3 + 3)

            split_hi(1, 0, None)
            stored_unit(0, 0, 0, proj_s[0])
            m_, tmp = rows[0:H, R_M, :], rows[0:H, R_EM, :]
            act.wait_ge(sem("g_abs"), 1)
            act.activation(tmp, tmp, ACT.Exp, scale=-1.0).then_inc(sem("g_exp"), 1)
            act.wait_ge(sem("g_one"), 1)
            act.activation(tmp, tmp, ACT.Ln).then_inc(sem("g_exp"), 1)
            stored_unit(0, 1, 3, proj_s[1])
            act.wait_ge(sem("g_m"), 1)
            act.activation(tmp, m_, ACT.Exp, scale=-1.0).then_inc(sem("g_fin"), 1)
            act.wait_ge(sem("g_inter"), 1)
            act.activation(rows[0:H, R_INTER, :], rows[0:H, R_INTER, :], ACT.Exp).then_inc(sem("g_fin"), 1)
            act.wait_ge(sem("g_fin"), 2)
            act.dma_start(gate_s.rearrange("r h t -> h r t"), rows[0:H, 0:2, :]).then_inc(sem("gate_st"), 16)
            act.dma_start(m_prompt[0].rearrange("b h -> h b"), rows[0:H, R_M, SEQ - 1:SEQ]).then_inc(sem("m_st"), 16)
            act.dma_start(m_sample[0].rearrange("b h -> h b"), rows[0:H, R_M, T - 1:T]).then_inc(sem("m_st"), 16)
            act.wait_ge(sem("cs_zero"), 1)
            sc_, sn_ = state_c[0, 0], state_n[0, 0]
            for a in range(2):
                r = slice(64 * a, 64 * a + 64)
                act.dma_start(CS[r, :, a, 0:DV], sc_.rearrange("(q a) d e -> a d q e", a=2)[a]).then_inc(sem("cs_in"), 16)
                with nc.allow_non_contiguous_dma(reason="one normaliser column"):
                    act.dma_start(CS[r, :, a, DV:DV + 1], sn_.rearrange("(q a) (d o) -> a d q o", a=2, o=1)[a])\
                        .then_inc(sem("cs_in"), 16)
            with act.Fori(1, 8) as i:
                for s in range(2):
                    stored_unit(i, s, 6 * i + 3 * s, proj_s[2 * i + s])

            def load_qkv(C):
                act.dma_start(CH[:, C.par, :, C.f], proj_s[0:16, :, C.cols].rearrange("b p t -> p b t"))\
                    .then_inc(sem(f"ch_in{C.par}"), 16)

            def load_exponents(C):
                act.dma_start(DT[:, :, C.f], gate_s[0][:, C.cols].unsqueeze(0).to_broadcast([P, H, C.L]))\
                    .then_inc(sem("dt_in"), 16)

            def load_inter(C):
                for a in range(2):
                    act.dma_start(QI[64 * a:64 * a + 64, :, C.f],
                                  gate_s[1].rearrange("(p a) t -> a p t", a=2)[a][:, C.cols].unsqueeze(0)
                                  .to_broadcast([64, NPAIR, C.L])).then_inc(sem("qi_in"), 16)

            def load_rows(C):
                act.dma_start(RC[:, :, C.f], rows[0:H, 2:4, C.cols]).then_inc(sem("rc_in"), 16)

            act.wait_ge(sem("stg0"), 16 * 8)
            act.wait_ge(sem("stg1"), 16 * 8)
            act.wait_ge(sem("gate_st"), 16)
            load_qkv(Chunk(0, 0))
            load_exponents(Chunk(0, 0))
            load_inter(Chunk(0, 0))
            load_rows(Chunk(0, 0))
            load_qkv(Chunk(0, 1))
            stored_unit(8, 0, 48, proj_s[16], True)

            def chunk_in(C):
                act.wait_ge(sem("c_turned"), C.n + 1)
                act.activation(KN[C.f, :], PS[C.f, 6, :], ACT.Copy, scale=K_SCALE).then_inc(sem("c_kn"), 1)
                act.activation(VC[C.f, 0:4, 0:DV], PS[C.f, 0, :].rearrange("p (h e) -> p h e", h=4), ACT.Copy)\
                    .then_inc(sem("c_vc"), 1)
                act.wait_ge(sem("c_cols"), C.n + 1)
                act.wait_ge(sem("c_masked"), C.n + 1)
                for h in range(H):
                    act.activation(DT[C.f, h, C.f], DT[C.f, h, C.f], ACT.Exp, bias=MS[C.f, C.par, 0, h:h + 1])\
                        .then_inc(sem("c_dt"), 1)

            def chunk_out(C):
                act.wait_ge(sem("c_num"), C.n + 1)
                act.wait_ge(sem("c_hT"), C.n + 1)
                for b in range(2):
                    act.activation(HN[C.f, 4 * b:4 * b + 4, :], PS[C.f, b, :].rearrange("p (h e) -> p h e", h=4), ACT.Copy)\
                        .then_inc(sem("c_hn"), 1)
                act.wait_ge(sem("c_hn"), 2 * C.n + 4)
                act.activation(SN[C.f, :, :], HN[C.f, :, :], ACT.Square).then_inc(sem("c_sn"), 1)

            def step(C, N, N2, filled):
                act.wait_ge(sem("c_kw"), C.n + 1)
                load_exponents(N)
                if N2 is not None:
                    act.wait_ge(sem("c_scores"), C.n + 1)
                    act.wait_ge(sem("c_qi"), C.n + 1)
                    load_qkv(N2)
                chunk_out(C)
                load_inter(N)
                chunk_in(N)
                if N2 is not None:
                    load_rows(N2)
                if filled:
                    stored_unit(C.half + (8 + C.par), (C.par + 1) % 2, 3 * C.n + 3 * FILL0, proj_s[C.n + 17], True)

            act.sem_inc(sem("c_hn"), 2)
            chunk_in(Chunk(0, 0))
            load_rows(Chunk(0, 1))
            with act.Fori(0, NT // 2 - 1) as i:
                for m in range(2):
                    step(Chunk(i, m), Chunk(i, m + 1), Chunk(i, m + 2), True)
            step(Chunk(NT // 2 - 1, 0), Chunk(NT // 2 - 1, 1), Chunk(NT // 2, 0), True)
            step(Chunk(NT // 2 - 1, 1), Chunk(NT // 2, 0), None, False)

            def state_out(S, c_o, n_o):
                for a in range(2):
                    r = slice(64 * a, 64 * a + 64)
                    act.dma_start(c_o.rearrange("(q a) d e -> a d q e", a=2)[a], S[r, :, a, 0:DV]).then_inc(sem("st_out"), 16)
                    with nc.allow_non_contiguous_dma(reason="one normaliser column"):
                        act.dma_start(n_o.rearrange("(q a) (d o) -> a d q o", a=2, o=1)[a], S[r, :, a, DV:DV + 1])\
                            .then_inc(sem("st_out"), 16)

            def load_o(k):
                act.dma_start(OG[:, k % 4, :], proj_s[16 + k]).then_inc(sem(f"og_in{k % 4}"), 16)

            act.wait_ge(sem("c_qi"), NT + 1)
            act.wait_ge(sem("c_scores"), NT + 1)
            act.wait_ge(sem("stg0"), 16 * 12)
            act.wait_ge(sem("stg1"), 16 * 12)
            for k in range(4):
                load_o(k)
            chunk_out(Chunk(NT // 2, 0))
            act.wait_ge(sem("c_upd"), 5 * NT + 5)
            state_out(CB, c_prompt[0, 0], n_prompt[0, 0])
            for k in range(KB):
                act.wait_ge(sem("h_gated"), k + 1)
                act.activation(XH[:, k, :], Y[:, k, :], ACT.Copy).then_inc(sem("x_hi"), 1)
                if k < 4:
                    load_o(k + 4)
            act.wait_ge(sem("c_upd"), 5 * NT + 10)
            state_out(CS, c_sample[0, 0], n_sample[0, 0])

            def dense_hi(g0, u0):
                def one(i, s, ahead=True):
                    if ahead:
                        split_hi(1 - s, i + (u0 // 2 + s), 6 * i + (g0 + 3 * s))
                    for g in range(NG):
                        act.wait_ge(bank_free, RING + 6 * i + (g0 + 3 * s + g + 1))
                        square(Y[:, 2 * i + s, grp(g)], s, g)
                one(0, 0, False)
                one(0, 1)
                with act.Fori(1, KB // 2) as i:
                    for s in range(2):
                        one(i, s)

            dense_hi(G_OUT, U_OUT)
            act.wait_ge(sem("st_out"), 128)
            act.wait_ge(sem("m_st"), 32)

            def boundary(name, pre, u0, g0):
                if pre:
                    split_hi(1, u0 // 2, g0)
                take_rms(name + "y")
                if pre:
                    for k in range(KB):
                        act.wait_ge(sem("x_new"), KB * BOUNDS[name] + k + 1)
                        act.activation(XH[:, k, :], X[:, k, :], ACT.Copy, scale=gcol(pre, k)).then_inc(sem("x_hi"), 1)
                        if k >= 2:
                            act.wait_ge(sem("sq_sum"), SUMS[name + "y"] + k - 1)
                        act.activation(SQ[:, :] if k == 0 else STG[:, k % 2, :], X[:, k, :], ACT.Square)\
                            .then_inc(sem("squared_x"), 1)
                    if name in RAW_PAIR:
                        split_hi(0, u0 // 2 + 1, g0 + 3)
                        split_hi(1, u0 // 2 + 1, g0 + 6)
                    take_rms(name + "x")

            def mlp(l, u0, g0):
                def group(j, first=False, last=False):
                    for m in range(4):
                        if not (first and m < 3):
                            split_hi((m + 1) % 2, 4 * j + (u0 // 2 + (m + 1) // 2), 36 * j + (g0 + 3 * m))
                        for g in range(NG):
                            n = 3 * m + g
                            if first and m < 2:
                                act.wait_ge(sem("raw_scaled"), 6 * l + n + 1)
                            else:
                                act.wait_ge(bank_free, RING + 36 * j + (g0 + n + 1))
                            act.activation(HH[:, m, grp(g)], MT[:, n % 2, :], ACT.Square).then_inc(sem("h_hi"), 1)
                    for d in range(4):
                        if not (last and l == 1 and d == 3):
                            split_hi((d + 1) % 2, 4 * j + (u0 // 2 + (d + 5) // 2), 36 * j + (g0 + 12 + 6 * d))
                        for b in range(2 if last else 0):
                            for g in range(NG):
                                act.wait_ge(bank_free, RING + 36 * j + (g0 + 12 + 6 * d + 3 * b + g + 1))
                                square(Y[:, 2 * d + b, grp(g)], b, g)
                group(0, first=True)
                with act.Fori(1, FFG - 1) as j:
                    group(j)
                group(FFG - 1, last=True)

            boundary("b0", "ffn_pre0", U_MLP0, G_MLP0)
            mlp(0, U_MLP0, G_MLP0)
            boundary("b1", "kv", U_KV, G_KV)

            kp = k_prompt[0].rearrange("(t p) h a d -> h p t (a d)", p=P)
            ks = k_sample[0].rearrange("t h a d -> h t (a d)")
            vp = v_prompt[0].rearrange("(t p) h d -> h p t d", p=P)
            vs = v_sample[0].rearrange("t h d -> h t d")

            def kv_unit(i, s, h, dp, ds_, keys, behind_split=None):
                act.wait_ge(bank_free, RING + 6 * i + (G_KV + 3 * s + 3))
                if keys:
                    store(s, kT_s[h], STG[:, s, :], "kt_st")
                split_hi(s, i + (U_KV // 2 + 1), 6 * i + (G_KV + 3 * s + 3))
                if behind_split is not None:
                    behind_split()
                act.wait_ge(sem(f"kv_st{s}"), 32 * i)
                for b in range(2):
                    act.wait_ge(sem("kv_turned"), 6 * i + (3 * s + b + 1))
                    act.activation(OT[:, s, 4 * b:4 * b + 4, :], PS[:, 6 + b, :].rearrange("p (t c) -> p t c", t=4),
                                   ACT.Copy).then_inc(sem("kv_rows"), 1)
                act.wait_ge(sem("kv_turned"), 6 * i + (3 * s + 3))
                act.activation(OT[0:DEC, s, NT, :], PS[0:DEC, 6, 0:P], ACT.Copy).then_inc(sem("kv_rows"), 1)
                act.wait_ge(sem("kv_rows"), 6 * i + (3 * s + 3))
                store(s, dp[h], OT[:, s, 0:NT, :], "kv_st")
                store(s, ds_[h], OT[0:DEC, s, NT, :], "kv_st")

            kv_unit(0, 0, 0, kp, ks, True)
            kv_unit(0, 1, 1, kp, ks, True)
            with act.Fori(1, 4) as i:
                for s in range(2):
                    kv_unit(i, s, 2 * i + s, kp, ks, True)
            with act.Fori(4, 7) as i:
                for s in range(2):
                    kv_unit(i, s, 2 * i + (s - 8), vp, vs, False)

            def queries_in(blocks):
                for k in blocks:
                    act.activation(XH[:, k, :], X[:, k, :], ACT.Copy, scale=gcol("mix_pre1", k)).then_inc(sem("x_hi"), 1)
            kv_unit(7, 0, 6, vp, vs, False)
            kv_unit(7, 1, 7, vp, vs, False, lambda: queries_in(range(2)))
            queries_in(range(2, KB))

            for s in range(2):
                act.wait_ge(sem(f"kt_st{s}"), 16 * 4)
                act.wait_ge(sem(f"kv_st{s}"), 32 * 8)
            for a in range(2):
                act.activation(lam[:, 2 + a:3 + a], lam[:, a:a + 1], ACT.Exp).then_inc(sem("lam_exp"), 1)
            ck = cache_k[0].rearrange("(t p) h a d -> h p t (a d)", p=P)
            cv = cache_v[0].rearrange("(t p) h d -> h p t d", p=P)

            def load_k(h):
                act.dma_start(KR, kT_s[h]).then_inc(sem("k_in"), 16)

            def load_ck(h):
                act.dma_start(CK[:, :, :], ck[h]).then_inc(sem("ck_in"), 16)

            def load_v(h):
                act.dma_start(VR[:, 0:NT, :], vp[h]).then_inc(sem("v_in"), 16)
                act.dma_start(VR[:, NT:NT + 4, :], cv[h]).then_inc(sem("vc_in"), 16)
                act.dma_start(VR[0:DEC, NT + 4, :], vs[h]).then_inc(sem("vs_in"), 16)

            def split_k(h1, a_scores):
                act.wait_ge(sem("k_in"), 16 * h1)
                if a_scores is not None:
                    act.wait_ge(sem("a_scores"), a_scores)
                act.activation(KH[:, 0:SEQ], KR[:, 0:SEQ], ACT.Copy).then_inc(sem("k_hi"), 1)

            def split_q(h, s, g):
                act.wait_ge(bank_free, 3 * h + (RING + G_Q + g + 1))
                act.activation(QH[:, s, grp(g)], QR[:, grp(g)], ACT.Copy).then_inc(sem("q_hi"), 1)

            def att_extras(q, t, first, last):
                h, more = t.h, not (last and t.hp == 1)
                if t.i == 0:
                    act.wait_ge(sem("a_ckT"), h + 1)
                    act.wait_ge(sem("a_scores"), 2 * t.n)
                    act.activation(KH[:, SCOL:NKEY], KR[:, SEQ:T], ACT.Copy)
                    act.activation(KH[:, SEQ:SCOL], PS[:, 7, :], ACT.Copy).then_inc(sem("kc_hi"), 1)
                    split_hi(t.hp, q + (U_Q // 2 + 1), 6 * q + (G_Q + 3 * (t.hp + 1)))
                if t.i == 1:
                    act.wait_ge(sem("v_in"), 16 * h + 16)
                    if not (first and t.hp == 0):
                        act.wait_ge(sem("a_out"), t.n - 2)
                    act.activation(VH[:, 0:NT, :], VR[:, 0:NT, :], ACT.Copy).then_inc(sem("v_hi"), 1)
                if t.i == 2 and more:
                    act.wait_ge(sem("kc_lo"), h + 1)
                    load_k(h + 1)
                    load_ck(h + 1)
                if t.i == 3:
                    act.wait_ge(sem("vc_in"), 16 * h + 16)
                    act.wait_ge(sem("vs_in"), 16 * h + 16)
                    if not (first and t.hp == 0):
                        act.wait_ge(sem("a_out"), t.n - 3)
                    act.activation(VH[:, NT:NT + 4, :], VR[:, NT:NT + 4, :], ACT.Copy)
                    act.activation(VH[0:DEC, NT + 4, :], VR[0:DEC, NT + 4, :], ACT.Copy).then_inc(sem("vc_hi"), 1)
                if t.i == 5 and more:
                    act.wait_ge(sem("v_lo"), h + 1)
                    act.wait_ge(sem("vc_lo"), h + 1)
                    load_v(h + 1)
                if t.i == 8 and more:
                    split_k(h + 2, 2 * t.n)
                if t.i in SPLIT and more:
                    split_q(h + 1, (t.hp + 1) % 2, SPLIT.index(t.i))
                if not more:
                    if 1 <= t.i < H:
                        k = t.i - 1
                        act.wait_ge(sem(f"o_in{k % 2}"), 16 * (k // 2 + 1))
                        act.activation(XH[:, k, :], STG[:, k % 2, :], ACT.Copy, scale=gcol("sub", k))\
                            .then_inc(sem("x_hi"), 1)
                    if t.i < H - 1:
                        k = t.i
                        act.wait_ge(sem("q_lo"), NG * H)
                        act.wait_ge(sem("kc_lo"), H)
                        act.wait_ge(sem("o_st"), 32 * (k + 1))
                        if k >= 2:
                            act.wait_ge(sem("x_lo"), KB * SPLITS["wo"] + k - 1)
                        act.dma_start(STG[:, k % 2, :], o_s[k]).then_inc(sem(f"o_in{k % 2}"), 16)

            def att_sumsq(t):
                act.wait_ge(sem("a_oc"), t.n + 1)
                act.activation(ON[t.f, t.par, :], OC[t.f, t.par, :], ACT.Square, scale=t.number(6), accum_out=t.number(8))\
                    .then_inc(sem("a_ss"), 1)

            def att_exp(t, m, first):
                act.wait_ge(sem("a_max"), 2 * t.n + (m + 1))
                if m == 0 and not (first and t.n < 2):
                    act.wait_ge(sem("a_turned"), t.n - 1)
                if m == 1:
                    act.wait_ge(sem("a_comb"), t.n)
                dst = P0[t.f, t.par, 0:t.keys] if m == 0 else P1[t.f, 0:t.keys]
                act.activation(dst, t.score(m), ACT.Exp, bias=t.number(m),
                               accum_out=t.number(4 + m)).then_inc(sem("a_exp"), 1)

            def att_take_out(t, first, last):
                if t.i == 0 and not (first and t.hp == 0):
                    act.wait_ge(sem("o_st"), 32 * t.h)
                act.wait_ge(sem("a_oT"), t.n + 1)
                act.activation(OTS[:, t.q0:t.q0 + t.L], PS[:, 6, P:P + t.L], ACT.Copy)\
                    .then_inc(sem("a_otc"), 1)
                if t.i in (NT - 1, NT) and not (last and t.hp == 1):
                    act.wait_ge(sem("a_otc"), t.n + 1)
                    c = slice(0, SEQ) if t.i == NT - 1 else slice(SEQ, T)
                    act.dma_start(o_s[t.h][:, c], OTS[:, c]).then_inc(sem("o_st"), 16)

            def att_turned_hi(t, first):
                act.wait_ge(sem("a_turned"), t.n + 1)
                if not (first and t.n < 2):
                    act.wait_ge(sem("a_out"), t.n - 1)
                for src, dst in t.turned(TH):
                    ins = act.activation(dst, src, ACT.Copy)
                ins.then_inc(sem("a_thi"), 1)

            load_k(0)
            load_ck(0)
            load_v(0)
            split_k(1, None)
            for g in range(NG):
                split_q(0, 0, g)

            def att_turn_of_loop(q, first=False, last=False):
                for m in range(TPT + (4 if last else 0)):
                    t = Tile(q, m)
                    if m < TPT:
                        att_exp(t, 0, first)
                    if not (first and m < 4):
                        att_take_out(Tile(q, m - 4), first, last and m >= 4)
                    if m - 1 < TPT and not (first and m < 1):
                        att_turned_hi(Tile(q, m - 1), first)
                    if m < TPT:
                        att_exp(t, 1, first)
                    if m - 3 < TPT and not (first and m < 3):
                        att_sumsq(Tile(q, m - 3))
                    if m < TPT:
                        att_extras(q, t, first, last)

            att_turn_of_loop(0, first=True)
            with act.Fori(1, NPAIR - 1) as q:
                att_turn_of_loop(q)
            att_turn_of_loop(NPAIR - 1, last=True)

            act.wait_ge(sem("a_otc"), TPT * NPAIR)
            act.activation(XH[:, KB - 1, :], OTS, ACT.Copy, scale=gcol("sub", KB - 1)).then_inc(sem("x_hi"), 1)
            dense_hi(G_WO, U_WO)
            boundary("b2", "ffn_pre1", U_MLP1, G_MLP1)
            mlp(1, U_MLP1, G_MLP1)
            boundary("b3", None, None, None)

            for t in range(NCH):
                act.wait_ge(sem("y_turned"), t + 1)
                act.activation(y_half(t, 0), PS[0:P if t < NT else DEC, 2 * (t % 4), :], ACT.Copy).then_inc(sem("y_out_a"), 1)

        @block.vector
        def _(dve):
            mm_done, bank_free, w_hi, w_lo = sem("mm_done"), sem("bank_free"), sem("w_hi"), sem("w_lo")

            def split_lo(s, u1):
                dve.wait_ge(w_hi, u1)
                dve.tensor_tensor(WL[:, s, :], WR[:, s, :], WH[:, s, :].bitcast(F32), ALU.subtract).then_inc(w_lo, 1)

            def add_square(s, g, n):
                dve.wait_ge(sem("squared"), n)
                dve.tensor_tensor(SQ[:, grp(g)], SQ[:, grp(g)], STG[:, s, grp(g)], ALU.add).then_inc(sem("sq_sum"), 1)

            def token_rms(name):
                n = NORMS[name]
                if name != "n0":
                    dve.wait_ge(sem("tok_sum"), n)
                    dve.tensor_copy(TV[:, 0, 0:NT], PS[:, 7, 0:NT])
                    dve.tensor_copy(TV[0:DEC, 0, NT:NCH], PS[0:DEC, 7, NT:NCH]).then_inc(sem("tok_var"), 1)
                else:
                    dve.wait_ge(sem("x_sumsq"), NCH)
                    dve.sem_inc(sem("tok_var"), 1)
                dve.wait_ge(sem("tok_var"), 2 * n + 1)
                dve.tensor_scalar(TV[:, 1, :], TV[:, 0, :], 1.0 / D, EPS, ALU.mult, ALU.add).then_inc(sem("tok_var"), 1)

            def x_lo(k, gain, name):
                dve.wait_ge(sem("x_hi"), KB * SPLITS[name] + k + 1)
                if gain is None:
                    dve.tensor_tensor(XL[:, k, :], Y[:, k, :], XH[:, k, :].bitcast(F32), ALU.subtract)\
                        .then_inc(sem("x_lo"), 1)
                    return
                src = X[:, k, :] if name != "wo" else STG[:, k % 2, :] if k < KB - 1 else OTS
                dve.scalar_tensor_tensor(XL[:, k, :], src, gcol(gain, k), XH[:, k, :].bitcast(F32),
                                         ALU.mult, ALU.subtract).then_inc(sem("x_lo"), 1)

            dve.memset(TV[:, :, :], 1.0)
            dve.memset(half[:, :], -0.5)
            dve.memset(mean_eps[:, 0:1], 1.0 / P)
            dve.memset(mean_eps[:, 1:2], EPS)
            dve.memset(ones[:, :], 1.0)
            dve.sem_inc(bank_free, RING)
            dve.sem_inc(sem("x_cp_d"), 2)
            barrier(dve, PH["load"])
            dve.wait_ge(sem("gains"), 1)
            dve.tensor_scalar(GN[:, 80:88], GN[:, 80:88], 1.0 - LAM_INIT, None, ALU.mult)
            def weights_lo():
                split_lo(0, 1)
                dve.wait_ge(sem("wg_zero"), 2)
                dve.wait_ge(sem("wg_hi"), 2)
                dve.tensor_tensor(WGL[:, :, 0:8], WG[:, :, 0:8], WGH[:, :, 0:8].bitcast(F32), ALU.subtract)
                dve.tensor_tensor(WGL[:, :, 32:40], WG[:, :, 8:16], WGH[:, :, 32:40].bitcast(F32), ALU.subtract)\
                    .then_inc(sem("wg_lo"), 1)

            def x_tile(t):
                c, L = (slice(t * P, t * P + P), P) if t < NT else (slice(SEQ, T), DEC)
                dve.wait_ge(sem("x_turned"), t + 1)
                dve.tensor_copy(X[:, 4:8, c], PS[:, 2 * (t % 2) + 1, 0:4 * L].rearrange("p (b t) -> p b t", b=4))\
                    .then_inc(sem("x_cp_d"), 1)
                dve.wait_ge(sem("x_cp_d"), t + 3)
                dve.wait_ge(sem("x_cp_a"), t + 3)
                g0 = GAINS.index("mix_pre0") * KB
                dve.tensor_tensor(XG[:, t % 2, :, 0:L], X[:, :, c], GN[:, g0:g0 + KB].unsqueeze(2).to_broadcast([P, KB, L]),
                                  ALU.mult).then_inc(sem("x_scaled"), 1)

            def x_lo0(t):
                c, L = (slice(t * P, t * P + P), P) if t < NT else (slice(SEQ, T), DEC)
                dve.wait_ge(sem("x_hi0"), t + 1)
                dve.tensor_tensor(XL[:, :, c], XG[:, t % 2, :, 0:L], XH[:, :, c].bitcast(F32), ALU.subtract)\
                    .then_inc(sem("x_lo0"), 1)

            for t in range(NCH + 1):
                if t < NCH:
                    x_tile(t)
                if t >= 1:
                    x_lo0(t - 1)
                if t == WEIGHTS_AT:
                    weights_lo()
            token_rms("n0")
            link = [0]

            def ln(ins):
                link[0] += 1
                ins.then_inc(sem("lam"), 1)
                dve.wait_ge(sem("lam"), link[0])
            dve.wait_ge(sem("consts"), 16 * 7)
            ln(dve.tensor_tensor(lam_in[:, 0, :], lam_in[:, 0, :], lam_in[:, 1, :], ALU.mult))
            ln(dve.tensor_tensor(lam_in[:, 2, :], lam_in[:, 2, :], lam_in[:, 3, :], ALU.mult))
            ln(dve.reduce_sum(lam[:, 0:1], lam_in[:, 0, :], AX))
            ln(dve.reduce_sum(lam[:, 1:2], lam_in[:, 2, :], AX))

            dve.wait_ge(sem("rst"), 1)
            dve.wait_ge(sem("rb"), 3)
            for g in range(NG):
                dve.wait_ge(sem("gates_mm"), g + 1)
                dve.tensor_tensor(rows[0:H, R_LI, grp(g)], PS[0:H, 5 - g, 0:G], RB[0:H, grp(g)], ALU.mult)\
                    .then_inc(sem("gates_read"), 1)
                dve.tensor_tensor(rows[0:H, R_LF, grp(g)], PS[32:40, 5 - g, 0:G], RB[0:H, grp(g)], ALU.mult)\
                    .then_inc(sem("gates_read"), 1)

            def take(s, g, n):
                dve.wait_ge(mm_done, n)
                dve.tensor_tensor(STG[:, s, grp(g)], PS[:, 3 * s + g, 0:G], RB[:, grp(g)], ALU.mult)\
                    .then_inc(bank_free, 1)

            def proj_unit(i, s, n3, stored):
                if stored is not None:
                    dve.wait_ge(sem(f"stg{s}"), stored)
                for g in range(NG):
                    take(s, g, n3 + (g + 1))
                split_lo(s, 2 * i + (s + 3))

            split_lo(1, 2)
            proj_unit(0, 0, 0, None)
            row = lambda r: rows[0:H, r, :]
            li, lf, m_, fc, u_, gg, tmp = (row(r) for r in (R_LI, R_LF, R_M, R_FC, R_U, R_G, R_EM))
            glink = [0]

            def gl(ins):
                glink[0] += 1
                ins.then_inc(sem("g_dve"), 1)
                dve.wait_ge(sem("g_dve"), glink[0])
            gl(dve.tensor_scalar(li, li, bg[:, 0:1], None, ALU.add))
            gl(dve.tensor_scalar(lf, lf, bg[:, 1:2], None, ALU.add))
            gl(dve.tensor_scalar(gg, lf, -1.0, None, ALU.mult))
            dve.tensor_tensor(tmp, lf, gg, ALU.max).then_inc(sem("g_abs"), 1)
            dve.wait_ge(sem("g_exp"), 1)
            dve.tensor_scalar(tmp, tmp, 1.0, None, ALU.add).then_inc(sem("g_one"), 1)
            gl(dve.tensor_scalar(lf, lf, 0.0, None, ALU.min))
            proj_unit(0, 1, 3, None)
            dve.wait_ge(sem("g_exp"), 2)
            gl(dve.tensor_tensor(lf, lf, tmp, ALU.subtract))
            gl(dve.tensor_tensor_scan(fc, RST[:, :], lf, 0.0, ALU.mult, ALU.add))
            gl(dve.tensor_tensor_scan(rows[0:H, R_M, 0:SEQ], rows[0:H, R_LF, 0:SEQ], rows[0:H, R_LI, 0:SEQ], 0.0,
                                      ALU.add, ALU.max))
            dve.tensor_tensor_scan(rows[0:H, R_M, SEQ:T], rows[0:H, R_LF, SEQ:T], rows[0:H, R_LI, SEQ:T], bg[:, 2:3],
                                   ALU.add, ALU.max).then_inc(sem("g_m"), 1)
            dve.wait_ge(sem("g_m"), 1)
            gl(dve.memset(MP[:, 0:1], 0.0))
            gl(dve.tensor_copy(MP[:, 1:NT], rows[0:H, R_M, LC - 1:SEQ - LC:LC]))
            gl(dve.tensor_copy(MP[:, NT:NCH], bg[:, 2:3]))
            gl(dve.tensor_tensor(gg, li, fc, ALU.subtract))
            gl(dve.tensor_tensor(u_, fc, m_, ALU.subtract))
            dve.tensor_tensor(rows[0:H, R_INTER, 0:SEQ].rearrange("h (c t) -> h c t", c=NT),
                              rows[0:H, R_U, 0:SEQ].rearrange("h (c t) -> h c t", c=NT),
                              MP[:, 0:NT].unsqueeze(2).to_broadcast([H, NT, LC]), ALU.add)
            dve.tensor_scalar(rows[0:H, R_INTER, SEQ:T], rows[0:H, R_U, SEQ:T], MP[:, NT:NCH], None, ALU.add)\
                .then_inc(sem("g_inter"), 1)
            dve.memset(CS[:, :, :, :], 0.0).then_inc(sem("cs_zero"), 1)
            dve.memset(CB[:, :, :, :], 0.0).then_inc(sem("c_upd"), 5)
            dve.memset(VC[:, :, DV:DV + 1], 1.0)
            dve.sem_inc(sem("c_qn"), 1)
            dve.sem_inc(sem("c_y"), 2)
            with dve.Fori(1, 8) as i:
                for s in range(2):
                    proj_unit(i, s, 6 * i + 3 * s, 16 * i)
            proj_unit(8, 0, 48, 16 * 8)

            def masked(C):
                dve.wait_ge(sem("dt_in"), 16 * C.n + 16)
                dve.wait_ge(sem("sel"), 2)
                dve.tensor_tensor(DT[C.f, :, C.f], DT[C.f, :, C.f], mask[C.f, C.f].unsqueeze(1).to_broadcast([C.L, H, C.L]),
                                  ALU.add).then_inc(sem("c_masked"), 1)

            def inter(C):
                dve.wait_ge(sem("qi_in"), 32 * C.n + 32)
                dve.wait_ge(sem(f"ch_in{C.par}"), 16 * C.half + 16)
                dve.tensor_copy(DEC4[:, :], QI[:, :, C.L - 1]).then_inc(sem("c_dec"), 1)
                dve.wait_ge(sem("c_dec"), C.n + 1)
                dve.tensor_tensor(QI[:, :, C.f], CH[:, C.par, 0:4, C.f], QI[:, :, C.f], ALU.mult).then_inc(sem("c_qi"), 1)

            def chunk_in(C):
                dve.wait_ge(sem("c_turned"), C.n + 1)
                dve.tensor_copy(MS[C.f, C.par, 0:2, :], PS[C.f, 2, 0:2 * H].rearrange("p (r h) -> p r h", r=2))\
                    .then_inc(sem("c_cols"), 1)
                dve.tensor_copy(VC[C.f, 4:8, 0:DV], PS[C.f, 1, :].rearrange("p (h e) -> p h e", h=4))\
                    .then_inc(sem("c_vc2"), 1)

            def weighted(C):
                dve.wait_ge(sem("c_scores"), C.n + 1)
                dve.wait_ge(sem("c_dt"), 8 * C.n + 8)
                for a in range(2):
                    dve.scalar_tensor_tensor(SD[C.f, a:H:2, C.f], PS[C.f, 3 + a, 0:4 * C.L].rearrange("p (h t) -> p h t", h=4),
                                             K_SCALE, DT[C.f, a:H:2, C.f], ALU.mult, ALU.mult).then_inc(sem("c_sd"), 1)
                dve.wait_ge(sem("c_kn"), C.n + 1)
                k3 = KN[C.f, :].rearrange("p (h d) -> p h d", h=H)
                dve.tensor_tensor(k3, k3, DT[C.f, :, C.L - 1:C.L].to_broadcast([C.L, H, DK]), ALU.mult)\
                    .then_inc(sem("c_kw"), 1)

            def cl(C, k, ins):
                ins.then_inc(sem("c_den"), 1)
                dve.wait_ge(sem("c_den"), 8 * C.n + k)

            def denominator(C):
                dve.wait_ge(sem("c_num"), C.n + 1)
                dve.tensor_copy(C.number(2), PS[C.f, 2, 0:H]).then_inc(sem("c_qn"), 1)
                dve.wait_ge(sem("c_qn"), C.n + 2)
                cl(C, 1, dve.scalar_tensor_tensor(C.number(4), C.number(2), -1.0, C.number(2), ALU.mult, ALU.max))
                cl(C, 2, dve.tensor_tensor(C.number(4), C.number(4), C.number(1), ALU.max))
                cl(C, 3, dve.reciprocal(C.number(3), C.number(4)))

            def update(C):
                S, u0 = C.state, 5 * C.n + 5
                s3 = S[:, :, :, :].rearrange("p q a b -> p q (a b)")
                dve.tensor_tensor(s3, s3, DEC4[:, :].unsqueeze(2).to_broadcast([P, NPAIR, 2 * (DV + 1)]), ALU.mult)\
                    .then_inc(sem("c_upd"), 1)
                dve.wait_ge(sem("c_kv"), C.n + 1)
                dve.wait_ge(sem("c_upd"), u0 + 1)
                for a in range(2):
                    r = slice(64 * a, 64 * a + 64)
                    out = S[r, :, a, 0:DV].rearrange("p (b q) e -> p b q e", b=2)
                    new = PS[r, 3:5, :].rearrange("p b (q x e) -> p b q x e", q=2, x=2)[:, :, :, a, :]
                    dve.tensor_tensor(out, out, new, ALU.add).then_inc(sem("c_upd"), 1)
                    dve.tensor_tensor(S[r, :, a, DV], S[r, :, a, DV], PS[r, 5, 0:NPAIR], ALU.add).then_inc(sem("c_upd"), 1)

            def variance(C):
                dve.wait_ge(sem("c_sn"), C.n + 1)
                cl(C, 4, dve.reduce_sum(C.number(4), SN[C.f, :, :], AX))
                cl(C, 5, dve.tensor_tensor(C.number(5), C.number(3), C.number(3), ALU.mult))
                cl(C, 6, dve.tensor_tensor(C.number(5), C.number(5), C.number(4), ALU.mult))
                cl(C, 7, dve.tensor_scalar(C.number(5), C.number(5), 1.0 / DV, EPS, ALU.mult, ALU.add))

            def normed(C):
                dve.wait_ge(sem("c_pow"), C.n + 1)
                cl(C, 8, dve.tensor_tensor(C.number(7), C.number(6), C.number(3), ALU.mult))
                dve.tensor_tensor(HN[C.f, :, :], HN[C.f, :, :], C.number(7).unsqueeze(2).to_broadcast([C.L, H, DV]),
                                  ALU.mult).then_inc(sem("c_hs"), 1)

            def output(C):
                dve.wait_ge(sem("c_hT"), C.n + 2)
                dve.tensor_copy(Y[:, :, C.cols].rearrange("p (b h) t -> p b h t", b=2),
                                PS[:, 5:7, 0:4 * C.L].rearrange("p b (h t) -> p b h t", h=4)).then_inc(sem("c_y"), 1)

            def take_o(C, g):
                s = (C.par + 1) % 2
                if g == 0:
                    dve.wait_ge(sem(f"stg{s}"), 16 * C.half + 16 * (8 + C.par))
                dve.wait_ge(mm_done, 3 * C.n + (3 * FILL0 + g + 1))
                dve.tensor_tensor(STG[:, s, grp(g)], PS[:, 7, 0:G], RB[:, grp(g)], ALU.mult).then_inc(bank_free, 1)

            def step(C, N, filled):
                denominator(C)
                update(C)
                masked(N)
                variance(C)
                if filled:
                    take_o(C, 0)
                chunk_in(N)
                inter(N)
                normed(C)
                if filled:
                    take_o(C, 1)
                weighted(N)
                output(C)
                if filled:
                    take_o(C, 2)
                    split_lo((C.par + 1) % 2, C.n + (FILL0 + 3))

            masked(Chunk(0, 0))
            inter(Chunk(0, 0))
            chunk_in(Chunk(0, 0))
            weighted(Chunk(0, 0))
            dve.wait_ge(sem("m_st"), 32)
            with dve.Fori(0, NT // 2 - 1) as i:
                for m in range(2):
                    step(Chunk(i, m), Chunk(i, m + 1), True)
            step(Chunk(NT // 2 - 1, 0), Chunk(NT // 2 - 1, 1), True)
            step(Chunk(NT // 2 - 1, 1), Chunk(NT // 2, 0), False)
            C = Chunk(NT // 2, 0)
            denominator(C)
            variance(C)
            normed(C)
            update(C)
            output(C)

            for k in range(KB):
                if k == 0:
                    dve.wait_ge(sem("c_y"), NCH + 2)
                dve.wait_ge(sem(f"og_in{k % 4}"), 16 * (k // 4 + 1))
                dve.scalar_tensor_tensor(Y[:, k, :], Y[:, k, :], gcol("h", k), OG[:, k % 4, :], ALU.mult, ALU.mult)\
                    .then_inc(sem("h_gated"), 1)
                if k:
                    x_lo(k - 1, None, "h")
            x_lo(KB - 1, None, "h")

            def dense_y(u0, g0, q0):
                dve.memset(SQ[:, :], 0.0)

                def one(i, s, ahead=True):
                    if ahead:
                        split_lo(1 - s, 2 * i + (u0 + s + 2))
                    for g in range(NG):
                        dve.wait_ge(mm_done, 6 * i + (g0 + 3 * s + g + 1))
                        dve.tensor_copy(Y[:, 2 * i + s, grp(g)], PS[:, 3 * s + g, 0:G]).then_inc(bank_free, 1)
                        if g:
                            add_square(s, g - 1, 6 * i + (q0 + 3 * s + g))
                    add_square(s, 2, 6 * i + (q0 + 3 * s + 3))
                one(0, 0, False)
                one(0, 1)
                with dve.Fori(1, KB // 2) as i:
                    for s in range(2):
                        one(i, s)

            dense_y(U_OUT, G_OUT, 0)

            def boundary(name, post, pre, u0=None, g0=None):
                if pre:
                    split_lo(1, u0 + 2)
                token_rms(name + "y")
                dve.wait_ge(sem("rb"), 3 * (NORMS[name + "y"] + 1))
                for k in range(KB):
                    if k < POOL_Y:
                        dve.tensor_tensor(Y[:, k, :], Y[:, k, :], RB[:, :], ALU.mult).then_inc(sem("y_scaled_d"), 1)
                        dve.wait_ge(sem("y_scaled_d"), POOL_Y * BOUNDS[name] + k + 1)
                    else:
                        dve.wait_ge(sem("y_scaled"), (KB - POOL_Y) * BOUNDS[name] + k - POOL_Y + 1)
                    dve.scalar_tensor_tensor(X[:, k, :], Y[:, k, :], gcol(post, k), X[:, k, :], ALU.mult, ALU.add)\
                        .then_inc(sem("x_new"), 1)
                    if pre and k >= 1:
                        x_lo(k - 1, pre, name)
                if pre:
                    x_lo(KB - 1, pre, name)
                    if name in RAW_PAIR:
                        for n in range(2 * NG):
                            dve.wait_ge(mm_done, g0 + n + 1)
                            dve.tensor_scalar(RAW[:, n // 3, grp(n % 3)], PS[:, n, 0:G], 0.0, None, ALU.max)\
                                .then_inc(bank_free, 1)
                        split_lo(0, u0 + 3)
                        split_lo(1, u0 + 4)
                    token_rms(name + "x")
                    dve.wait_ge(sem("rb"), 3 * (NORMS[name + "x"] + 1))

            def mlp(l, u0, g0):
                def group(j, first=False, last=False):
                    if last:
                        dve.memset(SQ[:, :], 0.0)
                    def low(n):
                        dve.wait_ge(sem("h_hi"), 12 * j + (96 * l + n + 1))
                        dve.wait_ge(sem("h_sq"), 12 * j + (96 * l + n + 1))
                        dve.tensor_tensor(HL[:, n // 3, grp(n % 3)], M2[:, n % 2, :],
                                          HH[:, n // 3, grp(n % 3)].bitcast(F32), ALU.subtract).then_inc(sem("h_lo"), 1)
                    for m in range(4):
                        if not (first and m < 3):
                            split_lo((m + 1) % 2, 8 * j + (u0 + m + 2))
                        for g in range(NG):
                            n = 3 * m + g
                            if first and m < 2:
                                dve.tensor_tensor(MT[:, n % 2, :], RAW[:, m, grp(g)], RB[:, grp(g)], ALU.mult)\
                                    .then_inc(sem("raw_scaled"), 1)
                                if n:
                                    low(n - 1)
                                continue
                            dve.wait_ge(mm_done, 36 * j + (g0 + n + 1))
                            dve.scalar_tensor_tensor(MT[:, n % 2, :], PS[:, 3 * (m % 2) + g, 0:G], 0.0, RB[:, grp(g)],
                                                     ALU.max, ALU.mult).then_inc(bank_free, 1)
                            if n:
                                low(n - 1)
                    low(11)
                    if first:
                        dve.wait_ge(sem("y_zero"), KB * (l + 1))
                    q0 = 24 + 48 * l + 1
                    for d in range(4):
                        if not (last and l == 1 and d == 3):
                            split_lo((d + 1) % 2, 8 * j + (u0 + d + 6))
                        for b in range(2):
                            for g in range(NG):
                                n = 12 + 6 * d + 3 * b + g
                                dve.wait_ge(mm_done, 36 * j + (g0 + n + 1))
                                y = Y[:, 2 * d + b, grp(g)]
                                dve.tensor_tensor(y, y, PS[:, 3 * b + g, 0:G], ALU.add).then_inc(bank_free, 1)
                                q = n - 12
                                if last and q:
                                    add_square((q - 1) // 3 % 2, (q - 1) % 3, q0 + q - 1)
                    if last:
                        add_square(1, 2, q0 + 23)
                group(0, first=True)
                with dve.Fori(1, FFG - 1) as j:
                    group(j)
                group(FFG - 1, last=True)

            boundary("b0", "mix_post0", "ffn_pre0", U_MLP0, G_MLP0)
            mlp(0, U_MLP0, G_MLP0)
            boundary("b1", "ffn_post0", "kv", U_KV)

            def kv_unit(i, s, stored, first=False):
                if not first:
                    dve.wait_ge(sem("kv_turned"), 6 * i + (3 * s - 3))
                dve.wait_ge(sem(f"kt_st{s}"), stored)
                for g in range(NG):
                    take(s, g, 6 * i + (G_KV + 3 * s + g + 1))
                split_lo(s, 2 * i + (U_KV + s + 3))
            for s in range(2):
                kv_unit(0, s, 0, True)
            with dve.Fori(1, 4) as i:
                for s in range(2):
                    kv_unit(i, s, 16 * i)
            with dve.Fori(4, 8) as i:
                for s in range(2):
                    kv_unit(i, s, 16 * 4)

            for k in range(KB):
                x_lo(k, "mix_pre1", "n2")
            dve.wait_ge(sem("lam_exp"), 2)
            ln(dve.tensor_tensor(lam[:, 4:5], lam[:, 3:4], lam[:, 2:3], ALU.subtract))
            ln(dve.tensor_scalar(lam[:, 5:6], lam[:, 4:5], LAM_INIT, None, ALU.subtract))
            dve.wait_ge(sem("mask_in"), 5)
            dve.tensor_copy(MA[:, :], P0[:, 0, 0:P])
            dve.tensor_copy(MB[:, :], P0[:, 0, P:2 * P]).then_inc(sem("mask_r"), 1)

            def take_q(g, n, bank=None):
                dve.wait_ge(mm_done, n)
                dve.scalar_tensor_tensor(QR[:, grp(g)], PS[:, 7 if bank is None else bank, 0:G], ATT_SCALE, RB[:, grp(g)],
                                         ALU.mult, ALU.mult).then_inc(bank_free, 1)


            def lower(o, a, hi):
                return dve.tensor_tensor(o, a, hi.bitcast(F32), ALU.subtract)

            def split_k(h1):
                dve.wait_ge(sem("k_hi"), h1)
                lower(KL[:, 0:SEQ], KR[:, 0:SEQ], KH[:, 0:SEQ]).then_inc(sem("k_lo"), 1)

            def split_q(h, s, g):
                dve.wait_ge(sem("q_hi"), 3 * h + (g + 1))
                lower(QL[:, s, grp(g)], QR[:, grp(g)], QH[:, s, grp(g)]).then_inc(sem("q_lo"), 1)

            split_k(1)
            for g in range(NG):
                take_q(g, G_Q + g + 1, g)
            for g in range(NG):
                split_q(0, 0, g)

            def att_extras(q, t, last):
                h, more = t.h, not (last and t.hp == 1)
                if t.i == 0:
                    dve.wait_ge(sem("kc_hi"), h + 1)
                    lower(KL[:, SCOL:NKEY], KR[:, SEQ:T], KH[:, SCOL:NKEY])
                    lower(KL[:, SEQ:SCOL], PS[:, 7, :], KH[:, SEQ:SCOL]).then_inc(sem("kc_lo"), 1)
                    split_lo(t.hp, 2 * q + (U_Q + t.hp + 3))
                if t.i == 1:
                    dve.wait_ge(sem("v_hi"), h + 1)
                    lower(VL[:, 0:NT, :], VR[:, 0:NT, :], VH[:, 0:NT, :]).then_inc(sem("v_lo"), 1)
                if t.i == 8 and more:
                    split_k(h + 2)
                if t.i in SPLIT and more:
                    split_q(h + 1, (t.hp + 1) % 2, SPLIT.index(t.i))
                if not more and 1 <= t.i < H:
                    x_lo(t.i - 1, "sub", "wo")

            def att_take(t):
                dve.wait_ge(sem("a_out"), t.n + 1)
                dve.tensor_copy(OC[t.f, t.par, :], PS[t.f, 6, 0:P]).then_inc(sem("a_oc"), 1)

            def att_combine(t):
                dve.wait_ge(sem("a_exp"), 2 * t.n + 2)
                dve.reciprocal(t.number(6, 2), t.number(4, 2)).then_inc(sem("a_c"), 1)
                dve.wait_ge(sem("a_c"), 2 * t.n + 1)
                dve.scalar_tensor_tensor(t.number(10), t.number(4), t.number(7), lam[t.f, 5:6], ALU.mult, ALU.mult)\
                    .then_inc(sem("a_c"), 1)
                dve.wait_ge(sem("a_c"), 2 * t.n + 2)
                w = P0[t.f, t.par, 0:t.keys]
                dve.scalar_tensor_tensor(w, P1[t.f, 0:t.keys], t.number(10), w, ALU.mult, ALU.add)\
                    .then_inc(sem("a_comb"), 1)

            def att_turned_lo(t):
                dve.wait_ge(sem("a_thi"), t.n + 1)
                for (src, dst), (_, hi) in zip(t.turned(TL), t.turned(TH)):
                    ins = lower(dst, src, hi)
                ins.then_inc(sem("a_tlo"), 1)

            def att_norm(t):
                dve.wait_ge(sem("a_pow"), t.n + 1)
                dve.tensor_scalar(ON[t.f, t.par, :], OC[t.f, t.par, :], t.number(14), t.number(6), ALU.mult, ALU.mult)\
                    .then_inc(sem("a_on"), 1)

            def att_max(t, m):
                dve.wait_ge(sem("a_scores"), 2 * t.n + (m + 1))
                dve.tensor_reduce(t.number(m), t.score(m), AX, ALU.max, negate=True).then_inc(sem("a_max"), 1)

            def att_turn_of_loop(q, first=False, last=False):
                for m in range(TPT + (4 if last else 0)):
                    t = Tile(q, m)
                    if m - 1 < TPT and not (first and m < 1):
                        att_combine(Tile(q, m - 1))
                    if m - 3 < TPT and not (first and m < 3):
                        att_take(Tile(q, m - 3))
                    if not (first and m < 4):
                        att_norm(Tile(q, m - 4))
                    if m < TPT:
                        if t.i in TAKE and not (last and t.hp == 1):
                            g = TAKE.index(t.i)
                            take_q(g, 6 * q + (G_Q + 3 * (t.hp + 1) + g + 1))
                        att_max(t, 0)
                        att_max(t, 1)
                    if m - 1 < TPT and not (first and m < 1):
                        att_turned_lo(Tile(q, m - 1))
                    if m < TPT:
                        att_extras(q, t, last)

            att_turn_of_loop(0, first=True)
            with dve.Fori(1, NPAIR - 1) as q:
                att_turn_of_loop(q)
            att_turn_of_loop(NPAIR - 1, last=True)

            x_lo(KB - 1, "sub", "wo")
            dve.wait_ge(sem("x_lo"), KB * SPLITS["wo"] + KB)
            dense_y(U_WO, G_WO, 48)
            boundary("b2", "mix_post1", "ffn_pre1", U_MLP1, G_MLP1)
            mlp(1, U_MLP1, G_MLP1)
            boundary("b3", "ffn_post1", None)

            for t in range(NCH):
                dve.wait_ge(sem("y_turned"), t + 1)
                dve.tensor_copy(y_half(t, 1), PS[0:P if t < NT else DEC, 2 * (t % 4) + 1, :]).then_inc(sem("y_out_d"), 1)

        @block.gpsimd
        def _(pool):
            def token_pow(name):
                pool.wait_ge(sem("tok_var"), 2 * NORMS[name] + 2)
                pool.tensor_tensor(TV[:, 2, :], TV[:, 1, :], half[:, :], ALU.pow).then_inc(sem("tok_pow"), 1)

            pool.memset(ident[:, :], 0.0).then_inc(sem("ident"), 1)
            pool.wait_ge(sem("ident"), 1)
            pool.affine_select(out=ident[:, :], in_=ident[:, :], compare_op=ALU.not_equal, fill=1.0, base=0,
                               pattern=[[-1, P]], channel_multiplier=1).then_inc(sem("ident"), 1)
            pool.memset(WGH[:, :, :].bitcast(F32), 0.0).then_inc(sem("wg_zero"), 1)
            pool.memset(WGL[:, :, :].bitcast(F32), 0.0).then_inc(sem("wg_zero"), 1)
            pool.memset(RST[:, :], 1.0).then_inc(sem("setup"), 1)
            pool.wait_ge(sem("setup"), 1)
            pool.memset(RST[:, 0:T:LC], 0.0).then_inc(sem("rst"), 1)
            barrier(pool, PH["load"])
            token_pow("n0")
            pool.wait_ge(sem("gates_read"), 6)
            pool.memset(mask[:, :], 0.0).then_inc(sem("sel"), 1)
            pool.wait_ge(sem("sel"), 1)
            pool.affine_select(out=mask[:, :], in_=mask[:, :], compare_op=ALU.is_ge, fill=NEG, base=0,
                               pattern=[[1, LC]], channel_multiplier=-1).then_inc(sem("sel"), 1)

            def chunk_pow(C):
                pool.wait_ge(sem("c_den"), 8 * C.n + 7)
                pool.tensor_tensor(C.number(6), C.number(5), half[C.f, 0:H], ALU.pow).then_inc(sem("c_pow"), 1)
            with pool.Fori(0, NT // 2) as i:
                for m in range(2):
                    chunk_pow(Chunk(i, m))
            chunk_pow(Chunk(NT // 2, 0))

            def boundary(name, l=None, pre=True):
                token_pow(name + "y")
                pool.wait_ge(sem("rb"), 3 * (NORMS[name + "y"] + 1))
                for k in range(POOL_Y, KB):
                    pool.tensor_tensor(Y[:, k, :], Y[:, k, :], RB[:, :], ALU.mult).then_inc(sem("y_scaled"), 1)
                if not pre:
                    return
                for k in range(1, KB):
                    pool.wait_ge(sem("squared_x"), KB * BOUNDS[name] + k + 1)
                    pool.wait_ge(sem("sq_sum"), SUMS[name + "y"] + k - 1)
                    pool.tensor_tensor(SQ[:, :], SQ[:, :], STG[:, k % 2, :], ALU.add).then_inc(sem("sq_sum"), 1)
                token_pow(name + "x")
                if l is not None:
                    for k in range(KB):
                        pool.wait_ge(sem("x_new"), KB * BOUNDS[name] + k + 1)
                        pool.memset(Y[:, k, :], 0.0).then_inc(sem("y_zero"), 1)

            def mlp(l, g0):
                def group(j, first=False):
                    for n in range(12):
                        if first and n < 6:
                            pool.wait_ge(sem("raw_scaled"), 6 * l + n + 1)
                        else:
                            pool.wait_ge(sem("bank_free"), RING + 36 * j + (g0 + n + 1))
                        pool.tensor_tensor(M2[:, n % 2, :], MT[:, n % 2, :], MT[:, n % 2, :], ALU.mult)\
                            .then_inc(sem("h_sq"), 1)
                group(0, True)
                with pool.Fori(1, FFG) as j:
                    group(j)

            boundary("b0", 0)
            mlp(0, G_MLP0)
            boundary("b1")
            pool.wait_ge(sem("kv_st0"), 32 * 8)
            pool.wait_ge(sem("kv_st1"), 32 * 8)
            pool.memset(P0[:, 0, 0:2 * P], 0.0).then_inc(sem("mask_in"), 1)
            pool.wait_ge(sem("mask_in"), 1)
            for r in (0, 64):
                pool.memset(P0[r:r + 1, 0, 0:64], 1.0).then_inc(sem("mask_in"), 1)
                pool.memset(P0[r:r + 1, 0, P + 64:2 * P], NEG).then_inc(sem("mask_in"), 1)

            def att_turn_of_loop(q, first=False, last=False):
                for m in range(TPT + (3 if last else 0)):
                    t = Tile(q, m)
                    if not (first and m < 3):
                        o = Tile(q, m - 3)
                        pool.wait_ge(sem("a_ss"), o.n + 1)
                        pool.tensor_tensor(o.number(11), o.number(8), mean_eps[o.f, 0:1], ALU.mult)\
                            .then_inc(sem("a_var"), 1)
                        pool.wait_ge(sem("a_var"), 2 * o.n + 1)
                        pool.tensor_tensor(o.number(13), o.number(11), mean_eps[o.f, 1:2], ALU.add)\
                            .then_inc(sem("a_var"), 1)
                        pool.wait_ge(sem("a_var"), 2 * o.n + 2)
                        pool.tensor_tensor(o.number(14), o.number(13), half[o.f, 0:1], ALU.pow).then_inc(sem("a_pow"), 1)
                    if m < TPT and t.i == 3:
                        pool.wait_ge(sem("vc_hi"), t.h + 1)
                        pool.tensor_tensor(VL[:, NT:NT + 4, :], VR[:, NT:NT + 4, :], VH[:, NT:NT + 4, :].bitcast(F32),
                                           ALU.subtract)
                        pool.tensor_tensor(VL[0:DEC, NT + 4, :], VR[0:DEC, NT + 4, :],
                                           VH[0:DEC, NT + 4, :].bitcast(F32), ALU.subtract).then_inc(sem("vc_lo"), 1)
            att_turn_of_loop(0, first=True)
            with pool.Fori(1, NPAIR - 1) as q:
                att_turn_of_loop(q)
            att_turn_of_loop(NPAIR - 1, last=True)
            boundary("b2", 1)
            mlp(1, G_MLP1)
            boundary("b3", None, False)


_INS = ['x_prompt', 'x_sample', 'cache_k', 'cache_v', 'state_c', 'state_n', 'state_m', 'w_in_a', 'b_i_a', 'b_f_a',
        'g_h_a', 'w_out_a', 'g_kv', 'w_kv', 'w_q_b', 'lambda_q1', 'lambda_k1', 'lambda_q2', 'lambda_k2', 'g_sub_b',
        'w_o_b', 'g_mix_pre', 'g_mix_post', 'g_ffn_pre', 'g_ffn_post', 'w_up', 'w_down']
_OUTS = [(1, SEQ, D), (1, DEC, D), (1, 1, H, DK, DV), (1, 1, H, DK), (1, 1, H), (1, SEQ, H, 2, 64), (1, SEQ, H, 128),
         (1, 1, H, DK, DV), (1, 1, H, DK), (1, 1, H), (1, DEC, H, 2, 64), (1, DEC, H, 128)]


def kernel(**inputs):
    import numpy as _np
    import concourse.bacc as _bacc
    from concourse import mybir as _mybir
    from concourse.bass_utils import run_bass_kernel_spmd as _run

    nc = _bacc.Bacc("TRN2", target_bir_lowering=False, num_devices=1, dynamic_dma_scratch_size=1024)
    arrays, args = {}, []
    for name in _INS:
        a = _np.ascontiguousarray(inputs[name])
        arrays[f"in_{name}"] = a
        args.append(nc.dram_tensor(f"in_{name}", a.shape, _mybir.dt.from_np(a.dtype), kind="ExternalInput").ap())
    for i, shape in enumerate(_OUTS):
        args.append(nc.dram_tensor(f"out_{i}", shape, _mybir.dt.float32, kind="ExternalOutput").ap())
    for name, n in (("proj_s", 24), ("kT_s", H), ("o_s", H)):
        args.append(nc.dram_tensor(name, (n, P, T), _mybir.dt.float32).ap())
    args.append(nc.dram_tensor("gate_s", (2, H, T), _mybir.dt.float32).ap())
    stream_step(nc, *args)
    r = _run(nc, [arrays], core_ids=[0])
    return tuple(r.results[0][f"out_{i}"] for i in range(len(_OUTS)))
```
